# Optimizing a Trainium2 kernel written in Bass

```python
import jax, jax.numpy as jnp
from jax import lax
import numpy as np

D_MODEL = 1024
BATCH = 1
SEQ = 256
DEPTH = 1

PLE_DIM = 256
HEAD_DIM = 64
FOX_HEADS = 8
RWKV_HEADS = 8
FOX_WIDTH = FOX_HEADS * HEAD_DIM
RWKV_WIDTH = RWKV_HEADS * HEAD_DIM
MIX_WIDTH = FOX_WIDTH + RWKV_WIDTH
Q_BLOCK = 128
DECAY_LORA = 64
ICLR_LORA = 64
GATE_LORA = 128
FOX_IN = 4 * FOX_WIDTH + FOX_HEADS
RWKV_IN = 3 * RWKV_WIDTH + DECAY_LORA + ICLR_LORA + GATE_LORA
IN_WIDTH = FOX_IN + RWKV_IN
FOX_SPLIT_IDX = (FOX_WIDTH, 2 * FOX_WIDTH, 3 * FOX_WIDTH, 4 * FOX_WIDTH)
RWKV_SPLIT_IDX = (RWKV_WIDTH, 2 * RWKV_WIDTH, 3 * RWKV_WIDTH,
                  3 * RWKV_WIDTH + DECAY_LORA, 3 * RWKV_WIDTH + DECAY_LORA + ICLR_LORA)
N_EXPERTS = 32
TOP_K = 4
EXPERT_FF = 1024
SWIGLU_LIMIT = 7.0
SWIGLU_ALPHA = 1.702
MOE_BLOCK = 256
NORM_EPS = 1e-6
GN_EPS = 64e-5

kernel_name = "fox_rwkv7_hybrid_moe_ple_block"

def rmsnorm(x, g):
    xf = x.astype(jnp.float32)
    y = xf * lax.rsqrt(jnp.mean(xf * xf, axis=-1, keepdims=True) + NORM_EPS)
    return (y * g.astype(jnp.float32)).astype(x.dtype)

def token_shift(z):
    return jnp.pad(z[:, :-1], ((0, 0), (1, 0), (0, 0)))

def fox_attention(q, k, v, log_f):
    B, S, H, Dh = q.shape
    nblk = S // Q_BLOCK
    c = jnp.cumsum(log_f, axis=1)
    c_keys = c.transpose(0, 2, 1)
    qb = q.reshape(B, nblk, Q_BLOCK, H, Dh).transpose(1, 0, 2, 3, 4)
    cb = c.reshape(B, nblk, Q_BLOCK, H).transpose(1, 0, 3, 2)
    kpos = jnp.arange(S)
    scale = HEAD_DIM ** -0.5

    def block(args):
        i, q_i, c_i = args
        s = jnp.einsum('bqhd,bkhd->bhqk', q_i, k, preferred_element_type=jnp.float32) * scale
        s = s + (c_i[..., :, None] - c_keys[..., None, :])
        qpos = i * Q_BLOCK + jnp.arange(Q_BLOCK)
        s = jnp.where(kpos[None, :] <= qpos[:, None], s, -jnp.inf)
        pr = jax.nn.softmax(s, axis=-1)
        return jnp.einsum('bhqk,bkhd->bqhd', pr.astype(v.dtype), v)

    out = lax.map(block, (jnp.arange(nblk), qb, cb))
    return out.transpose(1, 0, 2, 3, 4).reshape(B, S, H, Dh)

def rwkv7_recurrence(r, w, k, v, a, b):
    B, S, H, N = r.shape

    def step(state, inp):
        r_t, w_t, k_t, v_t, a_t, b_t = inp
        sa = jnp.einsum('bhvk,bhk->bhv', state, a_t)
        state = (state * w_t[:, :, None, :] + sa[..., None] * b_t[:, :, None, :]
                 + v_t[..., None] * k_t[:, :, None, :])
        return state, jnp.einsum('bhvk,bhk->bhv', state, r_t)

    xs = tuple(t.transpose(1, 0, 2, 3) for t in (r, w, k, v, a, b))
    _, y = lax.scan(step, jnp.zeros((B, H, N, N), jnp.float32), xs)
    return y.transpose(1, 0, 2, 3)

def rwkv7_time_mix(z_all, mu, w0, w2, a0, a2, g2, k_k, k_a, r_k, ln_w, ln_b):
    B, S, _ = z_all.shape
    f32 = jnp.float32
    z = (z_all + (token_shift(z_all) - z_all) * mu).astype(f32)
    r, k, v, zw, za, zg = jnp.split(z, RWKV_SPLIT_IDX, axis=-1)
    w_log = -jax.nn.softplus(-(w0.astype(f32) + jnp.tanh(zw) @ w2.astype(f32))) - 0.5
    decay = jnp.exp(-jnp.exp(w_log))
    a = jax.nn.sigmoid(a0.astype(f32) + za @ a2.astype(f32))
    g = jax.nn.sigmoid(zg) @ g2.astype(f32)
    heads = lambda t: t.reshape(B, S, RWKV_HEADS, HEAD_DIM)
    kk = heads(k * k_k.astype(f32))
    kk = kk / jnp.maximum(jnp.sqrt(jnp.sum(kk * kk, axis=-1, keepdims=True)), 1e-12)
    k = k * (1.0 + (a - 1.0) * k_a.astype(f32))
    rh, kh, vh, ah = heads(r), heads(k), heads(v), heads(a)
    y = rwkv7_recurrence(rh, heads(decay), kh, vh, -kk, kk * ah)
    mean = jnp.mean(y, axis=-1, keepdims=True)
    var = jnp.mean(jnp.square(y - mean), axis=-1, keepdims=True)
    y = ((y - mean) * lax.rsqrt(var + GN_EPS)).reshape(B, S, RWKV_WIDTH)
    y = y * ln_w.astype(f32) + ln_b.astype(f32)
    bonus = jnp.sum(rh * kh * r_k.astype(f32), axis=-1, keepdims=True) * vh
    y = (y + bonus.reshape(B, S, RWKV_WIDTH)) * g
    return y.astype(z_all.dtype)

def moe_ffn(h, w_router, b_router, w_gu, b_gu, w_down, b_down):
    B, S, D = h.shape
    xt = h.reshape(-1, D)
    N = xt.shape[0]
    NK = N * TOP_K
    logits = (xt @ w_router).astype(jnp.float32) + b_router.astype(jnp.float32)
    top_val, top_idx = lax.top_k(logits, TOP_K)
    gates = jax.nn.softmax(top_val, axis=-1)
    flat_e = top_idx.reshape(-1)
    flat_tok = jnp.arange(NK) // TOP_K
    order = jnp.argsort(flat_e)
    e_sorted, tok_sorted, g_sorted = flat_e[order], flat_tok[order], gates.reshape(-1)[order]
    counts = jnp.bincount(flat_e, length=N_EXPERTS)
    group_start = jnp.cumsum(counts) - counts
    padded = ((counts + MOE_BLOCK - 1) // MOE_BLOCK) * MOE_BLOCK
    pad_end = jnp.cumsum(padded)
    pad_start = pad_end - padded
    dest = pad_start[e_sorted] + (jnp.arange(NK) - group_start[e_sorted])
    n_blocks = -(-NK // MOE_BLOCK) + N_EXPERTS
    P = n_blocks * MOE_BLOCK
    pad_tok = jnp.full((P,), N, jnp.int32).at[dest].set(tok_sorted.astype(jnp.int32))
    pad_gate = jnp.zeros((P,), jnp.float32).at[dest].set(g_sorted)
    block_e = jnp.clip(jnp.searchsorted(pad_end, jnp.arange(n_blocks) * MOE_BLOCK, side='right'),
                       0, N_EXPERTS - 1)

    def expert_block(args):
        idx, gt, e = args
        xb = jnp.take(xt, idx, axis=0, mode='fill', fill_value=0)
        hh = (xb @ w_gu[e] + b_gu[e]).astype(jnp.float32)
        glu = jnp.minimum(hh[:, :EXPERT_FF], SWIGLU_LIMIT)
        lin = jnp.clip(hh[:, EXPERT_FF:], -SWIGLU_LIMIT, SWIGLU_LIMIT)
        act = (glu * jax.nn.sigmoid(SWIGLU_ALPHA * glu) * (lin + 1.0)).astype(xt.dtype)
        return (act @ w_down[e] + b_down[e]).astype(jnp.float32) * gt[:, None]

    y_pad = lax.map(expert_block, (pad_tok.reshape(n_blocks, MOE_BLOCK),
                                   pad_gate.reshape(n_blocks, MOE_BLOCK), block_e))
    out = jnp.zeros((N, D), jnp.float32).at[pad_tok].add(y_pad.reshape(P, D), mode='drop')
    return out.astype(h.dtype).reshape(B, S, D)

def setup_inputs(seed: int = 0) -> dict:
    key = jax.random.key(seed)
    ks = iter(jax.random.split(key, 40))
    L = DEPTH
    f32 = jnp.float32

    def nrm(shape, scale):
        return jax.random.normal(next(ks), shape, f32) * scale

    def gain(shape):
        return 1.0 + nrm(shape, 0.05)

    def unif(shape, lo, hi):
        return jax.random.uniform(next(ks), shape, f32, minval=lo, maxval=hi)

    return {
        "x": nrm((BATCH, SEQ, D_MODEL), 1.0),
        "p": nrm((DEPTH, BATCH, SEQ, PLE_DIM), 1.0),
        "mix_norm": gain((L, D_MODEL)),
        "w_in": nrm((L, D_MODEL, IN_WIDTH), D_MODEL ** -0.5),
        "fox_f_bias": unif((L, FOX_HEADS), 1.0, 5.0),
        "fox_q_norm": gain((L, HEAD_DIM)),
        "fox_k_norm": gain((L, HEAD_DIM)),
        "rwkv_mu": unif((L, RWKV_IN), 0.0, 1.0),
        "rwkv_w0": unif((L, RWKV_WIDTH), -6.5, -1.5),
        "rwkv_w2": nrm((L, DECAY_LORA, RWKV_WIDTH), 0.1),
        "rwkv_a0": nrm((L, RWKV_WIDTH), 0.1),
        "rwkv_a2": nrm((L, ICLR_LORA, RWKV_WIDTH), 0.1),
        "rwkv_g2": nrm((L, GATE_LORA, RWKV_WIDTH), GATE_LORA ** -0.5),
        "rwkv_k_k": 0.85 + nrm((L, RWKV_WIDTH), 0.02),
        "rwkv_k_a": 1.0 + nrm((L, RWKV_WIDTH), 0.02),
        "rwkv_r_k": nrm((L, RWKV_HEADS, HEAD_DIM), 0.1),
        "rwkv_ln_w": gain((L, RWKV_WIDTH)),
        "rwkv_ln_b": nrm((L, RWKV_WIDTH), 0.01),
        "w_out": nrm((L, MIX_WIDTH, D_MODEL), MIX_WIDTH ** -0.5),
        "moe_norm": gain((L, D_MODEL)),
        "w_router": nrm((L, D_MODEL, N_EXPERTS), D_MODEL ** -0.5),
        "b_router": nrm((L, N_EXPERTS), 0.01),
        "w_gu": nrm((L, N_EXPERTS, D_MODEL, 2 * EXPERT_FF), D_MODEL ** -0.5),
        "b_gu": nrm((L, N_EXPERTS, 2 * EXPERT_FF), 0.01),
        "w_down": nrm((L, N_EXPERTS, EXPERT_FF, D_MODEL), EXPERT_FF ** -0.5),
        "b_down": nrm((L, N_EXPERTS, D_MODEL), 0.01),
        "ple_norm": gain((L, D_MODEL)),
        "w_ple_gate": nrm((L, D_MODEL, D_MODEL), D_MODEL ** -0.5),
        "w_ple_proj": nrm((L, PLE_DIM, D_MODEL), PLE_DIM ** -0.5),
        "final_norm": gain((D_MODEL,)),
    }

def reference(x, p, mix_norm, w_in, fox_f_bias, fox_q_norm, fox_k_norm, rwkv_mu, rwkv_w0, rwkv_w2,
              rwkv_a0, rwkv_a2, rwkv_g2, rwkv_k_k, rwkv_k_a, rwkv_r_k, rwkv_ln_w, rwkv_ln_b, w_out,
              moe_norm, w_router, b_router, w_gu, b_gu, w_down, b_down, ple_norm, w_ple_gate,
              w_ple_proj, final_norm):
    B, S, _ = x.shape
    for i in range(DEPTH):
        h = rmsnorm(x, mix_norm[i])
        z = h @ w_in[i]
        z_fox, z_rwkv = z[..., :FOX_IN], z[..., FOX_IN:]
        fq, fk, fv, fog, ff = jnp.split(z_fox, FOX_SPLIT_IDX, axis=-1)
        hd = lambda t: t.reshape(B, S, FOX_HEADS, HEAD_DIM)
        q = rmsnorm(hd(fq), fox_q_norm[i])
        k = rmsnorm(hd(fk), fox_k_norm[i])
        log_f = jax.nn.log_sigmoid(ff.astype(jnp.float32) + fox_f_bias[i].astype(jnp.float32))
        fox_out = fox_attention(q, k, hd(fv), log_f).reshape(B, S, FOX_WIDTH) * jax.nn.sigmoid(fog)
        rwkv_out = rwkv7_time_mix(z_rwkv, rwkv_mu[i], rwkv_w0[i], rwkv_w2[i], rwkv_a0[i], rwkv_a2[i],
                                  rwkv_g2[i], rwkv_k_k[i], rwkv_k_a[i], rwkv_r_k[i],
                                  rwkv_ln_w[i], rwkv_ln_b[i])
        x = x + jnp.concatenate([fox_out, rwkv_out], axis=-1) @ w_out[i]
        x = x + moe_ffn(rmsnorm(x, moe_norm[i]), w_router[i], b_router[i], w_gu[i], b_gu[i],
                        w_down[i], b_down[i])
        gate = jax.nn.sigmoid(rmsnorm(x, ple_norm[i]) @ w_ple_gate[i])
        x = x + gate * (p[i] @ w_ple_proj[i])
    return rmsnorm(x, final_norm)


_drawn_inputs = setup_inputs


def setup_inputs(seed=0):
    import zlib

    import numpy as np

    out = dict(_drawn_inputs(seed))
    spreads = {}
    factors = {'fox_q_norm': 3.666,
     'fox_k_norm': 3.784,
     'rwkv_k_k': 2.892,
     'rwkv_ln_b': 4.426,
     'b_gu': 8.0,
     'b_down': 8.0,
     'ple_norm': 6.95}
    for name, (base, spread) in spreads.items():
        noise = np.random.default_rng([zlib.crc32(name.encode()), seed]).standard_normal(out[name].shape)
        drawn = base * np.exp(spread * noise) if base else spread * noise
        out[name] = __import__('jax').numpy.asarray(drawn.astype(out[name].dtype))
    for name, factor in factors.items():
        out[name] = (out[name] * factor).astype(out[name].dtype)
    return out
```

```python
from contextlib import ExitStack

import concourse.bass as bass
from concourse import mybir

F32 = mybir.dt.float32
I32 = mybir.dt.int32
ALU = mybir.AluOpType
ACT = mybir.ActivationFunctionType
AX = mybir.AxisListType

P = 128
D = 1024
SEQ = 256
TB = SEQ // P
KD = D // P
PLE = 256
HD = 64
NHEAD = 8
NJ = NHEAD * HD // P
CH = 64
NC = SEQ // CH
NE = 32
TOPK = 4
FF = 1024
KF = FF // P
LIMIT = 7.0
SALPHA = 1.702
EPS = 1e-6
GN_EPS = 64e-5
DECAY = 0.6065306597126334
SLOTS = 64
NCH = SEQ // SLOTS
NITEM = NE + SEQ * TOPK // SLOTS
IW = NITEM + 1
NSLOT = 6
PW = 512
FAR = 1000.0

FOXW, RW0 = NHEAD * HD, 4 * NHEAD * HD + NHEAD
ZP = [(RW0 + 3 * FOXW, 256), (RW0 + FOXW, PW), (RW0, PW), (RW0 + 2 * FOXW, PW),
      (0, PW), (FOXW, PW), (3 * FOXW, PW), (2 * FOXW, PW)]
NPRE = len(ZP) + 2
Z_PIECE = [0] * 2 + [1] * 4 + [2] * 4 + [3] * 4 + [4] * 4 + [5] * 4 + [6] * 4
NZ = len(Z_PIECE)
N_SHIFT = 14
Z_DONE = [2, 6, 10, 14, 18, 22, 26, NZ + 3]


def layout(spec):
    at, out = 0, {}
    for name, n in spec:
        out[name] = (at, at + n)
        at += n
    return out, at


CONST, NCONST = layout([("ident", P), ("blk", P), ("inclT", CH), ("strictT", CH), ("m0", CH)]
                       + [(f"m{k}T", CH) for k in range(6)]
                       + [("eye", CH), ("causal", 3 * P), ("reset", SEQ), ("tri", P), ("ones", SEQ),
                          ("iota_s", SLOTS), ("delta", NHEAD), ("iota_i", IW), ("thr", 1), ("eval", 1),
                          ("far", P)])
PARAM, NPARAM = layout([("mix", KD), ("ple", KD), ("mu", N_SHIFT), ("w0", NJ), ("a0", NJ), ("k_k", NJ),
                        ("k_a", NJ), ("r_k", NJ), ("ln_w", NJ), ("ln_b", NJ), ("qn", 1), ("kn", 1), ("fb", 1)])

LEVELS = range(1, 6)
PE_STEPS = ([f"hT{k}" for k in range(KD)] + ["z0", "z1"] + [f"z{n}" for n in range(2, 6)] + ["uwua"]
            + [f"z{n}" for n in range(6, 10)] + ["g", "ssk"] + [f"z{n}" for n in range(10, 18)] + ["bn"]
            + [f"z{n}" for n in range(18, NZ + 3)]
            + ["vp", "bp", "kp", "qss", "ma", "kss", "mk", "aa"])


def head_steps(h):
    return [f"sc{h}", f"pt{h}", f"o{h}"]


MIX_ORDER = []
for _i, _k in enumerate(LEVELS):
    MIX_ORDER += [("level", _k), ("head", _i)]
for _c in range(NC):
    MIX_ORDER += [("chunk", _c)] + ([("head", 5 + _c)] if 5 + _c < NHEAD else [])
for _kind, _n in MIX_ORDER:
    if _kind == "level":
        PE_STEPS += [f"q{_n}"] + ([f"t{_n}"] if _n < 5 else []) + [f"tt{_n}"]
    elif _kind == "head":
        PE_STEPS += head_steps(_n)
    else:
        PE_STEPS += [f"x{_n}", f"u{_n}", f"d{_n}", f"y{_n}"]
PE_STEPS += ["mean", "var", "xo0", "xo1", "xo2", "xo3"] + [f"h2T{k}" for k in range(KD)]
PE_STEPS += ["logits", "rank", "rrT", "grT", "count", "pos", "ri", "gi", "ei"]


def fox_rwkv7_moe_ple(nc, t, out):
    with ExitStack() as ctx:
        def sb(name, shape, dt=F32):
            return ctx.enter_context(nc.sbuf_tensor(name, shape, dt))

        def sem(name):
            return ctx.enter_context(nc.semaphore(name))

        PS = ctx.enter_context(nc.psum_tensor("PS", [P, 8, 512], F32))
        PSF = PS[:, :, :].rearrange("p b n -> p (b n)")
        ring = sb("ring", [P, NSLOT, KD * PW])
        con = sb("con", [P, NCONST])
        prm = sb("prm", [P, NPARAM])
        xq = sb("xq", [P, TB * D])
        hT = sb("hT", [P, KD, SEQ])
        B = sb("B", [P, 15, D])
        FG = sb("FG", [P, NJ, SEQ])
        FV = sb("FV", [P, TB, FOXW])
        rz = sb("rz", [P, 4, SEQ + 4])
        LZ = sb("LZ", [P, 2, SEQ])
        lora = sb("lora", [P, 2 * FOXW])
        wff = sb("wff", [P, KD, NHEAD])
        wr = sb("wr", [P, KD, NE])
        brt = sb("brt", [P, NE])
        S = sb("S", [P, 2, NJ * HD])
        XU = sb("XU", [P, 2, NJ * HD])
        WC = sb("WC", [P, NJ * NC])
        col = sb("col", [P, 32])
        epsc = sb("epsc", [P, 4])
        EI = sb("EI", [1, 64], I32)
        RI = sb("RI", [P, IW, TB])
        GI = sb("GI", [P, IW, TB])
        bcur = sb("bcur", [P, 24])
        bT = FG[:, :, :].rearrange("p a b -> p (a b)")[:, 0:NE * 24].rearrange("p (e n) -> p e n", n=24)

        def c_(name):
            return con[:, CONST[name][0]:CONST[name][1]]

        def p_(name, i=0):
            a = PARAM[name][0] + i
            return prm[:, a:a + 1]

        def b4(i):
            return B[:, i, :].rearrange("p (j t) -> p j t", j=NJ)

        def b16(i):
            return B[:, i, :].rearrange("p (g c) -> p g c", g=NJ * NC)

        def bank(b, w=512):
            return PS[:, b, 0:w]

        def banks16(b):
            return PSF[:, b * 512:b * 512 + 1024].rearrange("p (g c) -> p g c", g=16)

        def two(b):
            return PSF[:, b * 512:b * 512 + 1024]

        xs = xq[:, :].rearrange("p (b d) -> p b d", b=TB)
        QT = xq[:, 0:D].rearrange("p (j t) -> p j t", j=NJ)
        KT = xq[:, D:2 * D].rearrange("p (j t) -> p j t", j=NJ)
        hn = B[:, 0:2, :]
        AR = B[:, 10:12, :].rearrange("p a n -> p (a n)").rearrange("p (g s c) -> p g s c", g=16, s=2)
        rzf = rz[:, :, :].rearrange("p a b -> p (a b)")[:, 0:1024]
        att = rz[:, :, :].rearrange("p a b -> p (a b)")[:, 0:768].rearrange("p (s n) -> p s n", s=2)
        lzf = LZ[:, :, :].rearrange("p a b -> p (a b)")[:, 0:384]
        mixT = hT
        H2 = B[:, 10:12, :]
        h2T = B[:, 0:2, :].rearrange("p a n -> p (a n)").rearrange("p (k t) -> p k t", k=KD)
        gmoe = B[:, 12, :]
        wgate = B[:, 0:8, :].rearrange("p (q a) n -> p q (a n)", q=2)
        wproj = B[:, 8:10, :]
        pTt = B[:, 13, 0:512].rearrange("p (k t) -> p k t", k=2)
        gfin = B[:, 14, :]
        ht2 = hT[:, :, :].rearrange("p a b -> p (a b)")
        e_g, e_s, e_l, e_act = (ht2[:, 512 * a:512 * a + 512] for a in range(4))
        fv2 = FV[:, :, :].rearrange("p a b -> p (a b)")
        xg = fv2[:, 0:512].rearrange("p (k t) -> p k t", k=KD)
        e_y = rzf[:, 0:512]
        PM, PG = (fv2[:, a:a + TB * SLOTS].rearrange("p (b t) -> p b t", b=TB) for a in (512, 768))
        GTs = rzf[0:SLOTS, 512:1024].rearrange("p (s t) -> p s t", s=2)
        CQ, CK, CKh = lora[:, 0:SEQ], lora[:, SEQ:2 * SEQ], lora[:, 2 * SEQ:3 * SEQ]
        tmp8 = B[0:8, 13, 0:768].rearrange("p (s t) -> p s t", s=3)
        R = B[:, 9, 0:24 * NE].rearrange("p (s e) -> p s e", e=NE)
        ysb = B[0:SLOTS, 12, :]

        s_in = sem("inputs_landed")
        s_aux = sem("small_weights_landed")
        s_slot = [sem(f"slot{i}_landed") for i in range(NSLOT)]
        s_vt = sem("gated_projection_done")
        s_x2 = sem("x_again_landed")
        s_gm = sem("moe_gain_landed")
        s_bt = sem("expert_bias_landed")
        s_tail = sem("tail_weights_landed")
        s_pe = sem("tensor_steps_done")
        s_dve = sem("vector_steps_done")
        s_act = sem("scalar_steps_done")
        s_vl = sem("vector_op_done")
        s_al = sem("scalar_op_done")
        s_used = sem("expert_pieces_used")
        s_gath = sem("tokens_gathered")
        s_xg = sem("gathered_tokens_in_sbuf")
        s_gt = sem("gate_matrix_in_sbuf")
        s_sel = sem("selection_built")
        s_glu = sem("glu_clamped")
        s_sig = sem("glu_sigmoid_done")
        s_eact = sem("expert_activation_done")
        s_ps6 = sem("glu_bank_free")
        s_yb = sem("expert_output_biased")
        s_yt = sem("expert_output_transposed")
        s_ys = sem("expert_output_in_sbuf")
        s_scat = sem("expert_output_added")
        s_tpe = sem("tail_tensor_steps_done")
        s_tdve = sem("tail_vector_steps_done")
        s_tact = sem("tail_scalar_steps_done")
        s_out = sem("output_stored")

        def value(names):
            return {n: i + 1 for i, n in enumerate(names)}

        pe_at = value(PE_STEPS)

        mixv, mixa = [], []
        for kind, n in MIX_ORDER:
            if kind == "level":
                mixv += [f"mq{n}"] + ([f"t{n}"] if n < 5 else []) + [f"tt{n}"]
                mixa += [f"q{n}"]
            elif kind == "head":
                mixv += [f"ck{n}", f"mx{n}", f"pr{n}"] + ([f"o{n}"] if n % 2 else [])
                mixa += [f"p{n}", f"pt{n}"]
            else:
                mixv += [f"u{n}", f"s{n}"]
                mixa += [f"x{n}", f"y{n}"]
        DVE_STEPS = (["init", "rstd", "hn"] + [f"hT{k}" for k in range(0, KD, 2)]
                     + [f"sh{n}" for n in range(6)] + ["ksq", "scan"] + [f"sh{n}" for n in range(6, 10)] + ["kk", "bprod"]
                     + [f"sh{n}" for n in range(10, 14)] + ["tildes", "ffabs", "fc", "qsq", "at", "qn", "ksqf", "mk", "kn", "aa"]
                     + mixv + ["cent", "vsq", "mix"] + [f"xo{g}" for g in range(4)]
                     + ["rs2", "h2"] + [f"h2T{k}" for k in range(0, KD, 2)]
                     + ["lg", "sel", "gr", "rr", "rrT", "valid", "oh", "tabs"])
        ACT_STEPS = (["ssq", "sd"] + [f"hT{k}" for k in range(1, KD, 2)]
                     + [f"z{n}" for n in range(6)] + ["lz", "swaa"] + [f"z{n}" for n in range(6, 10)] + ["nk", "exps", "g"]
                     + [f"z{n}" for n in range(10, NZ + 3)]
                     + ["ffe", "ffl", "vp", "bp", "kp", "qrs", "krs"] + mixa
                     + ["gsd", "ssq2", "sd2"] + [f"h2T{k}" for k in range(1, KD, 2)] + ["lex", "grT"])
        dve_at, act_at = value(DVE_STEPS), value(ACT_STEPS)
        TPE_STEPS = ["pp"] + [f"t{k}" for k in range(KD)] + ["gate0", "gate1"]
        TDVE_STEPS = ["x3", "rstd", "hn"] + [f"t{k}" for k in range(0, KD, 2)] + ["x40", "x41", "rstd2", "out0", "out1"]
        TACT_STEPS = ["ssq", "sd"] + [f"t{k}" for k in range(1, KD, 2)] + ["gate0", "gate1", "ssq2", "sd2"]
        tpe_at, tdve_at, tact_at = value(TPE_STEPS), value(TDVE_STEPS), value(TACT_STEPS)
        tables = {"dve": (DVE_STEPS, s_dve), "act": (ACT_STEPS, s_act), "pe": (PE_STEPS, s_pe),
                  "tdve": (TDVE_STEPS, s_tdve), "tact": (TACT_STEPS, s_tact), "tpe": (TPE_STEPS, s_tpe)}
        done = dict.fromkeys(tables, 0)

        def finish(ins, who, name):
            names, s = tables[who]
            assert names[done[who]] == name, (who, names[done[who]], name)
            done[who] += 1
            ins.then_inc(s, 1)

        block = ctx.enter_context(nc.Block())

        @block.sync
        def _(sp):
            sp.dma_start(xq[:, :], t["x"]).then_inc(s_in, 16)
            sp.dma_start(con[:, :], t["con"]).then_inc(s_in, 16)
            sp.dma_start(prm[:, :], t["prm"]).then_inc(s_in, 16)

            def piece(n, src, cols):
                sp.dma_start(ring[:, n % NSLOT, 0:KD * cols], src).then_inc(s_slot[n % NSLOT], 16)

            for n in range(NSLOT):
                piece(n, t[f"wz{n}"], ZP[n][1])
                if n == 0:
                    sp.dma_start(lora[:, :], t["lora"]).then_inc(s_aux, 16)
                    sp.dma_start(wff[:, :, :], t["wff"].rearrange("p (k n) -> p k n", k=KD)).then_inc(s_aux, 16)
                    sp.dma_start(wr[:, :, :], t["wr"].rearrange("p (k n) -> p k n", k=KD)).then_inc(s_aux, 16)
                    sp.dma_start(brt[:, :], t["brt"]).then_inc(s_aux, 16)
            for n in range(NSLOT, NPRE):
                last = Z_DONE[n - NSLOT] - 1
                sp.wait_ge(s_pe, pe_at[f"z{last}"])
                if n < len(ZP):
                    piece(n, t[f"wz{n}"], PW)
                else:
                    piece(n, t["wo"][n - len(ZP)], PW)
            for q in range(6):
                n = NPRE + q
                k = n - NSLOT
                sp.wait_ge(s_pe, pe_at[f"z{Z_DONE[k] - 1}"] if k < len(ZP) else pe_at["xo1" if k == len(ZP) else "xo3"])
                piece(n, t["we"][0, q], PW)
                if q == 3:
                    sp.wait_ge(s_pe, pe_at[f"sc{NHEAD - 1}"])
                    sp.dma_start(xq[:, :], t["x"]).then_inc(s_x2, 16)
                    sp.wait_ge(s_pe, pe_at[f"y{NC - 1}"])
                    sp.dma_start(gmoe, t["gmoe"]).then_inc(s_gm, 16)
                    sp.wait_ge(s_dve, dve_at[f"o{NHEAD - 1}"])
                    sp.dma_start(bT.rearrange("p e n -> p (e n)"), t["bT"]).then_inc(s_bt, 16)
            sp.wait_ge(s_pe, pe_at["logits"])
            sp.wait_ge(s_dve, dve_at["tabs"])
            for q in range(2):
                sp.dma_start(wgate[:, q, :], t["wgate"][q]).then_inc(s_tail, 16)
            sp.dma_start(wproj.rearrange("p a n -> p (a n)"), t["wproj"]).then_inc(s_tail, 16)
            sp.dma_start(pTt.rearrange("p k t -> p (k t)"), t["pT"]).then_inc(s_tail, 16)
            sp.dma_start(gfin, t["gfin"]).then_inc(s_tail, 16)
            W = sp.value_load(EI[0:1, NITEM + 1:NITEM + 2], min_val=NE, max_val=NITEM)
            with sp.Fori(1, W) as i:
                e = sp.value_load(EI[0:1, bass.ds(i, 1)], min_val=0, max_val=NE - 1)
                for q in range(6):
                    sp.wait_ge(s_used, 6 * i - 5 + q)
                    slot = (NPRE + q) % NSLOT
                    sp.dma_start(ring[:, slot, :], t["we"][bass.ds(e, 1), q, :, :].rearrange("a p n -> (a p) n"))\
                        .then_inc(s_slot[slot], 16)
            for b in range(TB):
                sp.wait_ge(s_tdve, tdve_at[f"out{b}"])
                sp.dma_start(out[:, b, :], xs[:, b, :]).then_inc(s_out, 16)
            sp.wait_ge(s_out, 16 * TB)

        @block.tensor
        def _(pe):
            def fin(mm, name):
                finish(mm, "pe", name)

            ident = c_("ident")
            blk = c_("blk")
            pe.wait_ge(s_in, 48)
            pe.wait_ge(s_dve, dve_at["hn"])
            for k in range(KD):
                if k >= 4:
                    if k % 2:
                        pe.wait_ge(s_act, act_at[f"hT{k - 4}"])
                    else:
                        pe.wait_ge(s_dve, dve_at[f"hT{k - 4}"])
                for b in range(TB):
                    mm = pe.transpose(PS[:, k % 4, b * P:(b + 1) * P], hn[:, b, k * P:(k + 1) * P], ident)
                fin(mm, f"hT{k}")
            pe.wait_ge(s_act, act_at[f"hT{KD - 1}"])
            pe.wait_ge(s_dve, dve_at[f"hT{KD - 2}"])

            def z(n):
                if n >= 4:
                    pe.wait_ge(s_act, act_at[f"z{n - 4}"])
                piece = Z_PIECE[n] if n < NZ else 7
                first = n >= NZ or n == 0 or Z_PIECE[n - 1] != piece
                if first and n != NZ:
                    pe.wait_ge(s_slot[piece % NSLOT], 16 * (piece // NSLOT + 1))
                if n == NZ:
                    pe.wait_ge(s_aux, 64)
                width = ZP[piece][1]
                w = ring[:, piece % NSLOT, 0:KD * width].rearrange("p (k c) -> p k c", k=KD)
                at = (n - Z_PIECE.index(piece)) * P if n < NZ else 0
                for k in range(KD):
                    flags = dict(start=(k == 0), stop=(k == KD - 1))
                    if n < NZ:
                        mm = pe.matmul(bank(n % 4, SEQ), w[:, k, at:at + P], hT[:, k, :], **flags)
                    elif n == NZ:
                        mm = pe.matmul(PS[0:NHEAD, n % 4, 0:SEQ], wff[:, k, :], hT[:, k, :], **flags)
                    else:
                        b = n - NZ - 1
                        mm = pe.matmul(bank(n % 4), hT[:, k, b * P:(b + 1) * P], w[:, k, :], **flags)
                fin(mm, f"z{n}")

            def sums(b0, src, name):
                for j in range(NJ):
                    mm = pe.matmul(PS[:, b0 + j // 2, (j % 2) * SEQ:(j % 2 + 1) * SEQ], blk, src[:, j, :],
                                   start=True, stop=True)
                fin(mm, name)

            for n in range(6):
                z(n)
            pe.wait_ge(s_act, act_at["lz"])
            pe.wait_ge(s_aux, 64)
            for j in range(NJ):
                cols = slice((j % 2) * SEQ, (j % 2 + 1) * SEQ)
                pe.matmul(PS[:, 4 + j // 2, cols], lora[0:64, j * P:(j + 1) * P], LZ[0:64, 0, :], start=True, stop=True)
                mm = pe.matmul(PS[:, 6 + j // 2, cols], lora[64:P, j * P:(j + 1) * P], LZ[64:P, 0, :],
                               start=True, stop=True)
            fin(mm, "uwua")
            for n in range(6, 10):
                z(n)
            pe.wait_ge(s_act, act_at["swaa"])
            for j in range(NJ):
                mm = pe.matmul(PS[:, 4 + j // 2, (j % 2) * SEQ:(j % 2 + 1) * SEQ],
                               lora[:, FOXW + j * P:FOXW + (j + 1) * P], LZ[:, 1, :], start=True, stop=True)
            fin(mm, "g")
            pe.wait_ge(s_dve, dve_at["ksq"])
            sums(6, b4(7), "ssk")
            for n in range(10, 18):
                z(n)
            pe.wait_ge(s_dve, dve_at["bprod"])
            pe.wait_ge(s_act, act_at["nk"])
            sums(6, b4(7), "bn")
            for n in range(18, NZ + 3):
                z(n)

            def per_head(b0, lhs, rhs, n=CH):
                for g in range(16):
                    for h2 in range(2):
                        rows = slice(64 * h2, 64 * h2 + 64)
                        f = PSF[rows, b0 * 512 + g * n:b0 * 512 + (g + 1) * n]
                        mm = pe.matmul(f, lhs(rows, g), rhs(rows, g), start=True, stop=True)
                return mm

            def eye(rows, g):
                return con[rows, CONST["ident"][0] + rows.start:CONST["ident"][0] + rows.stop]

            def blocks(i):
                return lambda rows, g: b16(i)[rows, g, :]

            pe.wait_ge(s_dve, dve_at["tildes"])
            pe.wait_ge(s_act, act_at["g"])
            fin(per_head(4, blocks(2), eye), "vp")
            fin(per_head(6, blocks(4), eye), "bp")
            pe.wait_ge(s_act, act_at["vp"])
            fin(per_head(4, blocks(1), eye), "kp")
            pe.wait_ge(s_dve, dve_at["qsq"])
            pe.wait_ge(s_act, act_at[f"z{NZ + 2}"])
            sums(0, rzf.rearrange("p (j t) -> p j t", j=NJ), "qss")
            pe.wait_ge(s_act, act_at["kp"])

            def ar(rows, g):
                return AR[rows, g, :, :].rearrange("p s c -> p (s c)")

            fin(per_head(4, blocks(4), ar, 2 * CH), "ma")
            pe.wait_ge(s_dve, dve_at["ksqf"])
            sums(2, rzf.rearrange("p (j t) -> p j t", j=NJ), "kss")
            pe.wait_ge(s_dve, dve_at["at"])
            fin(per_head(4, blocks(1), ar, 2 * CH), "mk")
            pe.wait_ge(s_dve, dve_at["mk"])
            fin(per_head(4, lambda rows, g: AR[rows, g, 0, :], blocks(4)), "aa")

            def level(k):
                pe.wait_ge(s_dve, dve_at[f"mq{k}"])
                fin(per_head(4, blocks(1), blocks(8)), f"q{k}")
                pe.wait_ge(s_act, act_at[f"q{k}"])
                if k < 5:
                    fin(per_head(6, blocks(14), blocks(4)), f"t{k}")
                fin(per_head(4, blocks(4), blocks(14)), f"tt{k}")

            def head(h):
                j, rows = h // 2, slice(64 * (h % 2), 64 * (h % 2) + 64)
                dec = slice(rows.start, rows.start + 40)
                pe.wait_ge(s_dve, dve_at[f"ck{h}"])
                for b in range(TB):
                    o = PS[:, h % 2, b * P:(2 * b + 1) * P]
                    n = (b + 1) * P
                    pe.matmul(o, QT[rows, j, b * P:(b + 1) * P], KT[rows, j, 0:n], start=True, stop=False)
                    mm = pe.matmul(o, CQ[dec, b * P:(b + 1) * P], CKh[dec, 0:n], start=False, stop=True)
                fin(mm, f"sc{h}")
                pe.wait_ge(s_dve, dve_at[f"pr{h}"])
                for i in range(3):
                    mm = pe.transpose(PS[:, 2, i * P:(i + 1) * P], att[:, h % 2, i * P:(i + 1) * P], ident)
                fin(mm, f"pt{h}")
                pe.wait_ge(s_act, act_at[f"pt{h}"])
                if h % 2 == 0 and h >= 2:
                    pe.wait_ge(s_dve, dve_at[f"o{h - 1}"])
                v = slice(h * HD, (h + 1) * HD)
                pe.matmul(PS[rows, 3, 0:P], FV[:, 0, v], lzf[:, 0:P], start=True, stop=True)
                pe.matmul(PS[rows, 3, P:2 * P], FV[:, 0, v], lzf[:, P:2 * P], start=True, stop=False)
                mm = pe.matmul(PS[rows, 3, P:2 * P], FV[:, 1, v], lzf[:, 2 * P:3 * P], start=False, stop=True)
                fin(mm, f"o{h}")

            def chunk(c):
                def both(b0, pairs):
                    for j in range(NJ):
                        g = j * NC + c
                        for h2 in range(2):
                            rows = slice(64 * h2, 64 * h2 + 64)
                            for i, (lhs, rhs) in enumerate(pairs):
                                mm = pe.matmul(PS[rows, b0, j * 64:(j + 1) * 64], lhs(rows, g, j), rhs(rows, g, j),
                                               start=(i == 0), stop=(i == len(pairs) - 1))
                    return mm

                def blk_(i):
                    return lambda rows, g, j: b16(i)[rows, g, :]

                def of(x, s):
                    return lambda rows, g, j: x[rows, s, j * 64:(j + 1) * 64]

                def ar_(s):
                    return lambda rows, g, j: AR[rows, g, s, :]

                if c == 0:
                    pe.wait_ge(s_dve, dve_at["tt5"])
                else:
                    pe.wait_ge(s_dve, dve_at[f"s{c - 1}"])
                    pe.wait_ge(s_act, act_at[f"y{c - 1}"])
                fin(both(4, [(ar_(0), of(S, c % 2)), (blk_(2), blk_(3))]), f"x{c}")
                pe.wait_ge(s_act, act_at[f"x{c}"])
                fin(both(5, [(blk_(14), of(XU, 0))]), f"u{c}")
                pe.wait_ge(s_dve, dve_at[f"u{c}"])
                fin(both(7, [(blk_(6), of(XU, 1)), (blk_(7), blk_(3))]), f"d{c}")
                fin(both(6, [(of(S, c % 2), ar_(1)), (of(XU, 1), blk_(12)), (blk_(3), blk_(13))]), f"y{c}")

            for kind, n in MIX_ORDER:
                {"level": level, "head": head, "chunk": chunk}[kind](n)
            pe.wait_ge(s_act, act_at[f"y{NC - 1}"])
            sums(4, b4(8), "mean")
            pe.wait_ge(s_dve, dve_at["vsq"])
            sums(6, b4(1), "var")
            pe.wait_ge(s_dve, dve_at["mix"])
            for q in range(2):
                slot = (len(ZP) + q) % NSLOT
                pe.wait_ge(s_slot[slot], 32)
                w = ring[:, slot, :].rearrange("p (k c) -> p k c", k=KD)
                for b in range(TB):
                    for k in range(KD):
                        mm = pe.matmul(bank(2 * q + b), mixT[:, k, b * P:(b + 1) * P], w[:, k, :],
                                       start=(k == 0), stop=(k == KD - 1))
                    fin(mm, f"xo{2 * q + b}")
            pe.wait_ge(s_dve, dve_at["h2"])
            for k in range(KD):
                if k >= 4:
                    if k % 2:
                        pe.wait_ge(s_act, act_at[f"h2T{k - 4}"])
                    else:
                        pe.wait_ge(s_dve, dve_at[f"h2T{k - 4}"])
                for b in range(TB):
                    mm = pe.transpose(PS[:, 4 + k % 4, b * P:(b + 1) * P], H2[:, b, k * P:(k + 1) * P], ident)
                fin(mm, f"h2T{k}")
            pe.wait_ge(s_act, act_at[f"h2T{KD - 1}"])
            pe.wait_ge(s_dve, dve_at[f"h2T{KD - 2}"])
            for b in range(TB):
                for k in range(KD):
                    mm = pe.matmul(PS[:, 0, b * NE:(b + 1) * NE], h2T[:, k, b * P:(b + 1) * P], wr[:, k, :],
                                   start=(k == 0), stop=(k == KD - 1))
            fin(mm, "logits")
            pe.wait_ge(s_dve, dve_at["sel"])
            pe.matmul(PS[:, 1, 0:NE], c_("tri"), R[:, 2, :], start=True, stop=True)
            pe.matmul(PS[:, 1, NE:2 * NE], c_("tri"), R[:, 3, :], start=True, stop=False)
            fin(pe.matmul(PS[:, 1, NE:2 * NE], c_("ones")[:, 0:P], R[:, 2, :], start=False, stop=True), "rank")

            def rows4(i):
                return R[:, i:i + 4, :].rearrange("p a b -> p (a b)")

            pe.wait_ge(s_dve, dve_at["rr"])
            for b in range(TB):
                mm = pe.transpose(PS[:, 2, b * P:(b + 1) * P], rows4(4 + 4 * b), ident)
            fin(mm, "rrT")
            for b in range(TB):
                mm = pe.transpose(PS[:, 3, b * P:(b + 1) * P], rows4(12 + 4 * b), ident)
            fin(mm, "grT")
            for b in range(TB):
                mm = pe.matmul(PS[:, 4, 0:1], B[:, 2 + b, 0:P], c_("ones")[:, 0:1], start=(b == 0), stop=(b == 1))
            fin(mm, "count")
            pe.wait_ge(s_dve, dve_at["valid"])
            fin(pe.matmul(PS[:, 5, 0:1], c_("tri"), col[:, 20:21], start=True, stop=True), "pos")
            pe.wait_ge(s_dve, dve_at["oh"])
            pe.wait_ge(s_act, act_at["grT"])
            OH = B[:, 4, 0:IW]
            for b in range(TB):
                mm = pe.matmul(PS[:, 6, b * 64:b * 64 + IW], B[:, 5, b * P:(b + 1) * P], OH, start=True, stop=True)
            fin(mm, "ri")
            for b in range(TB):
                mm = pe.matmul(PS[:, 7, b * 64:b * 64 + IW], B[:, 6, b * P:(b + 1) * P], OH, start=True, stop=True)
            fin(mm, "gi")
            pe.matmul(PS[0:1, 1, 0:IW], c_("eval"), OH, start=True, stop=True)
            fin(pe.matmul(PS[0:1, 1, NITEM + 1:NITEM + 2], col[:, 20:21], c_("ones")[:, 0:1], start=True, stop=True), "ei")
            pe.wait_ge(s_dve, dve_at["tabs"])
            for g in range(4):
                pe.matmul(bank(g), S[:, 0, 0:P], S[:, 0:2, :].rearrange("p a b -> p (a b)"),
                          start=True, stop=True)

            def gather(n):
                pe.wait_ge(s_sel, n)
                for k in range(KD):
                    for b in range(TB):
                        pe.matmul(PS[:, 4, k * SLOTS:(k + 1) * SLOTS], H2[:, b, k * P:(k + 1) * P],
                                  PM[:, b, :], start=(b == 0), stop=(b == 1))
                for b in range(TB):
                    mm = pe.transpose(PS[0:SLOTS, 5, b * P:(b + 1) * P], PG[:, b, :], ident)
                mm.then_inc(s_gath, 1)

            gather(1)
            W = pe.value_load(EI[0:1, NITEM + 1:NITEM + 2], min_val=NE, max_val=NITEM)
            with pe.Fori(0, W) as i:
                pe.wait_ge(s_xg, i + 1)
                for q in range(6):
                    slot = (NPRE + q) % NSLOT
                    w = ring[:, slot, :].rearrange("p (k c) -> p k c", k=KD)
                    if q == 4:
                        gather(i + 2)
                        pe.wait_ge(s_eact, i + 1)
                    pe.wait_ge(s_slot[slot], 16 * i + 16 * (3 if slot < 4 else 2))
                    for f in range(4):
                        n = (q % 2) * 4 + f
                        o = PS[:, (6, 7, 6)[q // 2], n * SLOTS:(n + 1) * SLOTS]
                        for k in range(KD):
                            rhs = xg[:, k, :] if q < 4 else e_act[:, k * SLOTS:(k + 1) * SLOTS]
                            mm = pe.matmul(o, w[:, k, f * P:(f + 1) * P], rhs, start=(k == 0), stop=(k == KD - 1))
                    mm.then_inc(s_used, 1)
                pe.wait_ge(s_yb, i + 1)
                pe.wait_ge(s_xg, i + 2)
                for n in range(KD):
                    o = PS[0:SLOTS, 4 + n // 4, (n % 4) * P:(n % 4 + 1) * P]
                    if n == 0:
                        pe.matmul(o, e_y[:, 0:SLOTS], ident, start=True, stop=True)
                    else:
                        mm = pe.transpose(o, e_y[:, n * SLOTS:(n + 1) * SLOTS], ident)
                mm.then_inc(s_yt, 1)
                pe.wait_ge(s_ys, 2 * i + 2)
                pe.wait_ge(s_gt, i + 1)
                for b in range(TB):
                    for q in range(2):
                        mm = pe.matmul(bank(2 * q + b), GTs[:, 0, b * P:(b + 1) * P],
                                       ysb[:, q * 512:(q + 1) * 512], start=False, stop=False, skip_group_check=True)
                mm.then_inc(s_scat, 1)
            pe.wait_ge(s_tail, 80)
            for b in range(TB):
                for q in range(2):
                    for k in range(2):
                        mm = pe.matmul(bank(4 + 2 * b + q), pTt[:, k, b * P:(b + 1) * P],
                                       wproj[:, k, q * 512:(q + 1) * 512], start=(k == 0), stop=(k == 1))
            finish(mm, "tpe", "pp")
            pe.wait_ge(s_tdve, tdve_at["hn"])
            for k in range(KD):
                if k >= 4:
                    if k % 2:
                        pe.wait_ge(s_tact, tact_at[f"t{k - 4}"])
                    else:
                        pe.wait_ge(s_tdve, tdve_at[f"t{k - 4}"])
                for b in range(TB):
                    mm = pe.transpose(PS[:, k % 4, b * P:(b + 1) * P], H2[:, b, k * P:(k + 1) * P], ident)
                finish(mm, "tpe", f"t{k}")
            pe.wait_ge(s_tact, tact_at[f"t{KD - 1}"])
            pe.wait_ge(s_tdve, tdve_at[f"t{KD - 2}"])
            for b in range(TB):
                for q in range(2):
                    w = wgate[:, q, :].rearrange("p (k c) -> p k c", k=KD)
                    for k in range(KD):
                        mm = pe.matmul(bank(2 * b + q), hT[:, k, b * P:(b + 1) * P], w[:, k, :],
                                       start=(k == 0), stop=(k == KD - 1))
                finish(mm, "tpe", f"gate{b}")

        @block.scalar
        def _(act):
            chain = [0]

            def link(ins):
                chain[0] += 1
                ins.then_inc(s_al, 1)
                act.wait_ge(s_al, chain[0])

            def fin(ins, name):
                finish(ins, "act", name)

            def pe_done(name):
                act.wait_ge(s_pe, pe_at[name])

            eps = epsc[:, 0:1]
            act.wait_ge(s_in, 48)
            act.wait_ge(s_dve, dve_at["init"])
            for b in range(TB):
                ins = act.activation(hT[:, 4 * b:4 * b + 4, :].rearrange("p a b -> p (a b)"), xs[:, b, :], ACT.Square,
                                     accum_out=col[:, b:b + 1])
            fin(ins, "ssq")
            act.wait_ge(s_act, act_at["ssq"])
            fin(act.activation(col[:, 2:4], col[:, 0:2], ACT.Sqrt, bias=eps, scale=1.0 / D), "sd")
            for k in range(1, KD, 2):
                pe_done(f"hT{k}")
                fin(act.activation(hT[:, k, :], bank(k % 4, SEQ), ACT.Copy, scale=p_("mix", k)), f"hT{k}")

            def z(n):
                pe_done(f"z{n}")
                if n < N_SHIFT:
                    if n >= 4:
                        act.wait_ge(s_dve, dve_at[f"sh{n - 4}"])
                    fin(act.activation(rz[:, n % 4, 1:SEQ + 1], bank(n % 4, SEQ), ACT.Copy), f"z{n}")
                elif n < 18:
                    fin(act.activation(QT[:, n - 14, :], bank(n % 4, SEQ), ACT.Copy), f"z{n}")
                elif n < 22:
                    fin(act.activation(KT[:, n - 18, :], bank(n % 4, SEQ), ACT.Copy), f"z{n}")
                elif n < NZ:
                    fin(act.activation(FG[:, n - 22, :], bank(n % 4, SEQ), ACT.Sigmoid), f"z{n}")
                elif n == NZ:
                    fin(act.activation(tmp8[:, 0, :], PS[0:NHEAD, n % 4, 0:SEQ], ACT.Identity,
                                       bias=p_("fb")[0:NHEAD, :]), f"z{n}")
                else:
                    fin(act.activation(FV[:, n - NZ - 1, :], bank(n % 4), ACT.Copy), f"z{n}")

            for n in range(6):
                z(n)
            act.wait_ge(s_dve, dve_at["sh1"])
            act.activation(LZ[0:64, 0, :], LZ[0:64, 0, :], ACT.Tanh)
            fin(act.activation(LZ[:, 1, :], LZ[:, 1, :], ACT.Sigmoid), "lz")
            pe_done("uwua")
            for j in range(NJ):
                cols = slice((j % 2) * SEQ, (j % 2 + 1) * SEQ)
                act.activation(b4(3)[:, j, :], PS[:, 4 + j // 2, cols], ACT.Sigmoid, bias=p_("w0", j))
                ins = act.activation(b4(4)[:, j, :], PS[:, 6 + j // 2, cols], ACT.Sigmoid, bias=p_("a0", j))
            fin(ins, "swaa")
            for n in range(6, 10):
                z(n)
            pe_done("ssk")
            fin(act.activation(B[:, 7, :], two(6), ACT.Sqrt), "nk")
            act.wait_ge(s_dve, dve_at["scan"])
            act.activation(B[:, 3, :], B[:, 3, :], ACT.Exp, scale=-DECAY)
            act.activation(B[:, 9, :], B[:, 8, :], ACT.Exp, scale=-DECAY)
            fin(act.activation(B[:, 8, :], B[:, 8, :], ACT.Exp, scale=DECAY), "exps")
            pe_done("g")
            fin(act.activation(B[:, 5, :], two(4), ACT.Copy), "g")
            for n in range(10, NZ + 3):
                z(n)
            act.wait_ge(s_dve, dve_at["ffabs"])
            fin(act.activation(tmp8[:, 1, :], tmp8[:, 1, :], ACT.Exp, scale=-1.0), "ffe")
            act.wait_ge(s_act, act_at["ffe"])
            fin(act.activation(tmp8[:, 1, :], tmp8[:, 1, :], ACT.Ln, bias=1.0), "ffl")
            for name, i, b0 in (("vp", 3, 4), ("bp", 6, 6), ("kp", 7, 4)):
                pe_done(name)
                fin(act.activation(B[:, i, :], two(b0), ACT.Copy), name)
            pe_done("qss")
            fin(act.activation(rzf, two(0), ACT.Sqrt, bias=eps, scale=1.0 / HD), "qrs")
            pe_done("kss")
            fin(act.activation(rzf, two(2), ACT.Sqrt, bias=eps, scale=1.0 / HD), "krs")

            def level(k):
                pe_done(f"q{k}")
                fin(act.activation(B[:, 4, :], two(4), ACT.Copy), f"q{k}")

            def head(h):
                act.wait_ge(s_dve, dve_at[f"mx{h}"])
                act.activation(att[:, h % 2, 0:P], att[:, h % 2, 0:P], ACT.Exp, bias=col[:, 6:7],
                               accum_out=col[:, 8:9])
                fin(act.activation(att[:, h % 2, P:3 * P], att[:, h % 2, P:3 * P], ACT.Exp, bias=col[:, 7:8],
                                   accum_out=col[:, 9:10]), f"p{h}")
                pe_done(f"pt{h}")
                if h:
                    pe_done(f"o{h - 1}")
                fin(act.activation(lzf, PS[:, 2, 0:3 * P], ACT.Copy), f"pt{h}")

            def chunk(c):
                pe_done(f"x{c}")
                fin(act.activation(XU[:, 0, :], PS[:, 4, 0:256], ACT.Copy), f"x{c}")
                pe_done(f"y{c}")
                fin(act.activation(b4(8)[:, :, c * CH:(c + 1) * CH], PS[:, 6, 0:256].rearrange("p (j t) -> p j t", j=NJ),
                                   ACT.Copy), f"y{c}")

            for kind, n in MIX_ORDER:
                {"level": level, "head": head, "chunk": chunk}[kind](n)
            pe_done("var")
            fin(act.activation(B[:, 1, :], two(6), ACT.Sqrt, bias=epsc[:, 1:2], scale=1.0 / HD), "gsd")
            act.wait_ge(s_dve, dve_at["xo3"])
            for b in range(TB):
                ins = act.activation(B[:, b, :], xs[:, b, :], ACT.Square, accum_out=col[:, b:b + 1])
            fin(ins, "ssq2")
            act.wait_ge(s_act, act_at["ssq2"])
            fin(act.activation(col[:, 2:4], col[:, 0:2], ACT.Sqrt, bias=eps, scale=1.0 / D), "sd2")
            for k in range(1, KD, 2):
                pe_done(f"h2T{k}")
                fin(act.activation(h2T[:, k, :], PS[:, 4 + k % 4, 0:SEQ], ACT.Copy), f"h2T{k}")
            act.wait_ge(s_dve, dve_at["lg"])
            for b in range(TB):
                ins = act.activation(R[:, 20 + b, :], R[:, b, :], ACT.Exp, bias=col[:, 10 + b:11 + b])
            fin(ins, "lex")
            pe_done("grT")
            fin(act.activation(B[:, 6, 0:SEQ], PS[:, 3, 0:SEQ], ACT.Copy), "grT")

            def take():
                ins = act.activation(xg[:, :, :].rearrange("p k t -> p (k t)"), bank(4), ACT.Copy)
                ins.then_inc(s_xg, 1)

            act.wait_ge(s_gath, 1)
            act.activation(GTs[:, 0, :], PS[0:SLOTS, 5, 0:SEQ], ACT.Copy).then_inc(s_gt, 1)
            take()
            W = act.value_load(EI[0:1, NITEM + 1:NITEM + 2], min_val=NE, max_val=NITEM)
            with act.Fori(0, W) as i:
                act.wait_ge(s_glu, i + 1)
                act.activation(e_s, e_g, ACT.Sigmoid, scale=SALPHA).then_inc(s_sig, 1)
                act.wait_ge(s_used, 6 * i + 4)
                act.wait_ge(s_gath, i + 2)
                take()
                act.wait_ge(s_yt, i + 1)
                act.activation(ysb[:, 0:512], PS[0:SLOTS, 4, :], ACT.Copy).then_inc(s_ys, 1)
                act.wait_ge(s_scat, i + 1)
                act.activation(GTs[:, 0, :], GTs[:, 1, :], ACT.Copy).then_inc(s_gt, 1)
            def squares(name):
                for b in range(TB):
                    ins = act.activation(ht2[:, b * D:(b + 1) * D], xs[:, b, :], ACT.Square, accum_out=col[:, b:b + 1])
                finish(ins, "tact", name)
                act.wait_ge(s_tact, tact_at[name])

            act.wait_ge(s_tdve, tdve_at["x3"])
            squares("ssq")
            finish(act.activation(col[:, 2:4], col[:, 0:2], ACT.Sqrt, bias=eps, scale=1.0 / D), "tact", "sd")
            for k in range(1, KD, 2):
                act.wait_ge(s_tpe, tpe_at[f"t{k}"])
                finish(act.activation(hT[:, k, :], bank(k % 4, SEQ), ACT.Copy, scale=p_("ple", k)), "tact", f"t{k}")
            for b in range(TB):
                act.wait_ge(s_tpe, tpe_at[f"gate{b}"])
                finish(act.activation(H2[:, b, :], two(2 * b), ACT.Sigmoid), "tact", f"gate{b}")
            act.wait_ge(s_tdve, tdve_at["x41"])
            squares("ssq2")
            finish(act.activation(col[:, 2:4], col[:, 0:2], ACT.Sqrt, bias=eps, scale=1.0 / D), "tact", "sd2")

        @block.vector
        def _(v):
            chain = [0]

            def link(ins):
                chain[0] += 1
                ins.then_inc(s_vl, 1)
                v.wait_ge(s_vl, chain[0])

            def fin(ins, name):
                finish(ins, "dve", name)
                v.wait_ge(s_dve, dve_at[name])

            def pe_done(name):
                v.wait_ge(s_pe, pe_at[name])

            def act_done(name):
                v.wait_ge(s_act, act_at[name])

            def tt(o, a, b, op):
                return v.tensor_tensor(o, a, b, op)

            def bc(name, g=16):
                return c_(name).unsqueeze(1).to_broadcast([P, g, CH])

            v.memset(epsc[:, 0:1], EPS)
            v.memset(epsc[:, 1:2], GN_EPS)
            v.memset(rz[:, :, 0:1], 0.0)
            fin(v.memset(S[:, :, :], 0.0), "init")
            act_done("sd")
            v.wait_ge(s_in, 48)
            fin(v.reciprocal(col[:, 4:6], col[:, 2:4]), "rstd")
            for b in range(TB):
                ins = v.tensor_scalar(hn[:, b, :], xs[:, b, :], col[:, 4 + b:5 + b], None, ALU.mult)
            fin(ins, "hn")
            for k in range(0, KD, 2):
                pe_done(f"hT{k}")
                fin(v.tensor_scalar(hT[:, k, :], bank(k % 4, SEQ), p_("mix", k), None, ALU.mult), f"hT{k}")

            def shift(n):
                dst = LZ[:, n, :] if n < 2 else b4((1, 0, 2)[(n - 2) // 4])[:, (n - 2) % 4, :]
                act_done(f"z{n}")
                link(tt(dst, rz[:, n % 4, 0:SEQ], rz[:, n % 4, 1:SEQ + 1], ALU.subtract))
                fin(v.scalar_tensor_tensor(out=dst, in0=dst, scalar=p_("mu", n), in1=rz[:, n % 4, 1:SEQ + 1],
                                           op0=ALU.mult, op1=ALU.add), f"sh{n}")

            for n in range(6):
                shift(n)
            for j in range(NJ):
                ins = v.tensor_scalar(b4(6)[:, j, :], b4(1)[:, j, :], p_("k_k", j), None, ALU.mult)
            link(ins)
            fin(tt(B[:, 7, :], B[:, 6, :], B[:, 6, :], ALU.mult), "ksq")
            act_done("swaa")
            for j in range(NJ):
                ins = v.tensor_tensor_scan(b4(8)[:, j, :], c_("reset"), b4(3)[:, j, :], 0.0, ALU.mult, ALU.add)
            link(ins)
            fin(tt(B[:, 3, :], B[:, 8, :], B[:, 3, :], ALU.subtract), "scan")
            for n in range(6, 10):
                shift(n)
            act_done("nk")
            link(v.tensor_scalar(B[:, 7, :], B[:, 7, :], 1e-12, None, ALU.max))
            link(v.reciprocal(B[:, 7, :], B[:, 7, :]))
            fin(tt(B[:, 6, :], B[:, 6, :], B[:, 7, :], ALU.mult), "kk")
            for j in range(NJ):
                ins = v.tensor_scalar(b4(10)[:, j, :], b4(4)[:, j, :], -1.0, p_("k_a", j), ALU.add, ALU.mult)
            link(ins)
            link(v.scalar_tensor_tensor(out=B[:, 1, :], in0=B[:, 10, :], scalar=1.0, in1=B[:, 1, :],
                                        op0=ALU.add, op1=ALU.mult))
            for j in range(NJ):
                ins = v.scalar_tensor_tensor(out=b4(7)[:, j, :], in0=b4(0)[:, j, :], scalar=p_("r_k", j),
                                             in1=b4(1)[:, j, :], op0=ALU.mult, op1=ALU.mult)
            fin(ins, "bprod")
            for n in range(10, 14):
                shift(n)
            act_done("exps")
            tt(AR[:, :, 1, :], b16(0), b16(9), ALU.mult)
            v.scalar_tensor_tensor(out=AR[:, :, 0, :], in0=b16(6), scalar=-1.0, in1=b16(3),
                                   op0=ALU.mult, op1=ALU.mult)
            v.tensor_copy(WC[:, :].unsqueeze(2), b16(9)[:, :, CH - 1:CH])
            tt(B[:, 1, :], B[:, 1, :], B[:, 8, :], ALU.mult)
            link(tt(B[:, 4, :], B[:, 4, :], B[:, 6, :], ALU.mult))
            link(tt(B[:, 4, :], B[:, 4, :], B[:, 8, :], ALU.mult))
            pe_done("bn")
            fin(tt(B[:, 0, :], two(6), B[:, 2, :], ALU.mult), "tildes")
            link(v.memset(lora[:, 0:2 * SEQ], 0.0))
            for a in (0, 64):
                v.memset(CQ[a + 32:a + 40, :], 1.0)
                v.memset(CK[a:a + 8, :], 1.0)
            act_done(f"z{NZ}")
            link(v.tensor_scalar(tmp8[:, 1, :], tmp8[:, 0, :], -1.0, None, ALU.mult))
            link(tt(tmp8[:, 1, :], tmp8[:, 0, :], tmp8[:, 1, :], ALU.max))
            fin(v.tensor_scalar(tmp8[:, 2, :], tmp8[:, 0, :], 0.0, None, ALU.min), "ffabs")
            act_done("ffl")
            link(tt(tmp8[:, 0, :], tmp8[:, 2, :], tmp8[:, 1, :], ALU.subtract))
            link(v.tensor_tensor_scan(CQ[0:8, :], c_("ones")[0:8, :], tmp8[:, 0, :], 0.0, ALU.mult, ALU.add))
            v.tensor_copy(CQ[64:72, :], CQ[0:8, :])
            v.tensor_scalar(CK[96:104, :], CQ[0:8, :], -1.0, None, ALU.mult)
            fin(v.tensor_scalar(CK[32:40, :], CQ[0:8, :], -1.0, None, ALU.mult), "fc")
            act_done(f"z{NZ - 1}")
            fin(tt(rzf, xq[:, 0:D], xq[:, 0:D], ALU.mult), "qsq")

            def blocks4():
                return PSF[:, 2048:4096].rearrange("p (g s c) -> p g s c", g=16, s=2)

            pe_done("ma")
            tt(b16(9), blocks4()[:, :, 0, :], bc("strictT"), ALU.mult)
            fin(tt(b16(12), blocks4()[:, :, 1, :], bc("inclT"), ALU.mult), "at")
            act_done("qrs")

            def normalise(off, name, scale, step):
                link(v.reciprocal(rzf, rzf))
                link(tt(xq[:, off:off + D], xq[:, off:off + D], rzf, ALU.mult))
                fin(v.tensor_scalar(xq[:, off:off + D], xq[:, off:off + D], p_(name), scale, ALU.mult, ALU.mult), step)

            normalise(0, "qn", HD ** -0.5, "qn")
            fin(tt(rzf, xq[:, D:2 * D], xq[:, D:2 * D], ALU.mult), "ksqf")
            pe_done("mk")
            tt(b16(2), blocks4()[:, :, 0, :], bc("strictT"), ALU.mult)
            fin(tt(b16(13), blocks4()[:, :, 1, :], bc("inclT"), ALU.mult), "mk")
            act_done("krs")
            normalise(D, "kn", 1.0, "kn")
            pe_done("aa")
            tt(b16(8), banks16(4), bc("m0"), ALU.mult)
            link(tt(b16(14), b16(9), bc("m0T"), ALU.mult))
            tt(b16(8), b16(8), bc("eye"), ALU.add)
            fin(tt(b16(14), b16(14), bc("eye"), ALU.add), "aa")

            def level(k):
                fin(tt(b16(1), b16(9), bc(f"m{k}T"), ALU.mult), f"mq{k}")
                if k < 5:
                    pe_done(f"t{k}")
                    fin(tt(B[:, 8, :], two(6), B[:, 8, :], ALU.add), f"t{k}")
                pe_done(f"tt{k}")
                fin(tt(B[:, 14, :], two(4), B[:, 14, :], ALU.add), f"tt{k}")

            def head(h):
                if h >= 2:
                    pe_done(f"sc{h - 2}")
                a = CONST["delta"][0] + h
                dec = slice(64 * (h % 2), 64 * (h % 2) + 40)
                fin(v.tensor_scalar(CKh[dec, :], CK[dec, :], con[dec, a:a + 1], None, ALU.mult), f"ck{h}")
                pe_done(f"sc{h}")
                if h >= 2:
                    pe_done(f"pt{h - 2}")
                link(tt(att[:, h % 2, :], PS[:, h % 2, 0:3 * P], c_("causal"), ALU.add))
                v.tensor_reduce(col[:, 6:7], att[:, h % 2, 0:P], AX.X, ALU.max)
                link(v.tensor_reduce(col[:, 7:8], att[:, h % 2, P:3 * P], AX.X, ALU.max))
                fin(v.tensor_scalar(col[:, 6:8], col[:, 6:8], -1.0, None, ALU.mult), f"mx{h}")
                act_done(f"p{h}")
                link(v.reciprocal(col[:, 8:10], col[:, 8:10]))
                v.tensor_scalar(att[:, h % 2, 0:P], att[:, h % 2, 0:P], col[:, 8:9], None, ALU.mult)
                fin(v.tensor_scalar(att[:, h % 2, P:3 * P], att[:, h % 2, P:3 * P], col[:, 9:10], None, ALU.mult), f"pr{h}")
                if h % 2:
                    pe_done(f"o{h}")
                    j = h // 2
                    fin(tt(mixT[:, j, :], PS[:, 3, 0:SEQ], FG[:, j, :], ALU.mult), f"o{h}")

            def chunk(c):
                pe_done(f"u{c}")
                fin(v.tensor_copy(XU[:, 1, :], PS[:, 5, 0:256]), f"u{c}")
                pe_done(f"d{c}")
                if c:
                    pe_done(f"y{c - 1}")
                link(tt(S[:, (c + 1) % 2, :], PS[:, 7, 0:256], S[:, c % 2, :], ALU.add))
                nxt = S[:, (c + 1) % 2, :].rearrange("p (j n) -> p j n", j=NJ)
                w = WC[:, :].rearrange("p (j c) -> p j c", j=NJ)[:, :, c:c + 1].to_broadcast([P, NJ, HD])
                fin(tt(nxt, nxt, w, ALU.mult), f"s{c}")

            for kind, n in MIX_ORDER:
                {"level": level, "head": head, "chunk": chunk}[kind](n)
            pe_done("mean")
            fin(v.scalar_tensor_tensor(out=B[:, 8, :], in0=two(4), scalar=-1.0 / HD, in1=B[:, 8, :],
                                       op0=ALU.mult, op1=ALU.add), "cent")
            fin(tt(B[:, 1, :], B[:, 8, :], B[:, 8, :], ALU.mult), "vsq")
            act_done("gsd")
            link(v.reciprocal(B[:, 1, :], B[:, 1, :]))
            link(tt(B[:, 8, :], B[:, 8, :], B[:, 1, :], ALU.mult))
            for j in range(NJ):
                ins = v.tensor_scalar(b4(8)[:, j, :], b4(8)[:, j, :], p_("ln_w", j), p_("ln_b", j), ALU.mult, ALU.add)
            link(ins)
            link(tt(B[:, 8, :], B[:, 8, :], B[:, 0, :], ALU.add))
            v.memset(S[:, :, :], 0.0)
            fin(tt(mixT[:, NJ:2 * NJ, :], b4(8), b4(5), ALU.mult), "mix")
            v.wait_ge(s_x2, 16)
            for g in range(4):
                pe_done(f"xo{g}")
                q, b = g // 2, g % 2
                dst = xs[:, b, q * 512:(q + 1) * 512]
                fin(tt(dst, bank(g), dst, ALU.add), f"xo{g}")
            act_done("sd2")
            fin(v.reciprocal(col[:, 4:6], col[:, 2:4]), "rs2")
            v.wait_ge(s_gm, 16)
            for b in range(TB):
                ins = v.scalar_tensor_tensor(out=H2[:, b, :], in0=xs[:, b, :], scalar=col[:, 4 + b:5 + b], in1=gmoe,
                                             op0=ALU.mult, op1=ALU.mult)
            fin(ins, "h2")
            for k in range(0, KD, 2):
                pe_done(f"h2T{k}")
                fin(v.tensor_copy(h2T[:, k, :], PS[:, 4 + k % 4, 0:SEQ]), f"h2T{k}")
            pe_done("logits")
            v.wait_ge(s_aux, 64)
            LG = R[:, 0:2, :]
            link(tt(LG, PS[:, 0, 0:2 * NE].rearrange("p (b e) -> p b e", b=TB),
                    brt[:, :].unsqueeze(1).to_broadcast([P, TB, NE]), ALU.add))
            top = B[:, 7, 0:16].rearrange("p (b n) -> p b n", b=TB)
            for b in range(TB):
                ins = v.max(top[:, b, :], R[:, b, :])
            link(ins)
            fin(v.tensor_scalar(col[:, 10:12].unsqueeze(2), top[:, :, 0:1], -1.0, None, ALU.mult), "lg")
            gt, eq, cum = (B[:, 8, a * 64:a * 64 + 64].rearrange("p (b e) -> p b e", b=TB) for a in range(3))
            for b in range(TB):
                v.tensor_scalar(gt[:, b, :], R[:, b, :], top[:, b, 3:4], None, ALU.is_gt)
                ins = v.tensor_scalar(eq[:, b, :], R[:, b, :], top[:, b, 3:4], None, ALU.is_equal)
            link(ins)
            v.tensor_reduce(col[:, 12:14], gt, AX.X, ALU.add)
            for b in range(TB):
                ins = v.tensor_tensor_scan(cum[:, b, :], c_("ones")[:, 0:NE], eq[:, b, :], 0.0, ALU.mult, ALU.add)
            link(ins)
            for b in range(TB):
                ins = v.tensor_scalar(cum[:, b, :], cum[:, b, :], col[:, 12 + b:13 + b], float(TOPK), ALU.add, ALU.is_le)
            link(ins)
            link(tt(cum, cum, eq, ALU.mult))
            SEL = R[:, 2:4, :]
            fin(tt(SEL, cum, gt, ALU.add), "sel")
            act_done("lex")
            EX = R[:, 20:22, :]
            link(tt(EX, EX, SEL, ALU.mult))
            link(v.tensor_reduce(col[:, 14:16], EX, AX.X, ALU.add))
            link(v.reciprocal(col[:, 16:18], col[:, 14:16]))
            for b in range(TB):
                ins = v.tensor_scalar(EX[:, b, :], EX[:, b, :], col[:, 16 + b:17 + b], None, ALU.mult)
            link(ins)
            for b in range(TB):
                v.tensor_copy(R[:, 12 + 4 * b:16 + 4 * b, :], EX[:, b, :].unsqueeze(1).to_broadcast([P, NCH, NE]))
                ins = v.tensor_copy(B[:, 2 + b, 0:P].rearrange("p (c e) -> p c e", c=NCH),
                                    SEL[:, b, :].unsqueeze(1).to_broadcast([P, NCH, NE]))
            fin(ins, "gr")
            pe_done("rank")
            RT = R[:, 22:24, :]
            link(v.scalar_tensor_tensor(out=RT, in0=PS[:, 1, 0:2 * NE].rearrange("p (b e) -> p b e", b=TB), scalar=FAR,
                                        in1=SEL, op0=ALU.add, op1=ALU.mult))
            for b in range(TB):
                ins = tt(R[:, 4 + 4 * b:8 + 4 * b, :], RT[:, b, :].unsqueeze(1).to_broadcast([P, NCH, NE]),
                         c_("far").rearrange("p (c e) -> p c e", c=NCH), ALU.add)
            fin(ins, "rr")
            pe_done("rrT")
            fin(v.tensor_copy(B[:, 5, 0:SEQ], PS[:, 2, 0:SEQ]), "rrT")
            pe_done("count")
            fin(v.tensor_scalar(col[:, 20:21], PS[:, 4, 0:1], c_("thr"), None, ALU.is_gt), "valid")
            pe_done("pos")
            link(v.tensor_copy(col[:, 21:22], PS[:, 5, 0:1]))
            fin(v.tensor_scalar(B[:, 4, 0:IW], c_("iota_i"), col[:, 21:22], col[:, 20:21], ALU.is_equal, ALU.mult), "oh")
            pe_done("ei")
            v.tensor_copy(RI[:, :, :], PS[:, 6, 0:128].rearrange("p (b i) -> p i b", b=TB)[:, 0:IW, :])
            v.tensor_copy(GI[:, :, :], PS[:, 7, 0:128].rearrange("p (b i) -> p i b", b=TB)[:, 0:IW, :])
            fin(v.tensor_copy(EI[0:1, 0:NITEM + 2], PS[0:1, 1, 0:NITEM + 2]), "tabs")

            def select(i):
                for b in range(TB):
                    r, g = (RI[:, i, b:b + 1], GI[:, i, b:b + 1]) if isinstance(i, int) else \
                        (RI[:, bass.ds(i, 1), b], GI[:, bass.ds(i, 1), b])
                    v.tensor_scalar(PM[:, b, :], c_("iota_s"), r, None, ALU.is_equal)
                    ins = v.tensor_scalar(PG[:, b, :], c_("iota_s"), r, g, ALU.is_equal, ALU.mult)
                ins.then_inc(s_sel, 1)

            select(0)
            v.wait_ge(s_bt, 16)
            base = chain[0]
            LINKS = 6
            W = v.value_load(EI[0:1, NITEM + 1:NITEM + 2], min_val=NE, max_val=NITEM)
            with v.Fori(0, W) as i:
                e = v.value_load(EI[0:1, bass.ds(i, 1)], min_val=0, max_val=NE - 1)
                n = [0]

                def link_i(ins):
                    n[0] += 1
                    ins.then_inc(s_vl, 1)
                    v.wait_ge(s_vl, i * LINKS + (base + n[0]))

                link_i(v.tensor_copy(bcur[:, :].unsqueeze(1), bT[:, bass.ds(e, 1), :]))
                v.wait_ge(s_gath, i + 1)
                select(i + 1)

                def bias(a, o, b0):
                    return tt(o.rearrange("p (k t) -> p k t", k=KD), bank(b0).rearrange("p (k t) -> p k t", k=KD),
                              bcur[:, a:a + KD].unsqueeze(2).to_broadcast([P, KD, SLOTS]), ALU.add)

                v.wait_ge(s_used, 6 * i + 2)
                link_i(bias(0, e_g, 6))
                ins = v.tensor_scalar(e_g, e_g, LIMIT, None, ALU.min)
                ins.then_inc(s_glu, 1)
                v.wait_ge(s_sig, i + 1)
                link_i(tt(e_s, e_g, e_s, ALU.mult))
                v.wait_ge(s_used, 6 * i + 4)
                link_i(bias(KD, e_l, 7))
                link_i(v.tensor_scalar(e_l, e_l, LIMIT, -LIMIT, ALU.min, ALU.max))
                v.scalar_tensor_tensor(out=e_act, in0=e_l, scalar=1.0, in1=e_s, op0=ALU.add, op1=ALU.mult)\
                    .then_inc(s_eact, 1)
                v.wait_ge(s_gath, i + 2)
                v.wait_ge(s_gt, i + 1)
                link_i(v.tensor_copy(GTs[:, 1, :], PS[0:SLOTS, 5, 0:SEQ]))
                v.wait_ge(s_used, 6 * i + 6)
                bias(2 * KD, e_y, 6).then_inc(s_yb, 1)
                v.wait_ge(s_yt, i + 1)
                v.tensor_copy(ysb[:, 512:1024], PS[0:SLOTS, 5, :]).then_inc(s_ys, 1)
                assert n[0] == LINKS
            def fin_t(ins, name):
                finish(ins, "tdve", name)
                v.wait_ge(s_tdve, tdve_at[name])

            v.wait_ge(s_scat, W)
            v.wait_ge(s_gath, W + 1)
            for g in range(4):
                q, b = g // 2, g % 2
                dst = xs[:, b, q * 512:(q + 1) * 512]
                ins = tt(dst, bank(g), dst, ALU.add)
            fin_t(ins, "x3")
            v.wait_ge(s_tact, tact_at["sd"])
            fin_t(v.reciprocal(col[:, 4:6], col[:, 2:4]), "rstd")
            for b in range(TB):
                ins = v.tensor_scalar(H2[:, b, :], xs[:, b, :], col[:, 4 + b:5 + b], None, ALU.mult)
            fin_t(ins, "hn")
            for k in range(0, KD, 2):
                v.wait_ge(s_tpe, tpe_at[f"t{k}"])
                fin_t(v.tensor_scalar(hT[:, k, :], bank(k % 4, SEQ), p_("ple", k), None, ALU.mult), f"t{k}")
            for b in range(TB):
                v.wait_ge(s_tact, tact_at[f"gate{b}"])
                ins = tt(H2[:, b, :], two(4 + 2 * b), H2[:, b, :], ALU.mult)
                ins.then_inc(s_vt, 1)
                v.wait_ge(s_vt, b + 1)
                fin_t(tt(xs[:, b, :], xs[:, b, :], H2[:, b, :], ALU.add), f"x4{b}")
            v.wait_ge(s_tact, tact_at["sd2"])
            fin_t(v.reciprocal(col[:, 4:6], col[:, 2:4]), "rstd2")
            v.wait_ge(s_tail, 80)
            for b in range(TB):
                fin_t(v.scalar_tensor_tensor(out=xs[:, b, :], in0=xs[:, b, :], scalar=col[:, 4 + b:5 + b], in1=gfin,
                                             op0=ALU.mult, op1=ALU.mult), f"out{b}")


def constants(np):
    con = np.zeros((P, NCONST), np.float32)

    def put(name, a):
        con[:, CONST[name][0]:CONST[name][1]] = a

    p, f = np.arange(P)[:, None], np.arange(P)[None, :]
    s, t = (p % CH), np.arange(CH)[None, :]
    put("ident", p == f)
    put("blk", p // HD == f // HD)
    put("inclT", s <= t)
    put("strictT", s < t)
    for k in range(6):
        put(f"m{k}T", ((s ^ t) >> k == 1) & (t > s))
    put("m0", ((s ^ t) == 1) & (s > t))
    put("eye", s == t)
    causal = np.where(f <= p, 0.0, -1e30)
    put("causal", np.concatenate([causal, np.zeros((P, P)), causal], 1))
    put("reset", np.broadcast_to(np.arange(SEQ)[None, :] % CH != 0, (P, SEQ)))
    put("tri", p < f)
    put("ones", 1.0)
    put("iota_s", np.arange(SLOTS)[None, :])
    h = np.arange(NHEAD)[None, :]
    put("delta", (p % 64 == h) | (p % 64 == h + 32))
    put("iota_i", np.arange(IW)[None, :])
    c = p // NE
    put("thr", np.where(c == 0, -1, SLOTS * c))
    put("eval", p % NE)
    put("far", -(FAR + SLOTS * (f // NE)))
    return con


def kernel(**inputs):
    import numpy as np
    import concourse.bacc as bacc
    from concourse.bass_utils import run_bass_kernel_spmd as run

    a = {k: np.asarray(v) for k, v in inputs.items()}

    def chunks(w):
        n = w.shape[-1]
        return np.ascontiguousarray(w.reshape(-1, P, n).transpose(1, 0, 2).reshape(P, -1))

    def cols(w):
        return w.reshape(-1, P).T

    def rep(w):
        return np.ascontiguousarray(np.broadcast_to(w.reshape(1, -1), (P, w.size)))

    mu = a["rwkv_mu"][0]
    R_, K_, V_, L_ = mu[0:512], mu[512:1024], mu[1024:1536], mu[1536:1792]
    prm = np.zeros((P, NPARAM), np.float32)
    for name, w in [("mix", cols(a["mix_norm"][0])), ("ple", cols(a["ple_norm"][0])),
                    ("mu", cols(np.concatenate([L_, K_, R_, V_]))),
                    ("w0", cols(a["rwkv_w0"][0])), ("a0", cols(a["rwkv_a0"][0])), ("k_k", cols(a["rwkv_k_k"][0])),
                    ("k_a", cols(a["rwkv_k_a"][0])), ("r_k", cols(a["rwkv_r_k"][0].reshape(-1))),
                    ("ln_w", cols(a["rwkv_ln_w"][0])), ("ln_b", cols(a["rwkv_ln_b"][0])),
                    ("qn", np.tile(a["fox_q_norm"][0], 2)[:, None]), ("kn", np.tile(a["fox_k_norm"][0], 2)[:, None])]:
        prm[:, PARAM[name][0]:PARAM[name][1]] = w
    prm[0:NHEAD, PARAM["fb"][0]] = a["fox_f_bias"][0]
    w_in = a["w_in"][0]
    host = {"x": chunks(a["x"][0]), "con": constants(np), "prm": prm,
            "lora": np.concatenate([np.concatenate([a["rwkv_w2"][0], a["rwkv_a2"][0]], 0), a["rwkv_g2"][0]], 1),
            "wff": chunks(w_in[:, 4 * FOXW:4 * FOXW + NHEAD]), "wr": chunks(a["w_router"][0]),
            "brt": rep(a["b_router"]), "gmoe": rep(a["moe_norm"]), "gfin": rep(a["final_norm"]),
            "pT": chunks(a["p"][0, 0].T), "wproj": chunks(a["w_ple_proj"][0]),
            "wo": np.stack([chunks(a["w_out"][0][:, q * PW:(q + 1) * PW]) for q in range(2)]),
            "wgate": np.stack([chunks(a["w_ple_gate"][0][:, q * PW:(q + 1) * PW]) for q in range(2)])}
    for n, (c0, w) in enumerate(ZP):
        host[f"wz{n}"] = chunks(w_in[:, c0:c0 + w])
    gu = a["w_gu"][0].reshape(NE, KD, P, 4, PW).transpose(0, 3, 2, 1, 4).reshape(NE, 4, P, KD * PW)
    dn = a["w_down"][0].reshape(NE, KF, P, 2, PW).transpose(0, 3, 2, 1, 4).reshape(NE, 2, P, KF * PW)
    host["we"] = np.concatenate([gu, dn], 1)
    bias = np.concatenate([a["b_gu"][0], a["b_down"][0]], 1).reshape(NE, 24, P).transpose(2, 0, 1)
    host["bT"] = np.ascontiguousarray(bias.reshape(P, NE * 24))

    nc = bacc.Bacc("TRN2", target_bir_lowering=False, num_devices=1)
    arrays, t = {}, {}
    for name, w in host.items():
        w = np.ascontiguousarray(w)
        arrays[f"in_{name}"] = w
        t[name] = nc.dram_tensor(f"in_{name}", w.shape, mybir.dt.from_np(w.dtype), kind="ExternalInput").ap()
    out = nc.dram_tensor("out_0", (SEQ, D), F32, kind="ExternalOutput").ap()
    fox_rwkv7_moe_ple(nc, t, out.rearrange("(b p) d -> p b d", p=P))
    r = run(nc, [arrays], core_ids=[0])
    return r.results[0]["out_0"].reshape(1, SEQ, D)
```

```python
from contextlib import ExitStack

import concourse.bass as bass
from concourse import mybir

F32 = mybir.dt.float32
F16 = mybir.dt.float16
I32 = mybir.dt.int32
ALU = mybir.AluOpType
ACT = mybir.ActivationFunctionType
AX = mybir.AxisListType

P = 128
D = 1024
SEQ = 256
TB = SEQ // P
KD = D // P
PLE = 256
HD = 64
NHEAD = 8
NJ = NHEAD * HD // P
CH = 64
NC = SEQ // CH
NE = 32
TOPK = 4
FF = 1024
KF = FF // P
LIMIT = 7.0
SALPHA = 1.702
EPS = 1e-6
GN_EPS = 64e-5
DECAY = 0.6065306597126334
SLOTS = 64
NCH = SEQ // SLOTS
NITEM = NE + SEQ * TOPK // SLOTS
IW = NITEM + 1
NSLOT = 6
NRAW = 3
WSCALE = 64.0
MARKS = 3
PW = 512
FAR = 1000.0

FOXW, RW0 = NHEAD * HD, 4 * NHEAD * HD + NHEAD
ZP = [(RW0 + 3 * FOXW, 256), (RW0 + FOXW, PW), (RW0, PW), (RW0 + 2 * FOXW, PW),
      (0, PW), (FOXW, PW), (3 * FOXW, PW), (2 * FOXW, PW)]
NPRE = len(ZP) + 2
Z_PIECE = [0] * 2 + [1] * 4 + [2] * 4 + [3] * 4 + [4] * 4 + [5] * 4 + [6] * 4
NZ = len(Z_PIECE)
N_SHIFT = 14
Z_DONE = [2, 6, 10, 14, 18, 22, 26, NZ + 3]


def layout(spec):
    at, out = 0, {}
    for name, n in spec:
        out[name] = (at, at + n)
        at += n
    return out, at


CONST, NCONST = layout([("ident", P), ("blk", P), ("inclT", CH), ("strictT", CH), ("m0", CH)]
                       + [(f"m{k}T", CH) for k in range(6)]
                       + [("eye", CH), ("causal", 3 * P), ("reset", SEQ), ("tri", P), ("ones", SEQ),
                          ("iota_s", 2 * SLOTS), ("delta", NHEAD), ("iota_i", IW), ("thr", 1), ("eval", 1),
                          ("far", P)])
PARAM, NPARAM = layout([("mix", KD), ("ple", KD), ("mu", N_SHIFT), ("w0", NJ), ("a0", NJ), ("k_k", NJ),
                        ("k_a", NJ), ("r_k", NJ), ("ln_w", NJ), ("ln_b", NJ), ("qn", 1), ("kn", 1), ("fb", 1)])

LEVELS = range(1, 6)
PE_STEPS = ([f"hT{k}" for k in range(KD)] + ["z0", "z1"] + [f"z{n}" for n in range(2, 6)] + ["uwua"]
            + [f"z{n}" for n in range(6, 10)] + ["g", "ssk"] + [f"z{n}" for n in range(10, 18)] + ["bn"]
            + [f"z{n}" for n in range(18, NZ + 3)]
            + ["vp", "bp", "kp", "qss", "ma", "kss", "mk", "aa"])


def head_steps(h):
    return [f"sc{h}", f"pt{h}", f"o{h}"]


MIX_ORDER = []
for _i, _k in enumerate(LEVELS):
    MIX_ORDER += [("level", _k), ("head", _i)]
for _c in range(NC):
    MIX_ORDER += [("chunk", _c)] + ([("head", 5 + _c)] if 5 + _c < NHEAD else [])
for _kind, _n in MIX_ORDER:
    if _kind == "level":
        PE_STEPS += [f"q{_n}"] + ([f"t{_n}"] if _n < 5 else []) + [f"tt{_n}"]
    elif _kind == "head":
        PE_STEPS += head_steps(_n)
    else:
        PE_STEPS += [f"x{_n}", f"u{_n}", f"d{_n}", f"y{_n}"]
PE_STEPS += ["mean", "var", "xo0", "xo1", "xo2", "xo3"] + [f"h2T{k}" for k in range(KD)]
PE_STEPS += ["logits", "rank", "rrT", "grT", "count", "pos", "ri", "gi", "ei"]


def fox_rwkv7_moe_ple(nc, t, out):
    with ExitStack() as ctx:
        def sb(name, shape, dt=F32):
            return ctx.enter_context(nc.sbuf_tensor(name, shape, dt))

        def sem(name):
            return ctx.enter_context(nc.semaphore(name))

        PS = ctx.enter_context(nc.psum_tensor("PS", [P, 8, 512], F32))
        PSF = PS[:, :, :].rearrange("p b n -> p (b n)")
        ring = sb("ring", [P, NSLOT, KD * PW])
        con = sb("con", [P, NCONST])
        prm = sb("prm", [P, NPARAM])
        xq = sb("xq", [P, TB * D])
        hT = sb("hT", [P, KD, SEQ])
        B = sb("B", [P, 15, D])
        FG = sb("FG", [P, NJ, SEQ])
        FV = sb("FV", [P, TB, FOXW])
        rz = sb("rz", [P, 4, SEQ + 4])
        LZ = sb("LZ", [P, 2, SEQ])
        lora = sb("lora", [P, 2 * FOXW])
        wff = sb("wff", [P, KD, NHEAD])
        wr = sb("wr", [P, KD, NE])
        brt = sb("brt", [P, NE])
        S = sb("S", [P, 2, NJ * HD])
        XU = sb("XU", [P, 2, NJ * HD])
        WC = sb("WC", [P, NJ * NC])
        col = sb("col", [P, 32])
        epsc = sb("epsc", [P, 4])
        EI = sb("EI", [1, 64], I32)
        RI = sb("RI", [P, IW, TB])
        GI = sb("GI", [P, IW, TB])
        bcur = sb("bcur", [P, 16])
        bT = FG[:, :, :].rearrange("p a b -> p (a b)")[:, 0:NE * 16].rearrange("p (e n) -> p e n", n=16)

        def c_(name):
            return con[:, CONST[name][0]:CONST[name][1]]

        def p_(name, i=0):
            a = PARAM[name][0] + i
            return prm[:, a:a + 1]

        def b4(i):
            return B[:, i, :].rearrange("p (j t) -> p j t", j=NJ)

        def b16(i):
            return B[:, i, :].rearrange("p (g c) -> p g c", g=NJ * NC)

        def bank(b, w=512):
            return PS[:, b, 0:w]

        def banks16(b):
            return PSF[:, b * 512:b * 512 + 1024].rearrange("p (g c) -> p g c", g=16)

        def two(b):
            return PSF[:, b * 512:b * 512 + 1024]

        xs = xq[:, :].rearrange("p (b d) -> p b d", b=TB)
        QT = xq[:, 0:D].rearrange("p (j t) -> p j t", j=NJ)
        KT = xq[:, D:2 * D].rearrange("p (j t) -> p j t", j=NJ)
        hn = B[:, 0:2, :]
        AR = B[:, 10:12, :].rearrange("p a n -> p (a n)").rearrange("p (g s c) -> p g s c", g=16, s=2)
        rzf = rz[:, :, :].rearrange("p a b -> p (a b)")[:, 0:1024]
        att = rz[:, :, :].rearrange("p a b -> p (a b)")[:, 0:768].rearrange("p (s n) -> p s n", s=2)
        lzf = LZ[:, :, :].rearrange("p a b -> p (a b)")[:, 0:384]
        mixT = hT
        H2 = B[:, 10:12, :]
        H3 = B[:, 12:14, :]
        h2T = B[:, 0:2, :].rearrange("p a n -> p (a n)").rearrange("p (k t) -> p k t", k=KD)
        gmoe = B[:, 14, :]
        wgate = B[:, 0:8, :].rearrange("p (q a) n -> p q (a n)", q=2)
        wproj = B[:, 8:10, :]
        pTt = B[:, 14, 0:512].rearrange("p (k t) -> p k t", k=2)
        gfin = B[:, 10, :]
        bdn = ring[0:NE, NRAW, 0:D]
        ht2 = hT[:, :, :].rearrange("p a b -> p (a b)")
        e_g, e_s, e_l, e_act = (ht2[:, 512 * a:512 * a + 512] for a in range(4))
        fv2 = FV[:, :, :].rearrange("p a b -> p (a b)")

        def half(ap):
            return ap.bitcast(F16)

        HH = half(B[:, 12, :]).rearrange("p (b d) -> p b d", b=TB)
        HL = half(B[:, 13, :]).rearrange("p (b d) -> p b d", b=TB)
        xh, xl, ah, al = (half(fv2[:, a:a + 256]) for a in (0, 256, 512, 768))
        PM = half(rzf[:, 0:TB * SLOTS // 2]).rearrange("p (b t) -> p b t", b=TB)
        PG = rzf[:, 128:128 + 2 * TB * SLOTS].rearrange("p (b t) -> p b t", b=TB)
        GTs = rzf[:, 512:768]
        ysb = B[:, 11, 0:512]
        zpad = B[:, 11, 512:1024]
        CQ, CK, CKh = lora[:, 0:SEQ], lora[:, SEQ:2 * SEQ], lora[:, 2 * SEQ:3 * SEQ]
        tmp8 = B[0:8, 13, 0:768].rearrange("p (s t) -> p s t", s=3)
        R = B[:, 9, 0:24 * NE].rearrange("p (s e) -> p s e", e=NE)

        s_in = sem("inputs_landed")
        s_aux = sem("small_weights_landed")
        s_slot = [sem(f"slot{i}_landed") for i in range(NSLOT)]
        s_vt = sem("gated_projection_done")
        s_x2 = sem("x_again_landed")
        s_gm = sem("moe_gain_landed")
        s_bt = sem("expert_bias_landed")
        s_tail = sem("tail_weights_landed")
        s_pe = sem("tensor_steps_done")
        s_dve = sem("vector_steps_done")
        s_act = sem("scalar_steps_done")
        s_vl = sem("vector_op_done")
        s_al = sem("scalar_op_done")
        s_hi = sem("high_parts_split")
        s_lo = sem("low_parts_split")
        s_used = sem("expert_pieces_used")
        s_sel = sem("selection_built")
        s_gath = sem("tokens_gathered")
        s_xh = sem("gathered_high_parts")
        s_xl = sem("gathered_low_parts")
        s_gtp = sem("gate_matrix_transposed")
        s_gt = sem("gate_matrix_in_sbuf")
        s_glu = sem("glu_clamped")
        s_sig = sem("glu_sigmoid_done")
        s_eact = sem("expert_activation_done")
        s_ysb = sem("expert_output_in_sbuf")
        s_scat = sem("expert_output_added")
        s_tpe = sem("tail_tensor_steps_done")
        s_tdve = sem("tail_vector_steps_done")
        s_tact = sem("tail_scalar_steps_done")
        s_out = sem("output_stored")

        def value(names):
            return {n: i + 1 for i, n in enumerate(names)}

        pe_at = value(PE_STEPS)

        mixv, mixa = [], []
        for kind, n in MIX_ORDER:
            if kind == "level":
                mixv += [f"mq{n}"] + ([f"t{n}"] if n < 5 else []) + [f"tt{n}"]
                mixa += [f"q{n}"]
            elif kind == "head":
                mixv += [f"ck{n}", f"mx{n}", f"pr{n}"] + ([f"o{n}"] if n % 2 else [])
                mixa += [f"p{n}", f"pt{n}"]
            else:
                mixv += [f"u{n}", f"s{n}"]
                mixa += [f"x{n}", f"y{n}"]
        DVE_STEPS = (["init", "rstd", "hn"] + [f"hT{k}" for k in range(0, KD, 2)]
                     + [f"sh{n}" for n in range(6)] + ["ksq", "scan"] + [f"sh{n}" for n in range(6, 10)] + ["kk", "bprod"]
                     + [f"sh{n}" for n in range(10, 14)] + ["tildes", "ffabs", "fc", "qsq", "at", "qn", "ksqf", "mk", "kn", "aa"]
                     + mixv + ["cent", "vsq", "mix"] + [f"xo{g}" for g in range(4)]
                     + ["rs2", "h2"] + [f"h2T{k}" for k in range(0, KD, 2)]
                     + ["lg", "sel", "gr", "rr", "rrT", "valid", "oh", "tabs"])
        ACT_STEPS = (["ssq", "sd"] + [f"hT{k}" for k in range(1, KD, 2)]
                     + [f"z{n}" for n in range(6)] + ["lz", "swaa"] + [f"z{n}" for n in range(6, 10)] + ["nk", "exps", "g"]
                     + [f"z{n}" for n in range(10, NZ + 3)]
                     + ["ffe", "ffl", "vp", "bp", "kp", "qrs", "krs"] + mixa
                     + ["gsd", "ssq2", "sd2"] + [f"h2T{k}" for k in range(1, KD, 2)] + ["hh", "lex", "grT"])
        dve_at, act_at = value(DVE_STEPS), value(ACT_STEPS)
        TPE_STEPS = ["pp"] + [f"t{k}" for k in range(KD)] + ["gate0", "gate1"]
        TDVE_STEPS = ["x3", "rstd", "hn"] + [f"t{k}" for k in range(0, KD, 2)] + ["x40", "x41", "rstd2", "out0", "out1"]
        TACT_STEPS = ["ssq", "sd"] + [f"t{k}" for k in range(1, KD, 2)] + ["gate0", "gate1", "ssq2", "sd2"]
        tpe_at, tdve_at, tact_at = value(TPE_STEPS), value(TDVE_STEPS), value(TACT_STEPS)
        tables = {"dve": (DVE_STEPS, s_dve), "act": (ACT_STEPS, s_act), "pe": (PE_STEPS, s_pe),
                  "tdve": (TDVE_STEPS, s_tdve), "tact": (TACT_STEPS, s_tact), "tpe": (TPE_STEPS, s_tpe)}
        done = dict.fromkeys(tables, 0)

        def finish(ins, who, name):
            names, s = tables[who]
            assert names[done[who]] == name, (who, names[done[who]], name)
            done[who] += 1
            ins.then_inc(s, 1)

        block = ctx.enter_context(nc.Block())

        @block.sync
        def _(sp):
            sp.dma_start(xq[:, :], t["x"]).then_inc(s_in, 16)
            sp.dma_start(con[:, :], t["con"]).then_inc(s_in, 16)
            sp.dma_start(prm[:, :], t["prm"]).then_inc(s_in, 16)

            def piece(n, src, cols):
                sp.dma_start(ring[:, n % NSLOT, 0:KD * cols], src).then_inc(s_slot[n % NSLOT], 16)

            for n in range(NSLOT):
                piece(n, t[f"wz{n}"], ZP[n][1])
                if n == 0:
                    sp.dma_start(lora[:, :], t["lora"]).then_inc(s_aux, 16)
                    sp.dma_start(wff[:, :, :], t["wff"].rearrange("p (k n) -> p k n", k=KD)).then_inc(s_aux, 16)
                    sp.dma_start(wr[:, :, :], t["wr"].rearrange("p (k n) -> p k n", k=KD)).then_inc(s_aux, 16)
                    sp.dma_start(brt[:, :], t["brt"]).then_inc(s_aux, 16)
            for n, slot, before in ((6, 0, 1), (7, 1, 5), (8, 4, 17), (9, 5, 21)):
                sp.wait_ge(s_pe, pe_at[f"z{before}"])
                src = t[f"wz{n}"] if n < len(ZP) else t["wo"][n - len(ZP)]
                sp.dma_start(ring[:, slot, :], src).then_inc(s_slot[slot], 16)
            for q, before in ((0, 25), (1, NZ + 2), (2, 9)):
                sp.wait_ge(s_pe, pe_at[f"z{before}"])
                sp.dma_start(ring[:, q, :], t["we"][0, q]).then_inc(s_slot[q], 16)
            sp.wait_ge(s_pe, pe_at[f"sc{NHEAD - 1}"])
            sp.dma_start(xq[:, :], t["x"]).then_inc(s_x2, 16)
            sp.wait_ge(s_dve, dve_at[f"o{NHEAD - 1}"])
            sp.dma_start(bT.rearrange("p e n -> p (e n)"), t["bT"]).then_inc(s_bt, 16)
            sp.wait_ge(s_pe, pe_at[f"y{NC - 1}"])
            sp.dma_start(gmoe, t["gmoe"]).then_inc(s_gm, 16)
            sp.dma_start(bdn, t["bdn"]).then_inc(s_gm, 16)
            sp.wait_ge(s_dve, dve_at["lg"])
            sp.dma_start(pTt.rearrange("p k t -> p (k t)"), t["pT"]).then_inc(s_tail, 16)
            sp.dma_start(gfin, t["gfin"]).then_inc(s_tail, 16)
            sp.wait_ge(s_dve, dve_at["tabs"])
            sp.wait_ge(s_used, 1)
            for q in range(2):
                sp.dma_start(wgate[:, q, :], t["wgate"][q]).then_inc(s_tail, 16)
            sp.dma_start(wproj.rearrange("p a n -> p (a n)"), t["wproj"]).then_inc(s_tail, 16)
            for q in range(3, 6):
                sp.wait_ge(s_lo, q - 2)
                sp.dma_start(ring[:, q - 3, :], t["we"][0, q]).then_inc(s_slot[q - 3], 16)
            W = sp.value_load(EI[0:1, NITEM + 1:NITEM + 2], min_val=NE, max_val=NITEM)
            with sp.Fori(1, W) as i:
                e = sp.value_load(EI[0:1, bass.ds(i, 1)], min_val=0, max_val=NE - 1)
                for q in range(6):
                    sp.wait_ge(s_lo, 6 * i + q - 2)
                    sp.dma_start(ring[:, q % NRAW, :], t["we"][bass.ds(e, 1), q, :, :].rearrange("a p n -> (a p) n"))\
                        .then_inc(s_slot[q % NRAW], 16)
            for b in range(TB):
                sp.wait_ge(s_tdve, tdve_at[f"out{b}"])
                sp.dma_start(out[:, b, :], xs[:, b, :]).then_inc(s_out, 16)
            sp.wait_ge(s_out, 16 * TB)

        @block.tensor
        def _(pe):
            def fin(mm, name):
                finish(mm, "pe", name)

            ident = c_("ident")
            blk = c_("blk")
            pe.wait_ge(s_in, 48)
            pe.wait_ge(s_dve, dve_at["hn"])
            for k in range(KD):
                if k >= 4:
                    if k % 2:
                        pe.wait_ge(s_act, act_at[f"hT{k - 4}"])
                    else:
                        pe.wait_ge(s_dve, dve_at[f"hT{k - 4}"])
                for b in range(TB):
                    mm = pe.transpose(PS[:, k % 4, b * P:(b + 1) * P], hn[:, b, k * P:(k + 1) * P], ident)
                fin(mm, f"hT{k}")
            pe.wait_ge(s_act, act_at[f"hT{KD - 1}"])
            pe.wait_ge(s_dve, dve_at[f"hT{KD - 2}"])

            def z(n):
                if n >= 4:
                    pe.wait_ge(s_act, act_at[f"z{n - 4}"])
                piece = Z_PIECE[n] if n < NZ else 7
                first = n >= NZ or n == 0 or Z_PIECE[n - 1] != piece
                if first and n != NZ:
                    pe.wait_ge(s_slot[piece % NSLOT], 16 * (piece // NSLOT + 1))
                if n == NZ:
                    pe.wait_ge(s_aux, 64)
                width = ZP[piece][1]
                w = ring[:, piece % NSLOT, 0:KD * width].rearrange("p (k c) -> p k c", k=KD)
                at = (n - Z_PIECE.index(piece)) * P if n < NZ else 0
                for k in range(KD):
                    flags = dict(start=(k == 0), stop=(k == KD - 1))
                    if n < NZ:
                        mm = pe.matmul(bank(n % 4, SEQ), w[:, k, at:at + P], hT[:, k, :], **flags)
                    elif n == NZ:
                        mm = pe.matmul(PS[0:NHEAD, n % 4, 0:SEQ], wff[:, k, :], hT[:, k, :], **flags)
                    else:
                        b = n - NZ - 1
                        mm = pe.matmul(bank(n % 4), hT[:, k, b * P:(b + 1) * P], w[:, k, :], **flags)
                fin(mm, f"z{n}")

            def sums(b0, src, name):
                for j in range(NJ):
                    mm = pe.matmul(PS[:, b0 + j // 2, (j % 2) * SEQ:(j % 2 + 1) * SEQ], blk, src[:, j, :],
                                   start=True, stop=True)
                fin(mm, name)

            for n in range(6):
                z(n)
            pe.wait_ge(s_act, act_at["lz"])
            pe.wait_ge(s_aux, 64)
            for j in range(NJ):
                cols = slice((j % 2) * SEQ, (j % 2 + 1) * SEQ)
                pe.matmul(PS[:, 4 + j // 2, cols], lora[0:64, j * P:(j + 1) * P], LZ[0:64, 0, :], start=True, stop=True)
                mm = pe.matmul(PS[:, 6 + j // 2, cols], lora[64:P, j * P:(j + 1) * P], LZ[64:P, 0, :],
                               start=True, stop=True)
            fin(mm, "uwua")
            for n in range(6, 10):
                z(n)
            pe.wait_ge(s_act, act_at["swaa"])
            for j in range(NJ):
                mm = pe.matmul(PS[:, 4 + j // 2, (j % 2) * SEQ:(j % 2 + 1) * SEQ],
                               lora[:, FOXW + j * P:FOXW + (j + 1) * P], LZ[:, 1, :], start=True, stop=True)
            fin(mm, "g")
            pe.wait_ge(s_dve, dve_at["ksq"])
            sums(6, b4(7), "ssk")
            for n in range(10, 18):
                z(n)
            pe.wait_ge(s_dve, dve_at["bprod"])
            pe.wait_ge(s_act, act_at["nk"])
            sums(6, b4(7), "bn")
            for n in range(18, NZ + 3):
                z(n)

            def per_head(b0, lhs, rhs, n=CH):
                for g in range(16):
                    for h2 in range(2):
                        rows = slice(64 * h2, 64 * h2 + 64)
                        f = PSF[rows, b0 * 512 + g * n:b0 * 512 + (g + 1) * n]
                        mm = pe.matmul(f, lhs(rows, g), rhs(rows, g), start=True, stop=True)
                return mm

            def eye(rows, g):
                return con[rows, CONST["ident"][0] + rows.start:CONST["ident"][0] + rows.stop]

            def blocks(i):
                return lambda rows, g: b16(i)[rows, g, :]

            pe.wait_ge(s_dve, dve_at["tildes"])
            pe.wait_ge(s_act, act_at["g"])
            fin(per_head(4, blocks(2), eye), "vp")
            fin(per_head(6, blocks(4), eye), "bp")
            pe.wait_ge(s_act, act_at["vp"])
            fin(per_head(4, blocks(1), eye), "kp")
            pe.wait_ge(s_dve, dve_at["qsq"])
            pe.wait_ge(s_act, act_at[f"z{NZ + 2}"])
            sums(0, rzf.rearrange("p (j t) -> p j t", j=NJ), "qss")
            pe.wait_ge(s_act, act_at["kp"])

            def ar(rows, g):
                return AR[rows, g, :, :].rearrange("p s c -> p (s c)")

            fin(per_head(4, blocks(4), ar, 2 * CH), "ma")
            pe.wait_ge(s_dve, dve_at["ksqf"])
            sums(2, rzf.rearrange("p (j t) -> p j t", j=NJ), "kss")
            pe.wait_ge(s_dve, dve_at["at"])
            fin(per_head(4, blocks(1), ar, 2 * CH), "mk")
            pe.wait_ge(s_dve, dve_at["mk"])
            fin(per_head(4, lambda rows, g: AR[rows, g, 0, :], blocks(4)), "aa")

            def level(k):
                pe.wait_ge(s_dve, dve_at[f"mq{k}"])
                fin(per_head(4, blocks(1), blocks(8)), f"q{k}")
                pe.wait_ge(s_act, act_at[f"q{k}"])
                if k < 5:
                    fin(per_head(6, blocks(14), blocks(4)), f"t{k}")
                fin(per_head(4, blocks(4), blocks(14)), f"tt{k}")

            def head(h):
                j, rows = h // 2, slice(64 * (h % 2), 64 * (h % 2) + 64)
                dec = slice(rows.start, rows.start + 40)
                pe.wait_ge(s_dve, dve_at[f"ck{h}"])
                for b in range(TB):
                    o = PS[:, h % 2, b * P:(2 * b + 1) * P]
                    n = (b + 1) * P
                    pe.matmul(o, QT[rows, j, b * P:(b + 1) * P], KT[rows, j, 0:n], start=True, stop=False)
                    mm = pe.matmul(o, CQ[dec, b * P:(b + 1) * P], CKh[dec, 0:n], start=False, stop=True)
                fin(mm, f"sc{h}")
                pe.wait_ge(s_dve, dve_at[f"pr{h}"])
                for i in range(3):
                    mm = pe.transpose(PS[:, 2, i * P:(i + 1) * P], att[:, h % 2, i * P:(i + 1) * P], ident)
                fin(mm, f"pt{h}")
                pe.wait_ge(s_act, act_at[f"pt{h}"])
                if h % 2 == 0 and h >= 2:
                    pe.wait_ge(s_dve, dve_at[f"o{h - 1}"])
                v = slice(h * HD, (h + 1) * HD)
                pe.matmul(PS[rows, 3, 0:P], FV[:, 0, v], lzf[:, 0:P], start=True, stop=True)
                pe.matmul(PS[rows, 3, P:2 * P], FV[:, 0, v], lzf[:, P:2 * P], start=True, stop=False)
                mm = pe.matmul(PS[rows, 3, P:2 * P], FV[:, 1, v], lzf[:, 2 * P:3 * P], start=False, stop=True)
                fin(mm, f"o{h}")

            def chunk(c):
                def both(b0, pairs):
                    for j in range(NJ):
                        g = j * NC + c
                        for h2 in range(2):
                            rows = slice(64 * h2, 64 * h2 + 64)
                            for i, (lhs, rhs) in enumerate(pairs):
                                mm = pe.matmul(PS[rows, b0, j * 64:(j + 1) * 64], lhs(rows, g, j), rhs(rows, g, j),
                                               start=(i == 0), stop=(i == len(pairs) - 1))
                    return mm

                def blk_(i):
                    return lambda rows, g, j: b16(i)[rows, g, :]

                def of(x, s):
                    return lambda rows, g, j: x[rows, s, j * 64:(j + 1) * 64]

                def ar_(s):
                    return lambda rows, g, j: AR[rows, g, s, :]

                if c == 0:
                    pe.wait_ge(s_dve, dve_at["tt5"])
                else:
                    pe.wait_ge(s_dve, dve_at[f"s{c - 1}"])
                    pe.wait_ge(s_act, act_at[f"y{c - 1}"])
                fin(both(4, [(ar_(0), of(S, c % 2)), (blk_(2), blk_(3))]), f"x{c}")
                pe.wait_ge(s_act, act_at[f"x{c}"])
                fin(both(5, [(blk_(14), of(XU, 0))]), f"u{c}")
                pe.wait_ge(s_dve, dve_at[f"u{c}"])
                fin(both(7, [(blk_(6), of(XU, 1)), (blk_(7), blk_(3))]), f"d{c}")
                fin(both(6, [(of(S, c % 2), ar_(1)), (of(XU, 1), blk_(12)), (blk_(3), blk_(13))]), f"y{c}")

            for kind, n in MIX_ORDER:
                {"level": level, "head": head, "chunk": chunk}[kind](n)
            pe.wait_ge(s_act, act_at[f"y{NC - 1}"])
            sums(4, b4(8), "mean")
            pe.wait_ge(s_dve, dve_at["vsq"])
            sums(6, b4(1), "var")
            pe.wait_ge(s_dve, dve_at["mix"])
            for q in range(2):
                slot = 4 + q
                pe.wait_ge(s_slot[slot], 32)
                w = ring[:, slot, :].rearrange("p (k c) -> p k c", k=KD)
                for b in range(TB):
                    for k in range(KD):
                        mm = pe.matmul(bank(2 * q + b), mixT[:, k, b * P:(b + 1) * P], w[:, k, :],
                                       start=(k == 0), stop=(k == KD - 1))
                    fin(mm, f"xo{2 * q + b}")
            pe.wait_ge(s_dve, dve_at["h2"])
            for k in range(KD):
                if k >= 4:
                    if k % 2:
                        pe.wait_ge(s_act, act_at[f"h2T{k - 4}"])
                    else:
                        pe.wait_ge(s_dve, dve_at[f"h2T{k - 4}"])
                for b in range(TB):
                    mm = pe.transpose(PS[:, 4 + k % 4, b * P:(b + 1) * P], H2[:, b, k * P:(k + 1) * P], ident)
                fin(mm, f"h2T{k}")
            pe.wait_ge(s_act, act_at[f"h2T{KD - 1}"])
            pe.wait_ge(s_dve, dve_at[f"h2T{KD - 2}"])
            for b in range(TB):
                for k in range(KD):
                    mm = pe.matmul(PS[:, 0, b * NE:(b + 1) * NE], h2T[:, k, b * P:(b + 1) * P], wr[:, k, :],
                                   start=(k == 0), stop=(k == KD - 1))
            fin(mm, "logits")
            pe.wait_ge(s_dve, dve_at["sel"])
            pe.matmul(PS[:, 1, 0:NE], c_("tri"), R[:, 2, :], start=True, stop=True)
            pe.matmul(PS[:, 1, NE:2 * NE], c_("tri"), R[:, 3, :], start=True, stop=False)
            fin(pe.matmul(PS[:, 1, NE:2 * NE], c_("ones")[:, 0:P], R[:, 2, :], start=False, stop=True), "rank")

            def rows4(i):
                return R[:, i:i + 4, :].rearrange("p a b -> p (a b)")

            pe.wait_ge(s_dve, dve_at["rr"])
            for b in range(TB):
                mm = pe.transpose(PS[:, 2, b * P:(b + 1) * P], rows4(4 + 4 * b), ident)
            fin(mm, "rrT")
            for b in range(TB):
                mm = pe.transpose(PS[:, 3, b * P:(b + 1) * P], rows4(12 + 4 * b), ident)
            fin(mm, "grT")
            for b in range(TB):
                mm = pe.matmul(PS[:, 4, 0:1], B[:, 2 + b, 0:P], c_("ones")[:, 0:1], start=(b == 0), stop=(b == 1))
            fin(mm, "count")
            pe.wait_ge(s_dve, dve_at["valid"])
            fin(pe.matmul(PS[:, 5, 0:1], c_("tri"), col[:, 20:21], start=True, stop=True), "pos")
            pe.wait_ge(s_dve, dve_at["oh"])
            pe.wait_ge(s_act, act_at["grT"])
            OH = B[:, 4, 0:IW]
            for b in range(TB):
                mm = pe.matmul(PS[:, 6, b * 64:b * 64 + IW], B[:, 5, b * P:(b + 1) * P], OH, start=True, stop=True)
            fin(mm, "ri")
            for b in range(TB):
                mm = pe.matmul(PS[:, 7, b * 64:b * 64 + IW], B[:, 6, b * P:(b + 1) * P], OH, start=True, stop=True)
            fin(mm, "gi")
            pe.matmul(PS[0:1, 1, 0:IW], c_("eval"), OH, start=True, stop=True)
            fin(pe.matmul(PS[0:1, 1, NITEM + 1:NITEM + 2], col[:, 20:21], c_("ones")[:, 0:1], start=True, stop=True), "ei")
            pe.wait_ge(s_dve, dve_at["tabs"])
            pe.wait_ge(s_gm, 32)
            for b in range(TB):
                for q in range(2):
                    mm = pe.matmul(bank(2 * q + b), B[0:NE, 6, b * P:(b + 1) * P], bdn[:, q * 512:(q + 1) * 512],
                                   start=True, stop=True)
            for n in range(MARKS):
                mm = pe.matmul(bank(4), zpad[:, 0:P], zpad, start=True, stop=True)
                mm.then_inc(s_used, 1)

            def gather(n):
                pe.wait_ge(s_sel, n)
                for k in range(KD):
                    for a, src in enumerate((HH, HL)):
                        for b in range(TB):
                            mm = pe.matmul(PS[:, 6, k * SLOTS:(k + 1) * SLOTS], src[:, b, k * P:(k + 1) * P],
                                           PM[:, b, :], start=(a + b == 0), stop=(a + b == 2))
                mm.then_inc(s_gath, 1)

            def scatter():
                for b in range(TB):
                    for q in range(2):
                        rows = slice(64 * q, 64 * q + 64)
                        mm = pe.matmul(bank(2 * q + b), GTs[rows, b * P:(b + 1) * P], ysb[rows, :],
                                       start=False, stop=False, skip_group_check=True)
                mm.then_inc(s_scat, 1)

            def parts(q):
                w = half(ring[:, NRAW + q % NRAW, :]).rearrange("p (s k c) -> p s k c", s=2, k=KD)
                return w[:, 0], w[:, 1]

            gather(1)
            W = pe.value_load(EI[0:1, NITEM + 1:NITEM + 2], min_val=NE, max_val=NITEM)
            with pe.Fori(0, W) as i:
                pe.wait_ge(s_xl, i + 1)
                for q in range(4):
                    wh, wl = parts(q)
                    pe.wait_ge(s_lo, 6 * i + q + 1)
                    for f in range(4):
                        n = (q % 2) * 4 + f
                        o = PS[:, 6 + q // 2, n * SLOTS:(n + 1) * SLOTS]
                        cols = slice(f * P, (f + 1) * P)
                        for k in range(KD):
                            slots = slice(k * SLOTS, (k + 1) * SLOTS)
                            pe.matmul(o, wh[:, k, cols], xh[:, slots], start=(k == 0), stop=False)
                            pe.matmul(o, wh[:, k, cols], xl[:, slots], start=False, stop=False)
                            mm = pe.matmul(o, wl[:, k, cols], xh[:, slots], start=False, stop=(k == KD - 1))
                    mm.then_inc(s_used, 1)
                pe.wait_ge(s_glu, i + 1)
                gather(i + 2)
                pe.wait_ge(s_ysb, i + 1)
                pe.wait_ge(s_gt, i + 1)
                scatter()
                for b in range(TB):
                    mm = pe.transpose(PS[:, 5, b * P:(b + 1) * P], PG[:, b, :], ident)
                mm.then_inc(s_gtp, 1)
                pe.wait_ge(s_eact, i + 1)
                for q in range(4, 6):
                    wh, wl = parts(q)
                    pe.wait_ge(s_lo, 6 * i + q + 1)
                    o = PS[64 * (q - 4):64 * (q - 4) + 64, 4, :]
                    for k in range(KF):
                        slots = slice(k * SLOTS, (k + 1) * SLOTS)
                        pe.matmul(o, ah[:, slots], wh[:, k, :], start=(k == 0), stop=False)
                        pe.matmul(o, ah[:, slots], wl[:, k, :], start=False, stop=False)
                        mm = pe.matmul(o, al[:, slots], wh[:, k, :], start=False, stop=(k == KF - 1))
                    mm.then_inc(s_used, 1)
            pe.wait_ge(s_ysb, W + 1)
            pe.wait_ge(s_gt, W + 1)
            scatter()
            pe.wait_ge(s_tail, 80)
            for b in range(TB):
                for q in range(2):
                    for k in range(2):
                        mm = pe.matmul(bank(4 + 2 * b + q), pTt[:, k, b * P:(b + 1) * P],
                                       wproj[:, k, q * 512:(q + 1) * 512], start=(k == 0), stop=(k == 1))
            finish(mm, "tpe", "pp")
            pe.wait_ge(s_tdve, tdve_at["hn"])
            for k in range(KD):
                if k >= 4:
                    if k % 2:
                        pe.wait_ge(s_tact, tact_at[f"t{k - 4}"])
                    else:
                        pe.wait_ge(s_tdve, tdve_at[f"t{k - 4}"])
                for b in range(TB):
                    mm = pe.transpose(PS[:, k % 4, b * P:(b + 1) * P], H3[:, b, k * P:(k + 1) * P], ident)
                finish(mm, "tpe", f"t{k}")
            pe.wait_ge(s_tact, tact_at[f"t{KD - 1}"])
            pe.wait_ge(s_tdve, tdve_at[f"t{KD - 2}"])
            for b in range(TB):
                for q in range(2):
                    w = wgate[:, q, :].rearrange("p (k c) -> p k c", k=KD)
                    for k in range(KD):
                        mm = pe.matmul(bank(2 * b + q), hT[:, k, b * P:(b + 1) * P], w[:, k, :],
                                       start=(k == 0), stop=(k == KD - 1))
                finish(mm, "tpe", f"gate{b}")

        @block.scalar
        def _(act):
            chain = [0]

            def link(ins):
                chain[0] += 1
                ins.then_inc(s_al, 1)
                act.wait_ge(s_al, chain[0])

            def fin(ins, name):
                finish(ins, "act", name)

            def pe_done(name):
                act.wait_ge(s_pe, pe_at[name])

            eps = epsc[:, 0:1]
            act.wait_ge(s_in, 48)
            act.wait_ge(s_dve, dve_at["init"])
            for b in range(TB):
                ins = act.activation(hT[:, 4 * b:4 * b + 4, :].rearrange("p a b -> p (a b)"), xs[:, b, :], ACT.Square,
                                     accum_out=col[:, b:b + 1])
            fin(ins, "ssq")
            act.wait_ge(s_act, act_at["ssq"])
            fin(act.activation(col[:, 2:4], col[:, 0:2], ACT.Sqrt, bias=eps, scale=1.0 / D), "sd")
            for k in range(1, KD, 2):
                pe_done(f"hT{k}")
                fin(act.activation(hT[:, k, :], bank(k % 4, SEQ), ACT.Copy, scale=p_("mix", k)), f"hT{k}")

            def z(n):
                pe_done(f"z{n}")
                if n < N_SHIFT:
                    if n >= 4:
                        act.wait_ge(s_dve, dve_at[f"sh{n - 4}"])
                    fin(act.activation(rz[:, n % 4, 1:SEQ + 1], bank(n % 4, SEQ), ACT.Copy), f"z{n}")
                elif n < 18:
                    fin(act.activation(QT[:, n - 14, :], bank(n % 4, SEQ), ACT.Copy), f"z{n}")
                elif n < 22:
                    fin(act.activation(KT[:, n - 18, :], bank(n % 4, SEQ), ACT.Copy), f"z{n}")
                elif n < NZ:
                    fin(act.activation(FG[:, n - 22, :], bank(n % 4, SEQ), ACT.Sigmoid), f"z{n}")
                elif n == NZ:
                    fin(act.activation(tmp8[:, 0, :], PS[0:NHEAD, n % 4, 0:SEQ], ACT.Identity,
                                       bias=p_("fb")[0:NHEAD, :]), f"z{n}")
                else:
                    fin(act.activation(FV[:, n - NZ - 1, :], bank(n % 4), ACT.Copy), f"z{n}")

            for n in range(6):
                z(n)
            act.wait_ge(s_dve, dve_at["sh1"])
            act.activation(LZ[0:64, 0, :], LZ[0:64, 0, :], ACT.Tanh)
            fin(act.activation(LZ[:, 1, :], LZ[:, 1, :], ACT.Sigmoid), "lz")
            pe_done("uwua")
            for j in range(NJ):
                cols = slice((j % 2) * SEQ, (j % 2 + 1) * SEQ)
                act.activation(b4(3)[:, j, :], PS[:, 4 + j // 2, cols], ACT.Sigmoid, bias=p_("w0", j))
                ins = act.activation(b4(4)[:, j, :], PS[:, 6 + j // 2, cols], ACT.Sigmoid, bias=p_("a0", j))
            fin(ins, "swaa")
            for n in range(6, 10):
                z(n)
            pe_done("ssk")
            fin(act.activation(B[:, 7, :], two(6), ACT.Sqrt), "nk")
            act.wait_ge(s_dve, dve_at["scan"])
            act.activation(B[:, 3, :], B[:, 3, :], ACT.Exp, scale=-DECAY)
            act.activation(B[:, 9, :], B[:, 8, :], ACT.Exp, scale=-DECAY)
            fin(act.activation(B[:, 8, :], B[:, 8, :], ACT.Exp, scale=DECAY), "exps")
            pe_done("g")
            fin(act.activation(B[:, 5, :], two(4), ACT.Copy), "g")
            for n in range(10, NZ + 3):
                z(n)
            act.wait_ge(s_dve, dve_at["ffabs"])
            fin(act.activation(tmp8[:, 1, :], tmp8[:, 1, :], ACT.Exp, scale=-1.0), "ffe")
            act.wait_ge(s_act, act_at["ffe"])
            fin(act.activation(tmp8[:, 1, :], tmp8[:, 1, :], ACT.Ln, bias=1.0), "ffl")
            for name, i, b0 in (("vp", 3, 4), ("bp", 6, 6), ("kp", 7, 4)):
                pe_done(name)
                fin(act.activation(B[:, i, :], two(b0), ACT.Copy), name)
            pe_done("qss")
            fin(act.activation(rzf, two(0), ACT.Sqrt, bias=eps, scale=1.0 / HD), "qrs")
            pe_done("kss")
            fin(act.activation(rzf, two(2), ACT.Sqrt, bias=eps, scale=1.0 / HD), "krs")

            def level(k):
                pe_done(f"q{k}")
                fin(act.activation(B[:, 4, :], two(4), ACT.Copy), f"q{k}")

            def head(h):
                act.wait_ge(s_dve, dve_at[f"mx{h}"])
                act.activation(att[:, h % 2, 0:P], att[:, h % 2, 0:P], ACT.Exp, bias=col[:, 6:7],
                               accum_out=col[:, 8:9])
                fin(act.activation(att[:, h % 2, P:3 * P], att[:, h % 2, P:3 * P], ACT.Exp, bias=col[:, 7:8],
                                   accum_out=col[:, 9:10]), f"p{h}")
                pe_done(f"pt{h}")
                if h:
                    pe_done(f"o{h - 1}")
                fin(act.activation(lzf, PS[:, 2, 0:3 * P], ACT.Copy), f"pt{h}")

            def chunk(c):
                pe_done(f"x{c}")
                fin(act.activation(XU[:, 0, :], PS[:, 4, 0:256], ACT.Copy), f"x{c}")
                pe_done(f"y{c}")
                fin(act.activation(b4(8)[:, :, c * CH:(c + 1) * CH], PS[:, 6, 0:256].rearrange("p (j t) -> p j t", j=NJ),
                                   ACT.Copy), f"y{c}")

            for kind, n in MIX_ORDER:
                {"level": level, "head": head, "chunk": chunk}[kind](n)
            pe_done("var")
            fin(act.activation(B[:, 1, :], two(6), ACT.Sqrt, bias=epsc[:, 1:2], scale=1.0 / HD), "gsd")
            act.wait_ge(s_dve, dve_at["xo3"])
            for b in range(TB):
                ins = act.activation(B[:, b, :], xs[:, b, :], ACT.Square, accum_out=col[:, b:b + 1])
            fin(ins, "ssq2")
            act.wait_ge(s_act, act_at["ssq2"])
            fin(act.activation(col[:, 2:4], col[:, 0:2], ACT.Sqrt, bias=eps, scale=1.0 / D), "sd2")
            for k in range(1, KD, 2):
                pe_done(f"h2T{k}")
                fin(act.activation(h2T[:, k, :], PS[:, 4 + k % 4, 0:SEQ], ACT.Copy), f"h2T{k}")
            fin(act.activation(HH[:, :, :].rearrange("p b d -> p (b d)"), H2.rearrange("p b d -> p (b d)"), ACT.Copy),
                "hh")
            act.wait_ge(s_dve, dve_at["lg"])
            for b in range(TB):
                ins = act.activation(R[:, 20 + b, :], R[:, b, :], ACT.Exp, bias=col[:, 10 + b:11 + b])
            fin(ins, "lex")
            pe_done("grT")
            fin(act.activation(B[:, 6, 0:SEQ], PS[:, 3, 0:SEQ], ACT.Copy), "grT")


            def gathered(n):
                act.wait_ge(s_gath, n)
                act.activation(xh, bank(6), ACT.Copy).then_inc(s_xh, 1)

            def output(n):
                act.wait_ge(s_used, n)
                act.activation(ysb, bank(4), ACT.Copy, scale=1.0 / WSCALE).then_inc(s_ysb, 1)

            gathered(1)
            W = act.value_load(EI[0:1, NITEM + 1:NITEM + 2], min_val=NE, max_val=NITEM)
            with act.Fori(0, W) as i:
                def high(q):
                    act.wait_ge(s_slot[q % NRAW], 32 * i + 16 * ((2, 2, 1)[q % NRAW] + q // NRAW + 1))
                    act.wait_ge(s_used, 6 * i + q + MARKS - 2)
                    act.activation(half(ring[:, NRAW + q % NRAW, 0:2048]), ring[:, q % NRAW, :], ACT.Copy,
                                   scale=WSCALE).then_inc(s_hi, 1)

                high(0)
                high(1)
                output(6 * i + MARKS)
                high(2)
                high(3)
                act.wait_ge(s_glu, i + 1)
                act.activation(e_s, e_g, ACT.Sigmoid, scale=SALPHA).then_inc(s_sig, 1)
                high(4)
                act.wait_ge(s_used, 6 * i + 4 + MARKS)
                gathered(i + 2)
                high(5)
            output(6 * W + MARKS)
            def squares(name):
                for b in range(TB):
                    ins = act.activation(ht2[:, b * D:(b + 1) * D], xs[:, b, :], ACT.Square, accum_out=col[:, b:b + 1])
                finish(ins, "tact", name)
                act.wait_ge(s_tact, tact_at[name])

            act.wait_ge(s_tdve, tdve_at["x3"])
            squares("ssq")
            finish(act.activation(col[:, 2:4], col[:, 0:2], ACT.Sqrt, bias=eps, scale=1.0 / D), "tact", "sd")
            for k in range(1, KD, 2):
                act.wait_ge(s_tpe, tpe_at[f"t{k}"])
                finish(act.activation(hT[:, k, :], bank(k % 4, SEQ), ACT.Copy, scale=p_("ple", k)), "tact", f"t{k}")
            for b in range(TB):
                act.wait_ge(s_tpe, tpe_at[f"gate{b}"])
                finish(act.activation(H3[:, b, :], two(2 * b), ACT.Sigmoid), "tact", f"gate{b}")
            act.wait_ge(s_tdve, tdve_at["x41"])
            squares("ssq2")
            finish(act.activation(col[:, 2:4], col[:, 0:2], ACT.Sqrt, bias=eps, scale=1.0 / D), "tact", "sd2")

        @block.vector
        def _(v):
            chain = [0]

            def link(ins):
                chain[0] += 1
                ins.then_inc(s_vl, 1)
                v.wait_ge(s_vl, chain[0])

            def fin(ins, name):
                finish(ins, "dve", name)
                v.wait_ge(s_dve, dve_at[name])

            def pe_done(name):
                v.wait_ge(s_pe, pe_at[name])

            def act_done(name):
                v.wait_ge(s_act, act_at[name])

            def tt(o, a, b, op):
                return v.tensor_tensor(o, a, b, op)

            def bc(name, g=16):
                return c_(name).unsqueeze(1).to_broadcast([P, g, CH])

            v.memset(epsc[:, 0:1], EPS)
            v.memset(epsc[:, 1:2], GN_EPS)
            v.memset(rz[:, :, 0:1], 0.0)
            fin(v.memset(S[:, :, :], 0.0), "init")
            act_done("sd")
            v.wait_ge(s_in, 48)
            fin(v.reciprocal(col[:, 4:6], col[:, 2:4]), "rstd")
            for b in range(TB):
                ins = v.tensor_scalar(hn[:, b, :], xs[:, b, :], col[:, 4 + b:5 + b], None, ALU.mult)
            fin(ins, "hn")
            for k in range(0, KD, 2):
                pe_done(f"hT{k}")
                fin(v.tensor_scalar(hT[:, k, :], bank(k % 4, SEQ), p_("mix", k), None, ALU.mult), f"hT{k}")

            def shift(n):
                dst = LZ[:, n, :] if n < 2 else b4((1, 0, 2)[(n - 2) // 4])[:, (n - 2) % 4, :]
                act_done(f"z{n}")
                link(tt(dst, rz[:, n % 4, 0:SEQ], rz[:, n % 4, 1:SEQ + 1], ALU.subtract))
                fin(v.scalar_tensor_tensor(out=dst, in0=dst, scalar=p_("mu", n), in1=rz[:, n % 4, 1:SEQ + 1],
                                           op0=ALU.mult, op1=ALU.add), f"sh{n}")

            for n in range(6):
                shift(n)
            for j in range(NJ):
                ins = v.tensor_scalar(b4(6)[:, j, :], b4(1)[:, j, :], p_("k_k", j), None, ALU.mult)
            link(ins)
            fin(tt(B[:, 7, :], B[:, 6, :], B[:, 6, :], ALU.mult), "ksq")
            act_done("swaa")
            for j in range(NJ):
                ins = v.tensor_tensor_scan(b4(8)[:, j, :], c_("reset"), b4(3)[:, j, :], 0.0, ALU.mult, ALU.add)
            link(ins)
            fin(tt(B[:, 3, :], B[:, 8, :], B[:, 3, :], ALU.subtract), "scan")
            for n in range(6, 10):
                shift(n)
            act_done("nk")
            link(v.tensor_scalar(B[:, 7, :], B[:, 7, :], 1e-12, None, ALU.max))
            link(v.reciprocal(B[:, 7, :], B[:, 7, :]))
            fin(tt(B[:, 6, :], B[:, 6, :], B[:, 7, :], ALU.mult), "kk")
            for j in range(NJ):
                ins = v.tensor_scalar(b4(10)[:, j, :], b4(4)[:, j, :], -1.0, p_("k_a", j), ALU.add, ALU.mult)
            link(ins)
            link(v.scalar_tensor_tensor(out=B[:, 1, :], in0=B[:, 10, :], scalar=1.0, in1=B[:, 1, :],
                                        op0=ALU.add, op1=ALU.mult))
            for j in range(NJ):
                ins = v.scalar_tensor_tensor(out=b4(7)[:, j, :], in0=b4(0)[:, j, :], scalar=p_("r_k", j),
                                             in1=b4(1)[:, j, :], op0=ALU.mult, op1=ALU.mult)
            fin(ins, "bprod")
            for n in range(10, 14):
                shift(n)
            act_done("exps")
            tt(AR[:, :, 1, :], b16(0), b16(9), ALU.mult)
            v.scalar_tensor_tensor(out=AR[:, :, 0, :], in0=b16(6), scalar=-1.0, in1=b16(3),
                                   op0=ALU.mult, op1=ALU.mult)
            v.tensor_copy(WC[:, :].unsqueeze(2), b16(9)[:, :, CH - 1:CH])
            tt(B[:, 1, :], B[:, 1, :], B[:, 8, :], ALU.mult)
            link(tt(B[:, 4, :], B[:, 4, :], B[:, 6, :], ALU.mult))
            link(tt(B[:, 4, :], B[:, 4, :], B[:, 8, :], ALU.mult))
            pe_done("bn")
            fin(tt(B[:, 0, :], two(6), B[:, 2, :], ALU.mult), "tildes")
            link(v.memset(lora[:, 0:2 * SEQ], 0.0))
            for a in (0, 64):
                v.memset(CQ[a + 32:a + 40, :], 1.0)
                v.memset(CK[a:a + 8, :], 1.0)
            act_done(f"z{NZ}")
            link(v.tensor_scalar(tmp8[:, 1, :], tmp8[:, 0, :], -1.0, None, ALU.mult))
            link(tt(tmp8[:, 1, :], tmp8[:, 0, :], tmp8[:, 1, :], ALU.max))
            fin(v.tensor_scalar(tmp8[:, 2, :], tmp8[:, 0, :], 0.0, None, ALU.min), "ffabs")
            act_done("ffl")
            link(tt(tmp8[:, 0, :], tmp8[:, 2, :], tmp8[:, 1, :], ALU.subtract))
            link(v.tensor_tensor_scan(CQ[0:8, :], c_("ones")[0:8, :], tmp8[:, 0, :], 0.0, ALU.mult, ALU.add))
            v.tensor_copy(CQ[64:72, :], CQ[0:8, :])
            v.tensor_scalar(CK[96:104, :], CQ[0:8, :], -1.0, None, ALU.mult)
            fin(v.tensor_scalar(CK[32:40, :], CQ[0:8, :], -1.0, None, ALU.mult), "fc")
            act_done(f"z{NZ - 1}")
            fin(tt(rzf, xq[:, 0:D], xq[:, 0:D], ALU.mult), "qsq")

            def blocks4():
                return PSF[:, 2048:4096].rearrange("p (g s c) -> p g s c", g=16, s=2)

            pe_done("ma")
            tt(b16(9), blocks4()[:, :, 0, :], bc("strictT"), ALU.mult)
            fin(tt(b16(12), blocks4()[:, :, 1, :], bc("inclT"), ALU.mult), "at")
            act_done("qrs")

            def normalise(off, name, scale, step):
                link(v.reciprocal(rzf, rzf))
                link(tt(xq[:, off:off + D], xq[:, off:off + D], rzf, ALU.mult))
                fin(v.tensor_scalar(xq[:, off:off + D], xq[:, off:off + D], p_(name), scale, ALU.mult, ALU.mult), step)

            normalise(0, "qn", HD ** -0.5, "qn")
            fin(tt(rzf, xq[:, D:2 * D], xq[:, D:2 * D], ALU.mult), "ksqf")
            pe_done("mk")
            tt(b16(2), blocks4()[:, :, 0, :], bc("strictT"), ALU.mult)
            fin(tt(b16(13), blocks4()[:, :, 1, :], bc("inclT"), ALU.mult), "mk")
            act_done("krs")
            normalise(D, "kn", 1.0, "kn")
            pe_done("aa")
            tt(b16(8), banks16(4), bc("m0"), ALU.mult)
            link(tt(b16(14), b16(9), bc("m0T"), ALU.mult))
            tt(b16(8), b16(8), bc("eye"), ALU.add)
            fin(tt(b16(14), b16(14), bc("eye"), ALU.add), "aa")

            def level(k):
                fin(tt(b16(1), b16(9), bc(f"m{k}T"), ALU.mult), f"mq{k}")
                if k < 5:
                    pe_done(f"t{k}")
                    fin(tt(B[:, 8, :], two(6), B[:, 8, :], ALU.add), f"t{k}")
                pe_done(f"tt{k}")
                fin(tt(B[:, 14, :], two(4), B[:, 14, :], ALU.add), f"tt{k}")

            def head(h):
                if h >= 2:
                    pe_done(f"sc{h - 2}")
                a = CONST["delta"][0] + h
                dec = slice(64 * (h % 2), 64 * (h % 2) + 40)
                fin(v.tensor_scalar(CKh[dec, :], CK[dec, :], con[dec, a:a + 1], None, ALU.mult), f"ck{h}")
                pe_done(f"sc{h}")
                if h >= 2:
                    pe_done(f"pt{h - 2}")
                link(tt(att[:, h % 2, :], PS[:, h % 2, 0:3 * P], c_("causal"), ALU.add))
                v.tensor_reduce(col[:, 6:7], att[:, h % 2, 0:P], AX.X, ALU.max)
                link(v.tensor_reduce(col[:, 7:8], att[:, h % 2, P:3 * P], AX.X, ALU.max))
                fin(v.tensor_scalar(col[:, 6:8], col[:, 6:8], -1.0, None, ALU.mult), f"mx{h}")
                act_done(f"p{h}")
                link(v.reciprocal(col[:, 8:10], col[:, 8:10]))
                v.tensor_scalar(att[:, h % 2, 0:P], att[:, h % 2, 0:P], col[:, 8:9], None, ALU.mult)
                fin(v.tensor_scalar(att[:, h % 2, P:3 * P], att[:, h % 2, P:3 * P], col[:, 9:10], None, ALU.mult), f"pr{h}")
                if h % 2:
                    pe_done(f"o{h}")
                    j = h // 2
                    fin(tt(mixT[:, j, :], PS[:, 3, 0:SEQ], FG[:, j, :], ALU.mult), f"o{h}")

            def chunk(c):
                pe_done(f"u{c}")
                fin(v.tensor_copy(XU[:, 1, :], PS[:, 5, 0:256]), f"u{c}")
                pe_done(f"d{c}")
                if c:
                    pe_done(f"y{c - 1}")
                link(tt(S[:, (c + 1) % 2, :], PS[:, 7, 0:256], S[:, c % 2, :], ALU.add))
                nxt = S[:, (c + 1) % 2, :].rearrange("p (j n) -> p j n", j=NJ)
                w = WC[:, :].rearrange("p (j c) -> p j c", j=NJ)[:, :, c:c + 1].to_broadcast([P, NJ, HD])
                fin(tt(nxt, nxt, w, ALU.mult), f"s{c}")

            for kind, n in MIX_ORDER:
                {"level": level, "head": head, "chunk": chunk}[kind](n)
            pe_done("mean")
            fin(v.scalar_tensor_tensor(out=B[:, 8, :], in0=two(4), scalar=-1.0 / HD, in1=B[:, 8, :],
                                       op0=ALU.mult, op1=ALU.add), "cent")
            fin(tt(B[:, 1, :], B[:, 8, :], B[:, 8, :], ALU.mult), "vsq")
            act_done("gsd")
            link(v.reciprocal(B[:, 1, :], B[:, 1, :]))
            link(tt(B[:, 8, :], B[:, 8, :], B[:, 1, :], ALU.mult))
            for j in range(NJ):
                ins = v.tensor_scalar(b4(8)[:, j, :], b4(8)[:, j, :], p_("ln_w", j), p_("ln_b", j), ALU.mult, ALU.add)
            link(ins)
            link(tt(B[:, 8, :], B[:, 8, :], B[:, 0, :], ALU.add))
            v.memset(S[:, :, :], 0.0)
            fin(tt(mixT[:, NJ:2 * NJ, :], b4(8), b4(5), ALU.mult), "mix")
            v.wait_ge(s_x2, 16)
            for g in range(4):
                pe_done(f"xo{g}")
                q, b = g // 2, g % 2
                dst = xs[:, b, q * 512:(q + 1) * 512]
                fin(tt(dst, bank(g), dst, ALU.add), f"xo{g}")
            act_done("sd2")
            fin(v.reciprocal(col[:, 4:6], col[:, 2:4]), "rs2")
            v.wait_ge(s_gm, 32)
            for b in range(TB):
                ins = v.scalar_tensor_tensor(out=H2[:, b, :], in0=xs[:, b, :], scalar=col[:, 4 + b:5 + b], in1=gmoe,
                                             op0=ALU.mult, op1=ALU.mult)
            fin(ins, "h2")
            for k in range(0, KD, 2):
                pe_done(f"h2T{k}")
                fin(v.tensor_copy(h2T[:, k, :], PS[:, 4 + k % 4, 0:SEQ]), f"h2T{k}")
            act_done("hh")
            link(tt(HL, H2, HH, ALU.subtract))
            pe_done("logits")
            v.wait_ge(s_aux, 64)
            LG = R[:, 0:2, :]
            link(tt(LG, PS[:, 0, 0:2 * NE].rearrange("p (b e) -> p b e", b=TB),
                    brt[:, :].unsqueeze(1).to_broadcast([P, TB, NE]), ALU.add))
            top = B[:, 7, 0:16].rearrange("p (b n) -> p b n", b=TB)
            for b in range(TB):
                ins = v.max(top[:, b, :], R[:, b, :])
            link(ins)
            fin(v.tensor_scalar(col[:, 10:12].unsqueeze(2), top[:, :, 0:1], -1.0, None, ALU.mult), "lg")
            gt, eq, cum = (B[:, 8, a * 64:a * 64 + 64].rearrange("p (b e) -> p b e", b=TB) for a in range(3))
            for b in range(TB):
                v.tensor_scalar(gt[:, b, :], R[:, b, :], top[:, b, 3:4], None, ALU.is_gt)
                ins = v.tensor_scalar(eq[:, b, :], R[:, b, :], top[:, b, 3:4], None, ALU.is_equal)
            link(ins)
            v.tensor_reduce(col[:, 12:14], gt, AX.X, ALU.add)
            for b in range(TB):
                ins = v.tensor_tensor_scan(cum[:, b, :], c_("ones")[:, 0:NE], eq[:, b, :], 0.0, ALU.mult, ALU.add)
            link(ins)
            for b in range(TB):
                ins = v.tensor_scalar(cum[:, b, :], cum[:, b, :], col[:, 12 + b:13 + b], float(TOPK), ALU.add, ALU.is_le)
            link(ins)
            link(tt(cum, cum, eq, ALU.mult))
            SEL = R[:, 2:4, :]
            fin(tt(SEL, cum, gt, ALU.add), "sel")
            act_done("lex")
            EX = R[:, 20:22, :]
            link(tt(EX, EX, SEL, ALU.mult))
            link(v.tensor_reduce(col[:, 14:16], EX, AX.X, ALU.add))
            link(v.reciprocal(col[:, 16:18], col[:, 14:16]))
            for b in range(TB):
                ins = v.tensor_scalar(EX[:, b, :], EX[:, b, :], col[:, 16 + b:17 + b], None, ALU.mult)
            link(ins)
            for b in range(TB):
                v.tensor_copy(R[:, 12 + 4 * b:16 + 4 * b, :], EX[:, b, :].unsqueeze(1).to_broadcast([P, NCH, NE]))
                ins = v.tensor_copy(B[:, 2 + b, 0:P].rearrange("p (c e) -> p c e", c=NCH),
                                    SEL[:, b, :].unsqueeze(1).to_broadcast([P, NCH, NE]))
            fin(ins, "gr")
            pe_done("rank")
            RT = R[:, 22:24, :]
            link(v.scalar_tensor_tensor(out=RT, in0=PS[:, 1, 0:2 * NE].rearrange("p (b e) -> p b e", b=TB), scalar=FAR,
                                        in1=SEL, op0=ALU.add, op1=ALU.mult))
            for b in range(TB):
                ins = tt(R[:, 4 + 4 * b:8 + 4 * b, :], RT[:, b, :].unsqueeze(1).to_broadcast([P, NCH, NE]),
                         c_("far").rearrange("p (c e) -> p c e", c=NCH), ALU.add)
            fin(ins, "rr")
            pe_done("rrT")
            fin(v.tensor_copy(B[:, 5, 0:SEQ], PS[:, 2, 0:SEQ]), "rrT")
            pe_done("count")
            fin(v.tensor_scalar(col[:, 20:21], PS[:, 4, 0:1], c_("thr"), None, ALU.is_gt), "valid")
            pe_done("pos")
            link(v.tensor_copy(col[:, 21:22], PS[:, 5, 0:1]))
            fin(v.tensor_scalar(B[:, 4, 0:IW], c_("iota_i"), col[:, 21:22], col[:, 20:21], ALU.is_equal, ALU.mult), "oh")
            v.memset(zpad, 0.0)
            v.memset(GTs, 0.0).then_inc(s_gt, 1)
            pe_done("ei")
            v.tensor_copy(RI[:, :, :], PS[:, 6, 0:128].rearrange("p (b i) -> p i b", b=TB)[:, 0:IW, :])
            v.tensor_copy(GI[:, :, :], PS[:, 7, 0:128].rearrange("p (b i) -> p i b", b=TB)[:, 0:IW, :])
            fin(v.tensor_copy(EI[0:1, 0:NITEM + 2], PS[0:1, 1, 0:NITEM + 2]), "tabs")

            def tab(T, i, b):
                return T[:, i, b:b + 1] if isinstance(i, int) else T[:, bass.ds(i, 1), b]

            def select(i):
                for b in range(TB):
                    ins = v.tensor_scalar(PM[:, b, :], c_("iota_s")[:, 0:SLOTS], tab(RI, i, b), None, ALU.is_equal)
                ins.then_inc(s_sel, 1)

            def gathered(n):
                v.wait_ge(s_xh, n)
                tt(xl, bank(6), xh, ALU.subtract).then_inc(s_xl, 1)

            select(0)
            gathered(1)
            v.wait_ge(s_bt, 16)
            base = chain[0]
            LINKS = 6
            W = v.value_load(EI[0:1, NITEM + 1:NITEM + 2], min_val=NE, max_val=NITEM)
            with v.Fori(0, W) as i:
                e = v.value_load(EI[0:1, bass.ds(i, 1)], min_val=0, max_val=NE - 1)
                n = [0]

                def link_i(ins):
                    n[0] += 1
                    ins.then_inc(s_vl, 1)
                    v.wait_ge(s_vl, i * LINKS + (base + n[0]))

                def low(q):
                    hi, lo = (half(ring[:, NRAW + q % NRAW, a:a + 2048]) for a in (0, 2048))
                    v.wait_ge(s_hi, 6 * i + q + 1)
                    v.scalar_tensor_tensor(out=lo, in0=ring[:, q % NRAW, :], scalar=WSCALE, in1=hi,
                                           op0=ALU.mult, op1=ALU.subtract).then_inc(s_lo, 1)

                def bias(a, o, b0):
                    return v.scalar_tensor_tensor(
                        out=o.rearrange("p (k t) -> p k t", k=KD), in0=bank(b0).rearrange("p (k t) -> p k t", k=KD),
                        scalar=1.0 / WSCALE, in1=bcur[:, a:a + KD].unsqueeze(2).to_broadcast([P, KD, SLOTS]),
                        op0=ALU.mult, op1=ALU.add)

                low(0)
                low(1)
                v.tensor_copy(bcur[:, :].unsqueeze(1), bT[:, bass.ds(e, 1), :])
                v.wait_ge(s_gath, i + 1)
                select(i + 1)
                for b in range(TB):
                    ins = v.tensor_scalar(PG[:, b, :], c_("iota_s"), tab(RI, i, b), tab(GI, i, b),
                                          ALU.is_equal, ALU.mult)
                link_i(ins)
                low(2)
                v.wait_ge(s_used, 6 * i + 2 + MARKS)
                link_i(bias(0, e_g, 6))
                v.tensor_scalar(e_g, e_g, LIMIT, None, ALU.min).then_inc(s_glu, 1)
                low(3)
                low(4)
                v.wait_ge(s_sig, i + 1)
                tt(e_s, e_g, e_s, ALU.mult)
                v.wait_ge(s_used, 6 * i + 4 + MARKS)
                link_i(bias(KD, e_l, 7))
                link_i(v.tensor_scalar(e_l, e_l, LIMIT, -LIMIT, ALU.min, ALU.max))
                link_i(v.scalar_tensor_tensor(out=e_act, in0=e_l, scalar=1.0, in1=e_s, op0=ALU.add, op1=ALU.mult))
                link_i(v.tensor_copy(ah, e_act))
                tt(al, e_act, ah, ALU.subtract).then_inc(s_eact, 1)
                gathered(i + 2)
                v.wait_ge(s_gtp, i + 1)
                v.wait_ge(s_scat, i + 1)
                v.tensor_copy(GTs, PS[:, 5, 0:SEQ]).then_inc(s_gt, 1)
                low(5)
                assert n[0] == LINKS, n
            def fin_t(ins, name):
                finish(ins, "tdve", name)
                v.wait_ge(s_tdve, tdve_at[name])

            v.wait_ge(s_scat, W + 1)
            for g in range(4):
                q, b = g // 2, g % 2
                dst = xs[:, b, q * 512:(q + 1) * 512]
                ins = tt(dst, bank(g), dst, ALU.add)
            fin_t(ins, "x3")
            v.wait_ge(s_tact, tact_at["sd"])
            fin_t(v.reciprocal(col[:, 4:6], col[:, 2:4]), "rstd")
            for b in range(TB):
                ins = v.tensor_scalar(H3[:, b, :], xs[:, b, :], col[:, 4 + b:5 + b], None, ALU.mult)
            fin_t(ins, "hn")
            for k in range(0, KD, 2):
                v.wait_ge(s_tpe, tpe_at[f"t{k}"])
                fin_t(v.tensor_scalar(hT[:, k, :], bank(k % 4, SEQ), p_("ple", k), None, ALU.mult), f"t{k}")
            for b in range(TB):
                v.wait_ge(s_tact, tact_at[f"gate{b}"])
                ins = tt(H3[:, b, :], two(4 + 2 * b), H3[:, b, :], ALU.mult)
                ins.then_inc(s_vt, 1)
                v.wait_ge(s_vt, b + 1)
                fin_t(tt(xs[:, b, :], xs[:, b, :], H3[:, b, :], ALU.add), f"x4{b}")
            v.wait_ge(s_tact, tact_at["sd2"])
            fin_t(v.reciprocal(col[:, 4:6], col[:, 2:4]), "rstd2")
            v.wait_ge(s_tail, 80)
            for b in range(TB):
                fin_t(v.scalar_tensor_tensor(out=xs[:, b, :], in0=xs[:, b, :], scalar=col[:, 4 + b:5 + b], in1=gfin,
                                             op0=ALU.mult, op1=ALU.mult), f"out{b}")


def constants(np):
    con = np.zeros((P, NCONST), np.float32)

    def put(name, a):
        con[:, CONST[name][0]:CONST[name][1]] = a

    p, f = np.arange(P)[:, None], np.arange(P)[None, :]
    s, t = (p % CH), np.arange(CH)[None, :]
    put("ident", p == f)
    put("blk", p // HD == f // HD)
    put("inclT", s <= t)
    put("strictT", s < t)
    for k in range(6):
        put(f"m{k}T", ((s ^ t) >> k == 1) & (t > s))
    put("m0", ((s ^ t) == 1) & (s > t))
    put("eye", s == t)
    causal = np.where(f <= p, 0.0, -1e30)
    put("causal", np.concatenate([causal, np.zeros((P, P)), causal], 1))
    put("reset", np.broadcast_to(np.arange(SEQ)[None, :] % CH != 0, (P, SEQ)))
    put("tri", p < f)
    put("ones", 1.0)
    put("iota_s", np.arange(2 * SLOTS)[None, :] % SLOTS)
    h = np.arange(NHEAD)[None, :]
    put("delta", (p % 64 == h) | (p % 64 == h + 32))
    put("iota_i", np.arange(IW)[None, :])
    c = p // NE
    put("thr", np.where(c == 0, -1, SLOTS * c))
    put("eval", p % NE)
    put("far", -(FAR + SLOTS * (f // NE)))
    return con


def kernel(**inputs):
    import numpy as np
    import concourse.bacc as bacc
    from concourse.bass_utils import run_bass_kernel_spmd as run

    a = {k: np.asarray(v) for k, v in inputs.items()}

    def chunks(w):
        n = w.shape[-1]
        return np.ascontiguousarray(w.reshape(-1, P, n).transpose(1, 0, 2).reshape(P, -1))

    def cols(w):
        return w.reshape(-1, P).T

    def rep(w):
        return np.ascontiguousarray(np.broadcast_to(w.reshape(1, -1), (P, w.size)))

    mu = a["rwkv_mu"][0]
    R_, K_, V_, L_ = mu[0:512], mu[512:1024], mu[1024:1536], mu[1536:1792]
    prm = np.zeros((P, NPARAM), np.float32)
    for name, w in [("mix", cols(a["mix_norm"][0])), ("ple", cols(a["ple_norm"][0])),
                    ("mu", cols(np.concatenate([L_, K_, R_, V_]))),
                    ("w0", cols(a["rwkv_w0"][0])), ("a0", cols(a["rwkv_a0"][0])), ("k_k", cols(a["rwkv_k_k"][0])),
                    ("k_a", cols(a["rwkv_k_a"][0])), ("r_k", cols(a["rwkv_r_k"][0].reshape(-1))),
                    ("ln_w", cols(a["rwkv_ln_w"][0])), ("ln_b", cols(a["rwkv_ln_b"][0])),
                    ("qn", np.tile(a["fox_q_norm"][0], 2)[:, None]), ("kn", np.tile(a["fox_k_norm"][0], 2)[:, None])]:
        prm[:, PARAM[name][0]:PARAM[name][1]] = w
    prm[0:NHEAD, PARAM["fb"][0]] = a["fox_f_bias"][0]
    w_in = a["w_in"][0]
    host = {"x": chunks(a["x"][0]), "con": constants(np), "prm": prm,
            "lora": np.concatenate([np.concatenate([a["rwkv_w2"][0], a["rwkv_a2"][0]], 0), a["rwkv_g2"][0]], 1),
            "wff": chunks(w_in[:, 4 * FOXW:4 * FOXW + NHEAD]), "wr": chunks(a["w_router"][0]),
            "brt": rep(a["b_router"]), "gmoe": rep(a["moe_norm"]), "gfin": rep(a["final_norm"]),
            "pT": chunks(a["p"][0, 0].T), "wproj": chunks(a["w_ple_proj"][0]),
            "wo": np.stack([chunks(a["w_out"][0][:, q * PW:(q + 1) * PW]) for q in range(2)]),
            "wgate": np.stack([chunks(a["w_ple_gate"][0][:, q * PW:(q + 1) * PW]) for q in range(2)])}
    for n, (c0, w) in enumerate(ZP):
        host[f"wz{n}"] = chunks(w_in[:, c0:c0 + w])
    gu = a["w_gu"][0].reshape(NE, KD, P, 4, PW).transpose(0, 3, 2, 1, 4).reshape(NE, 4, P, KD * PW)
    dn = a["w_down"][0].reshape(NE, KF, P, 2, PW).transpose(0, 3, 2, 1, 4).reshape(NE, 2, P, KF * PW)
    host["we"] = np.concatenate([gu, dn], 1)
    host["bT"] = np.ascontiguousarray(a["b_gu"][0].reshape(NE, 16, P).transpose(2, 0, 1).reshape(P, NE * 16))
    host["bdn"] = a["b_down"][0]

    nc = bacc.Bacc("TRN2", target_bir_lowering=False, num_devices=1)
    arrays, t = {}, {}
    for name, w in host.items():
        w = np.ascontiguousarray(w)
        arrays[f"in_{name}"] = w
        t[name] = nc.dram_tensor(f"in_{name}", w.shape, mybir.dt.from_np(w.dtype), kind="ExternalInput").ap()
    out = nc.dram_tensor("out_0", (SEQ, D), F32, kind="ExternalOutput").ap()
    fox_rwkv7_moe_ple(nc, t, out.rearrange("(b p) d -> p b d", p=P))
    r = run(nc, [arrays], core_ids=[0])
    return r.results[0]["out_0"].reshape(1, SEQ, D)
```

```python
from contextlib import ExitStack

import concourse.bass as bass
from concourse import mybir

F32 = mybir.dt.float32
F16 = mybir.dt.float16
I32 = mybir.dt.int32
ALU = mybir.AluOpType
ACT = mybir.ActivationFunctionType
AX = mybir.AxisListType

P = 128
D = 1024
SEQ = 256
TB = SEQ // P
KD = D // P
PLE = 256
HD = 64
NHEAD = 8
NJ = NHEAD * HD // P
CH = 64
NC = SEQ // CH
NE = 32
TOPK = 4
FF = 1024
KF = FF // P
LIMIT = 7.0
SALPHA = 1.702
EPS = 1e-6
GN_EPS = 64e-5
DECAY = 0.6065306597126334
SLOTS = 64
NCH = SEQ // SLOTS
NITEM = NE + SEQ * TOPK // SLOTS
IW = NITEM + 1
NSLOT = 6
NRAW = 3
WSCALE = 64.0
MARKS = 3
PW = 512
FAR = 1000.0

FOXW, RW0 = NHEAD * HD, 4 * NHEAD * HD + NHEAD
ZP = [(RW0 + 3 * FOXW, 256), (RW0 + FOXW, PW), (RW0, PW), (RW0 + 2 * FOXW, PW),
      (0, PW), (FOXW, PW), (3 * FOXW, PW), (2 * FOXW, PW)]
Z_PIECE = [0] * 2 + [1] * 4 + [2] * 4 + [3] * 4 + [4] * 4 + [5] * 4 + [6] * 4
NZ = len(Z_PIECE)
N_SHIFT = 14
Z_DONE = [2, 6, 10, 14, 18, 22, 26, NZ + 3]


def layout(spec):
    at, out = 0, {}
    for name, n in spec:
        out[name] = (at, at + n)
        at += n
    return out, at


CONST, NCONST = layout([("ident", P), ("blk", P), ("inclT", CH), ("strictT", CH), ("m0", CH)]
                       + [(f"m{k}T", CH) for k in range(6)]
                       + [("eye", CH), ("causal", 3 * P), ("reset", SEQ), ("tri", P), ("ones", SEQ),
                          ("iota_s", 2 * SLOTS), ("delta", NHEAD), ("iota_i", IW), ("thr", 1), ("eval", 1),
                          ("far", P)])
PARAM, NPARAM = layout([("mix", KD), ("moe", KD), ("ple", KD), ("mu", N_SHIFT), ("w0", NJ), ("a0", NJ), ("k_k", NJ),
                        ("k_a", NJ), ("r_k", NJ), ("ln_w", NJ), ("ln_b", NJ), ("qn", 1), ("kn", 1), ("fb", 1)])

LEVELS = range(1, 6)
_heads = iter([("sc", 0), ("sc", 1)]
              + [x for h in range(NHEAD) for x in [("pt", h), ("o", h)] + [("sc", h + 2)] * (h + 2 < NHEAD)])


def take(n):
    return [x for _, x in zip(range(n), _heads)]


MIX_ORDER = [("z", 18), ("bp", 0), ("z", 19), ("kp", 0), ("z", 20), ("ma", 0), ("z", 21), ("mk", 0),
             ("z", 22), ("aa", 0), ("z", 23), ("zh", 24), ("q", 1), ("z", 24), ("t", 1), ("tt", 1),
             ("qss", 0), ("q", 2), ("t", 2), ("tt", 2), ("kss", 0), ("q", 3), ("zh", 25), ("t", 3), ("tt", 3),
             ("z", 25), ("q", 4), ("zh", 26), ("t", 4), ("tt", 4), ("z", 26), ("q", 5), ("zh", 27), ("tt", 5),
             ("z", 27), ("x", 0), ("zh", 28), ("u", 0), ("z", 28), ("d", 0)]
MIX_ORDER += take(1) + [("y", 0)]
for _c in range(1, NC):
    MIX_ORDER += take(1) + [("x", _c)] + take(1) + [("u", _c)] + take(2) + [("d", _c)] + take(1 + _c % 2)
    MIX_ORDER += [("y", _c)] + take(2)
MIX_ORDER += take(99)

PE_STEPS = ([f"hT{k}" for k in range(KD)] + ["z0", "z1"] + [f"z{n}" for n in range(2, 7)] + ["uwua"]
            + [f"z{n}" for n in range(7, 10)] + ["g", "ssk"] + [f"z{n}" for n in range(10, 16)] + ["vp0", "z16", "z17", "bn"])
PE_STEPS += [f"{kind}{n}" for kind, n in MIX_ORDER if kind != "zh"]
PE_STEPS += ["mean", "var", "xo0", "xo1", "xo2", "xo3"] + [f"h2T{k}" for k in range(KD)]
PE_STEPS += ["logits", "rank", "rrT", "grT", "count", "pos", "ri", "gi", "ei"]


ON_VECTOR = {"ma": ["at"], "mk": ["mk"], "aa": ["aa", "mq1"], "z": [], "bp": [], "kp": [],
             "qss": ["qn", "ksqf"], "kss": ["kn"], "x": [], "y": []}
ON_SCALAR = {"bp": ["bp"], "kp": ["kp"], "qss": ["qrs"], "kss": ["krs"]}
mixv, mixa = [], []
for kind, n in MIX_ORDER:
    mixv += ON_VECTOR.get(kind, [])
    mixa += ON_SCALAR.get(kind, [])
    if kind == "z":
        mixa += [f"z{n}"]
        mixv += ["qsq"] * (n == NZ - 3) + ["ffabs"] * (n == NZ) + ["fc", "ck0", "ck1"] * (n == NZ + 1)
        mixa += ["ffe", "ffl"] * (n == NZ)
    elif kind == "q":
        mixv += [f"mq{n + 1}"] * (n < 5)
        mixa += [f"q{n}"]
    elif kind in ("t", "tt"):
        mixv += [f"{kind}{n}"]
    elif kind == "sc":
        mixv += [f"mx{n}"] + [f"ck{n + 2}"] * (n + 2 < NHEAD)
        mixa += [f"p{n}"]
    elif kind == "pt":
        mixv += [f"pr{n}"]
        mixa += [f"pt{n}"]
    elif kind == "o":
        mixv += [f"o{n}"] * (n % 2)
    elif kind == "u":
        mixv += [f"u{n}"]
    elif kind == "d":
        mixv += [f"s{n}"]
    elif kind in ("x", "y"):
        mixa += [f"{kind}{n}"]
DVE_STEPS = (["init", "rstd0", "hn0", "rstd1", "hn1"] + [f"hT{k}" for k in range(0, KD, 2)]
             + [f"sh{n}" for n in range(6)] + ["ksq", "scan"] + [f"sh{n}" for n in range(6, 10)] + ["kmax", "kk", "bprod"]
             + [f"sh{n}" for n in range(10, 14)] + ["tildes"]
             + mixv + ["cent", "vsq", "mix"] + [f"xo{g}" for g in range(4)]
             + [f"h2T{k}" for k in range(0, KD, 2)] + ["rs2", "h2"]
             + ["lg", "sel", "gr", "rr", "rrT", "valid", "oh", "tabs"])
ACT_STEPS = (["ssq0", "sd0", "ssq1", "sd1"] + [f"hT{k}" for k in range(1, KD, 2)]
             + [f"z{n}" for n in range(6)] + ["lz", "z6", "swaa"] + [f"z{n}" for n in range(7, 10)] + ["nk", "exps", "g"]
             + [f"z{n}" for n in range(10, 18)] + ["vp"] + mixa
             + ["gsd"] + [f"h2T{k}" for k in range(1, KD, 2)] + ["ssq2", "sd2", "hh", "lex", "grT"])


def fox_rwkv7_moe_ple(nc, t, out):
    with ExitStack() as ctx:
        def sb(name, shape, dt=F32):
            return ctx.enter_context(nc.sbuf_tensor(name, shape, dt))

        def sem(name):
            return ctx.enter_context(nc.semaphore(name))

        PS = ctx.enter_context(nc.psum_tensor("PS", [P, 8, 512], F32))
        PSF = PS[:, :, :].rearrange("p b n -> p (b n)")
        ring = sb("ring", [P, NSLOT, KD * PW])
        con = sb("con", [P, NCONST])
        prm = sb("prm", [P, NPARAM])
        xq = sb("xq", [P, TB * D])
        hT = sb("hT", [P, KD, SEQ])
        B = sb("B", [P, 15, D])
        FG = sb("FG", [P, NJ, SEQ])
        FV = sb("FV", [P, TB, FOXW])
        rz = sb("rz", [P, 4, SEQ + 4])
        LZ = sb("LZ", [P, 2, SEQ])
        lora = sb("lora", [P, 2 * FOXW])
        wff = sb("wff", [P, KD, NHEAD])
        wr = sb("wr", [P, KD, NE])
        brt = sb("brt", [P, NE])
        S = sb("S", [P, 2, NJ * HD])
        XU = sb("XU", [P, 2, NJ * HD])
        WC = sb("WC", [P, NJ * NC])
        col = sb("col", [P, 32])
        epsc = sb("epsc", [P, 4])
        EI = sb("EI", [1, 64], I32)
        RI = sb("RI", [P, IW, TB])
        GI = sb("GI", [P, IW, TB])
        bcur = sb("bcur", [P, 16])
        bT = FG[:, :, :].rearrange("p a b -> p (a b)")[:, 0:NE * 16].rearrange("p (e n) -> p e n", n=16)

        def c_(name):
            return con[:, CONST[name][0]:CONST[name][1]]

        def p_(name, i=0):
            a = PARAM[name][0] + i
            return prm[:, a:a + 1]

        def b4(i):
            return B[:, i, :].rearrange("p (j t) -> p j t", j=NJ)

        def b16(i):
            return B[:, i, :].rearrange("p (g c) -> p g c", g=NJ * NC)

        def bank(b, w=512):
            return PS[:, b, 0:w]

        def banks16(b):
            return PSF[:, b * 512:b * 512 + 1024].rearrange("p (g c) -> p g c", g=16)

        def two(b):
            return PSF[:, b * 512:b * 512 + 1024]

        xs = xq[:, :].rearrange("p (b d) -> p b d", b=TB)
        QT = xq[:, 0:D].rearrange("p (j t) -> p j t", j=NJ)
        KT = xq[:, D:2 * D].rearrange("p (j t) -> p j t", j=NJ)
        hn = B[:, 0:2, :]
        AR = B[:, 10:12, :].rearrange("p a n -> p (a n)").rearrange("p (g s c) -> p g s c", g=16, s=2)
        rzf = rz[:, :, :].rearrange("p a b -> p (a b)")[:, 0:1024]
        att = rz[:, :, :].rearrange("p a b -> p (a b)")[:, 0:768].rearrange("p (s n) -> p s n", s=2)
        lzf = LZ[:, :, :].rearrange("p a b -> p (a b)")[:, 0:384]
        mixT = hT
        H2 = B[:, 10:12, :]
        H3 = B[:, 12:14, :]
        h2T = B[:, 0:2, :].rearrange("p a n -> p (a n)").rearrange("p (k t) -> p k t", k=KD)
        gmoe = B[:, 14, :]
        wgate = B[:, 2:10, :].rearrange("p (q a) n -> p q (a n)", q=2)
        wproj = B[:, 0:2, :]
        pTt = B[:, 14, 0:512].rearrange("p (k t) -> p k t", k=2)
        gfin = B[:, 10, :]
        ht2 = hT[:, :, :].rearrange("p a b -> p (a b)")
        bdn = ht2[0:NE, 0:D]
        e_g, e_s, e_l, e_act = (ht2[:, 512 * a:512 * a + 512] for a in range(4))
        fv2 = FV[:, :, :].rearrange("p a b -> p (a b)")

        def half(ap):
            return ap.bitcast(F16)

        HH = half(B[:, 12, :]).rearrange("p (b d) -> p b d", b=TB)
        HL = half(B[:, 13, :]).rearrange("p (b d) -> p b d", b=TB)
        xh, xl, ah, al = (half(fv2[:, a:a + 256]) for a in (0, 256, 512, 768))
        PM = half(rzf[:, 0:TB * SLOTS // 2]).rearrange("p (b t) -> p b t", b=TB)
        PG = rzf[:, 128:128 + 2 * TB * SLOTS].rearrange("p (b t) -> p b t", b=TB)
        GTs = rzf[:, 512:768]
        ysb = B[:, 11, 0:512]
        zpad = B[:, 11, 512:1024]
        CQ, CK, CKh = lora[:, 0:SEQ], lora[:, SEQ:2 * SEQ], lora[:, 2 * SEQ:3 * SEQ]
        tmp8 = rzf[0:8, 0:768].rearrange("p (s t) -> p s t", s=3)
        R = fv2[:, 0:24 * NE].rearrange("p (s e) -> p s e", e=NE)
        RRT, GRT = lora[:, 0:SEQ], lora[:, SEQ:2 * SEQ]
        SEL4 = lora[:, 2 * SEQ:3 * SEQ].rearrange("p (b n) -> p b n", b=TB)
        OH = lora[:, 768:768 + IW]
        TOP = lora[:, 832:848].rearrange("p (b n) -> p b n", b=TB)
        GTEQ = LZ[:, 0, 0:192]

        s_x = [sem(f"x{b}_landed") for b in range(TB)]
        s_in = sem("constants_landed")
        s_aux = sem("small_weights_landed")
        s_slot = [sem(f"slot{i}_landed") for i in range(NSLOT)]
        s_hl = sem("low_parts_of_x")
        s_bd = sem("b_down_landed")
        s_x2 = sem("x_again_landed")
        s_gm = sem("moe_gain_landed")
        s_bt = sem("expert_bias_landed")
        s_tail = sem("tail_weights_landed")
        s_pe = sem("tensor_steps_done")
        s_dve = sem("vector_steps_done")
        s_act = sem("scalar_steps_done")
        s_vl = sem("vector_op_done")
        s_al = sem("scalar_op_done")
        s_hi = sem("high_parts_split")
        s_lo = sem("low_parts_split")
        s_used = sem("expert_pieces_used")
        s_sel = sem("selection_built")
        s_gath = sem("tokens_gathered")
        s_xh = sem("gathered_high_parts")
        s_xl = sem("gathered_low_parts")
        s_gtp = sem("gate_matrix_transposed")
        s_gt = sem("gate_matrix_in_sbuf")
        s_glu = sem("glu_clamped")
        s_sig = sem("glu_sigmoid_done")
        s_eact = sem("expert_activation_done")
        s_ysb = sem("expert_output_in_sbuf")
        s_scat = sem("expert_output_added")
        s_tpe = sem("tail_tensor_steps_done")
        s_tdve = sem("tail_vector_steps_done")
        s_tact = sem("tail_scalar_steps_done")
        s_out = sem("output_stored")

        def value(names):
            return {n: i + 1 for i, n in enumerate(names)}

        pe_at = value(PE_STEPS)

        dve_at, act_at = value(DVE_STEPS), value(ACT_STEPS)
        TPE_STEPS = ["t0", "t1", "pp"] + [f"gate{g}" for g in range(4)]
        TDVE_STEPS = ["x30", "x31", "hT0", "hT1", "rstd"]
        TACT_STEPS = ["hT0", "ssq0", "hT1", "ssq1", "sd"]
        for g in range(4):
            TDVE_STEPS += [f"gp{g}", f"x4{g}"] + [f"sum{g // 2}", f"rstd{g // 2}", f"out{g - 1}", f"out{g}"] * (g % 2)
            TACT_STEPS += [f"gate{g}", f"sq{g}"] + [f"sd{g // 2}"] * (g % 2)
        tpe_at, tdve_at, tact_at = value(TPE_STEPS), value(TDVE_STEPS), value(TACT_STEPS)
        tables = {"dve": (DVE_STEPS, s_dve), "act": (ACT_STEPS, s_act), "pe": (PE_STEPS, s_pe),
                  "tdve": (TDVE_STEPS, s_tdve), "tact": (TACT_STEPS, s_tact), "tpe": (TPE_STEPS, s_tpe)}
        done = dict.fromkeys(tables, 0)

        def finish(ins, who, name):
            names, s = tables[who]
            assert names[done[who]] == name, (who, names[done[who]], name)
            done[who] += 1
            ins.then_inc(s, 1)

        block = ctx.enter_context(nc.Block())

        @block.sync
        def _(sp):
            for b in range(TB):
                sp.dma_start(xs[:, b, :], t["x"][:, b * D:(b + 1) * D]).then_inc(s_x[b], 16)
            sp.dma_start(con[:, :], t["con"]).then_inc(s_in, 16)
            sp.dma_start(prm[:, :], t["prm"]).then_inc(s_in, 16)

            def piece(n, src, cols):
                sp.dma_start(ring[:, n % NSLOT, 0:KD * cols], src).then_inc(s_slot[n % NSLOT], 16)

            for n in range(NSLOT):
                piece(n, t[f"wz{n}"], ZP[n][1])
                if n == 0:
                    sp.dma_start(lora[:, :], t["lora"]).then_inc(s_aux, 16)
                    sp.dma_start(wff[:, :, :], t["wff"].rearrange("p (k n) -> p k n", k=KD)).then_inc(s_aux, 16)
                    sp.dma_start(wr[:, :, :], t["wr"].rearrange("p (k n) -> p k n", k=KD)).then_inc(s_aux, 16)
                    sp.dma_start(brt[:, :], t["brt"]).then_inc(s_aux, 16)
            for n, slot, before in ((6, 0, 1), (7, 1, 5), (8, 4, 17), (9, 5, 21)):
                sp.wait_ge(s_pe, pe_at[f"z{before}"])
                src = t[f"wz{n}"] if n < len(ZP) else t["wo"][n - len(ZP)]
                sp.dma_start(ring[:, slot, :], src).then_inc(s_slot[slot], 16)
            for q, before in ((0, 25), (1, NZ + 2), (2, 9)):
                sp.wait_ge(s_pe, pe_at[f"z{before}"])
                sp.dma_start(ring[:, q, :], t["we"][0, q]).then_inc(s_slot[q], 16)
            sp.wait_ge(s_pe, pe_at[f"sc{NHEAD - 1}"])
            sp.dma_start(xq[:, :], t["x"]).then_inc(s_x2, 16)
            sp.wait_ge(s_dve, dve_at[f"o{NHEAD - 1}"])
            sp.dma_start(bT.rearrange("p e n -> p (e n)"), t["bT"]).then_inc(s_bt, 16)
            sp.wait_ge(s_pe, pe_at[f"y{NC - 1}"])
            sp.dma_start(gmoe, t["gmoe"]).then_inc(s_gm, 16)
            sp.wait_ge(s_dve, dve_at["mix"])
            for q in range(2):
                sp.dma_start(wgate[:, q, :], t["wgate"][q]).then_inc(s_tail, 16)

            def first_item(q):
                sp.wait_ge(s_lo, q - 2)
                sp.dma_start(ring[:, q - 3, :], t["we"][0, q]).then_inc(s_slot[q - 3], 16)

            first_item(3)
            first_item(4)
            sp.wait_ge(s_pe, pe_at["xo3"])
            sp.dma_start(bdn, t["bdn"]).then_inc(s_bd, 16)
            sp.wait_ge(s_dve, dve_at["lg"])
            sp.wait_ge(s_hl, 1)
            sp.dma_start(pTt.rearrange("p k t -> p (k t)"), t["pT"]).then_inc(s_tail, 16)
            sp.dma_start(gfin, t["gfin"]).then_inc(s_tail, 16)
            sp.dma_start(wproj.rearrange("p a n -> p (a n)"), t["wproj"]).then_inc(s_tail, 16)
            first_item(5)
            sp.wait_ge(s_dve, dve_at["tabs"])
            last_item = sp.value_load(EI[0:1, NITEM + 1:NITEM + 2], min_val=NE - 1, max_val=NITEM - 1)
            with sp.Fori(0, last_item) as i:
                e = sp.value_load(EI[0:1, bass.ds(i + 1, 1)], min_val=0, max_val=NE - 1)
                for q in range(6):
                    sp.wait_ge(s_lo, 6 * i + (q + 4))
                    sp.dma_start(ring[:, q % NRAW, :], t["we"][bass.ds(e, 1), q, :, :].rearrange("a p n -> (a p) n"))\
                        .then_inc(s_slot[q % NRAW], 16)
            for g in range(4):
                b, q = g // 2, g % 2
                cols = slice(q * PW, (q + 1) * PW)
                sp.wait_ge(s_tdve, tdve_at[f"out{g}"])
                sp.dma_start(out[:, b, cols], xs[:, b, cols]).then_inc(s_out, 16)
            sp.wait_ge(s_out, 16 * 4)

        @block.tensor
        def _(pe):
            def fin(mm, name):
                finish(mm, "pe", name)

            ident = c_("ident")
            blk = c_("blk")
            pe.wait_ge(s_in, 32)
            for b in range(TB):
                pe.wait_ge(s_dve, dve_at[f"hn{b}"])
                for k in range(KD):
                    mm = pe.transpose(PS[:, k, b * P:(b + 1) * P], hn[:, b, k * P:(k + 1) * P], ident)
                    if b == TB - 1:
                        fin(mm, f"hT{k}")
            pe.wait_ge(s_act, act_at[f"hT{KD - 1}"])
            pe.wait_ge(s_dve, dve_at[f"hT{KD - 2}"])

            def z(n, halves=(0, 1)):
                if n >= 4 and 0 in halves:
                    pe.wait_ge(s_act, act_at[f"z{n - 4}"])
                    if n == NZ - 1:
                        pe.wait_ge(s_act, act_at["qrs"])
                    elif n == NZ:
                        pe.wait_ge(s_act, act_at["krs"])
                piece = Z_PIECE[n] if n < NZ else 7
                first = n >= NZ or n == 0 or Z_PIECE[n - 1] != piece
                if first and n != NZ:
                    pe.wait_ge(s_slot[piece % NSLOT], 16 * (piece // NSLOT + 1))
                if n == NZ:
                    pe.wait_ge(s_aux, 64)
                width = ZP[piece][1]
                w = ring[:, piece % NSLOT, 0:KD * width].rearrange("p (k c) -> p k c", k=KD)
                at = (n - Z_PIECE.index(piece)) * P if n < NZ else 0
                for k in range(4 * halves[0], 4 * halves[-1] + 4):
                    flags = dict(start=(k == 0), stop=(k == KD - 1))
                    if n < NZ:
                        mm = pe.matmul(bank(n % 4, SEQ), w[:, k, at:at + P], hT[:, k, :], **flags)
                    elif n == NZ:
                        mm = pe.matmul(PS[0:NHEAD, n % 4, 0:SEQ], wff[:, k, :], hT[:, k, :], **flags)
                    else:
                        b = n - NZ - 1
                        mm = pe.matmul(bank(n % 4), hT[:, k, b * P:(b + 1) * P], w[:, k, :], **flags)
                if 1 in halves:
                    fin(mm, f"z{n}")

            def sums(b0, src, name):
                for j in range(NJ):
                    mm = pe.matmul(PS[:, b0 + j // 2, (j % 2) * SEQ:(j % 2 + 1) * SEQ], blk, src[:, j, :],
                                   start=True, stop=True)
                fin(mm, name)

            for n in range(7):
                z(n)
            pe.wait_ge(s_act, act_at["lz"])
            pe.wait_ge(s_aux, 64)
            for j in range(NJ):
                cols = slice((j % 2) * SEQ, (j % 2 + 1) * SEQ)
                pe.matmul(PS[:, 4 + j // 2, cols], lora[0:64, j * P:(j + 1) * P], LZ[0:64, 0, :], start=True, stop=True)
                mm = pe.matmul(PS[:, 6 + j // 2, cols], lora[64:P, j * P:(j + 1) * P], LZ[64:P, 0, :],
                               start=True, stop=True)
            fin(mm, "uwua")
            for n in range(7, 10):
                z(n)
            pe.wait_ge(s_act, act_at["swaa"])
            for j in range(NJ):
                mm = pe.matmul(PS[:, 4 + j // 2, (j % 2) * SEQ:(j % 2 + 1) * SEQ],
                               lora[:, FOXW + j * P:FOXW + (j + 1) * P], LZ[:, 1, :], start=True, stop=True)
            fin(mm, "g")
            pe.wait_ge(s_dve, dve_at["ksq"])
            sums(6, b4(7), "ssk")

            def per_head(b0, lhs, rhs, n=CH):
                for g in range(16):
                    for h2 in range(2):
                        rows = slice(64 * h2, 64 * h2 + 64)
                        f = PSF[rows, b0 * 512 + g * n:b0 * 512 + (g + 1) * n]
                        mm = pe.matmul(f, lhs(rows, g), rhs(rows, g), start=True, stop=True)
                return mm

            def eye(rows, g):
                return con[rows, CONST["ident"][0] + rows.start:CONST["ident"][0] + rows.stop]

            def blocks(i):
                return lambda rows, g: b16(i)[rows, g, :]

            for n in range(10, 18):
                if n == 16:
                    pe.wait_ge(s_dve, dve_at["sh13"])
                    pe.wait_ge(s_act, act_at["g"])
                    fin(per_head(4, blocks(2), eye), "vp0")
                z(n)
            pe.wait_ge(s_dve, dve_at["bprod"])
            pe.wait_ge(s_act, act_at["nk"])
            sums(6, b4(7), "bn")

            def ar(rows, g):
                return AR[rows, g, :, :].rearrange("p s c -> p (s c)")

            def matrices(kind):
                if kind == "bp":
                    pe.wait_ge(s_dve, dve_at["tildes"])
                    fin(per_head(6, blocks(4), eye), "bp0")
                elif kind == "kp":
                    pe.wait_ge(s_act, act_at["vp"])
                    fin(per_head(4, blocks(1), eye), "kp0")
                elif kind == "ma":
                    pe.wait_ge(s_act, act_at["kp"])
                    fin(per_head(4, blocks(4), ar, 2 * CH), "ma0")
                elif kind == "mk":
                    pe.wait_ge(s_dve, dve_at["at"])
                    fin(per_head(4, blocks(1), ar, 2 * CH), "mk0")
                elif kind == "aa":
                    pe.wait_ge(s_dve, dve_at["mk"])
                    fin(per_head(4, lambda rows, g: AR[rows, g, 0, :], blocks(4)), "aa0")
                elif kind == "qss":
                    pe.wait_ge(s_dve, dve_at["qsq"])
                    pe.wait_ge(s_act, act_at[f"z{NZ - 2}"])
                    sums(0, rzf.rearrange("p (j t) -> p j t", j=NJ), "qss0")
                elif kind == "kss":
                    pe.wait_ge(s_dve, dve_at["ksqf"])
                    sums(2, rzf.rearrange("p (j t) -> p j t", j=NJ), "kss0")

            def level(kind, k):
                if kind == "q":
                    pe.wait_ge(s_dve, dve_at[f"tt{k - 1}" if k > 1 else "mq1"])
                    fin(per_head(4, blocks(1), blocks(8)), f"q{k}")
                elif kind == "t":
                    pe.wait_ge(s_act, act_at[f"q{k}"])
                    fin(per_head(6, blocks(14), blocks(4)), f"t{k}")
                else:
                    pe.wait_ge(s_act, act_at[f"q{k}"])
                    fin(per_head(4, blocks(4), blocks(14)), f"tt{k}")

            def head(kind, h):
                j, rows = h // 2, slice(64 * (h % 2), 64 * (h % 2) + 64)
                dec = slice(rows.start, rows.start + 40)
                if kind == "sc":
                    pe.wait_ge(s_dve, dve_at[f"ck{h}"])
                    if h == 0:
                        pe.wait_ge(s_act, act_at[f"z{NZ + 2}"])
                    for b in range(TB):
                        o = PS[:, h % 2, b * P:(2 * b + 1) * P]
                        n = (b + 1) * P
                        pe.matmul(o, QT[rows, j, b * P:(b + 1) * P], KT[rows, j, 0:n], start=True, stop=False)
                        mm = pe.matmul(o, CQ[dec, b * P:(b + 1) * P], CKh[dec, 0:n], start=False, stop=True)
                elif kind == "pt":
                    pe.wait_ge(s_dve, dve_at[f"pr{h}"])
                    for i in range(3):
                        mm = pe.transpose(PS[:, 2, i * P:(i + 1) * P], att[:, h % 2, i * P:(i + 1) * P], ident)
                else:
                    pe.wait_ge(s_act, act_at[f"pt{h}"])
                    if h % 2 == 0 and h >= 2:
                        pe.wait_ge(s_dve, dve_at[f"o{h - 1}"])
                    v = slice(h * HD, (h + 1) * HD)
                    pe.matmul(PS[rows, 3, 0:P], FV[:, 0, v], lzf[:, 0:P], start=True, stop=True)
                    pe.matmul(PS[rows, 3, P:2 * P], FV[:, 0, v], lzf[:, P:2 * P], start=True, stop=False)
                    mm = pe.matmul(PS[rows, 3, P:2 * P], FV[:, 1, v], lzf[:, 2 * P:3 * P], start=False, stop=True)
                fin(mm, f"{kind}{h}")

            def state(kind, c):
                def both(b0, pairs):
                    for j in range(NJ):
                        g = j * NC + c
                        for h2 in range(2):
                            rows = slice(64 * h2, 64 * h2 + 64)
                            for i, (lhs, rhs) in enumerate(pairs):
                                mm = pe.matmul(PS[rows, b0, j * 64:(j + 1) * 64], lhs(rows, g, j), rhs(rows, g, j),
                                               start=(i == 0), stop=(i == len(pairs) - 1))
                    return mm

                def blk_(i):
                    return lambda rows, g, j: b16(i)[rows, g, :]

                def of(x, s):
                    return lambda rows, g, j: x[rows, s, j * 64:(j + 1) * 64]

                def ar_(s):
                    return lambda rows, g, j: AR[rows, g, s, :]

                if kind == "x":
                    if c == 0:
                        pe.wait_ge(s_dve, dve_at[f"tt{max(LEVELS)}"])
                    else:
                        pe.wait_ge(s_dve, dve_at[f"s{c - 1}"])
                    mm = both(4, [(ar_(0), of(S, c % 2)), (blk_(2), blk_(3))])
                elif kind == "u":
                    pe.wait_ge(s_act, act_at[f"x{c}"])
                    mm = both(5, [(blk_(14), of(XU, 0))])
                elif kind == "d":
                    pe.wait_ge(s_dve, dve_at[f"u{c}"])
                    mm = both(7, [(blk_(6), of(XU, 1)), (blk_(7), blk_(3))])
                else:
                    if c:
                        pe.wait_ge(s_act, act_at[f"y{c - 1}"])
                    mm = both(6, [(of(S, c % 2), ar_(1)), (of(XU, 1), blk_(12)), (blk_(3), blk_(13))])
                fin(mm, f"{kind}{c}")

            for kind, n in MIX_ORDER:
                if kind == "zh":
                    z(n, halves=(0,))
                elif kind == "z":
                    z(n, halves=(1,) if ("zh", n) in MIX_ORDER else (0, 1))
                elif kind in ("q", "t", "tt"):
                    level(kind, n)
                elif kind in ("sc", "pt", "o"):
                    head(kind, n)
                elif kind in ("x", "u", "d", "y"):
                    state(kind, n)
                else:
                    matrices(kind)
            def w_out(g, first):
                q, b = g // 2, g % 2
                w = ring[:, 4 + q, :].rearrange("p (k c) -> p k c", k=KD)
                for k in range(NJ) if first else range(NJ, KD):
                    mm = pe.matmul(bank(g), mixT[:, k, b * P:(b + 1) * P], w[:, k, :],
                                   start=(k == 0), stop=(k == KD - 1))
                return mm

            pe.wait_ge(s_act, act_at[f"y{NC - 1}"])
            sums(4, b4(8), "mean")
            pe.wait_ge(s_dve, dve_at[f"o{NHEAD - 1}"])
            pe.wait_ge(s_slot[4], 32)
            w_out(0, True)
            pe.wait_ge(s_dve, dve_at["vsq"])
            sums(6, b4(1), "var")
            w_out(1, True)
            pe.wait_ge(s_slot[5], 32)
            w_out(2, True)
            w_out(3, True)
            pe.wait_ge(s_dve, dve_at["mix"])
            for g in range(4):
                fin(w_out(g, False), f"xo{g}")
            pe.wait_ge(s_dve, dve_at["xo3"])
            for k in range(KD):
                if k >= 4:
                    if k % 2:
                        pe.wait_ge(s_act, act_at[f"h2T{k - 4}"])
                    else:
                        pe.wait_ge(s_dve, dve_at[f"h2T{k - 4}"])
                for b in range(TB):
                    mm = pe.transpose(PS[:, 4 + k % 4, b * P:(b + 1) * P], xs[:, b, k * P:(k + 1) * P], ident)
                fin(mm, f"h2T{k}")
            pe.wait_ge(s_act, act_at[f"h2T{KD - 1}"])
            pe.wait_ge(s_dve, dve_at[f"h2T{KD - 2}"])
            for b in range(TB):
                for k in range(KD):
                    mm = pe.matmul(PS[:, 0, b * NE:(b + 1) * NE], h2T[:, k, b * P:(b + 1) * P], wr[:, k, :],
                                   start=(k == 0), stop=(k == KD - 1))
            fin(mm, "logits")
            pe.wait_ge(s_dve, dve_at["sel"])
            pe.matmul(PS[:, 1, 0:NE], c_("tri"), R[:, 2, :], start=True, stop=True)
            pe.matmul(PS[:, 1, NE:2 * NE], c_("tri"), R[:, 3, :], start=True, stop=False)
            fin(pe.matmul(PS[:, 1, NE:2 * NE], c_("ones")[:, 0:P], R[:, 2, :], start=False, stop=True), "rank")

            def rows4(i):
                return R[:, i:i + 4, :].rearrange("p a b -> p (a b)")

            pe.wait_ge(s_dve, dve_at["rr"])
            for b in range(TB):
                mm = pe.transpose(PS[:, 2, b * P:(b + 1) * P], rows4(4 + 4 * b), ident)
            fin(mm, "rrT")
            for b in range(TB):
                mm = pe.transpose(PS[:, 3, b * P:(b + 1) * P], rows4(12 + 4 * b), ident)
            fin(mm, "grT")
            for b in range(TB):
                mm = pe.matmul(PS[:, 4, 0:1], SEL4[:, b, :], c_("ones")[:, 0:1], start=(b == 0), stop=(b == 1))
            fin(mm, "count")
            pe.wait_ge(s_dve, dve_at["valid"])
            fin(pe.matmul(PS[:, 5, 0:1], c_("tri"), col[:, 20:21], start=True, stop=True), "pos")
            pe.wait_ge(s_dve, dve_at["oh"])
            pe.wait_ge(s_act, act_at["grT"])
            for b in range(TB):
                mm = pe.matmul(PS[:, 6, b * 64:b * 64 + IW], RRT[:, b * P:(b + 1) * P], OH, start=True, stop=True)
            fin(mm, "ri")
            for b in range(TB):
                mm = pe.matmul(PS[:, 7, b * 64:b * 64 + IW], GRT[:, b * P:(b + 1) * P], OH, start=True, stop=True)
            fin(mm, "gi")
            pe.matmul(PS[0:1, 1, 0:IW], c_("eval"), OH, start=True, stop=True)
            fin(pe.matmul(PS[0:1, 1, NITEM + 1:NITEM + 2], col[:, 20:21], c_("ones")[:, 0:1], start=True, stop=True), "ei")

            def start_sums(b):
                for q in range(2):
                    pe.matmul(bank(2 * q + b), GRT[0:NE, b * P:(b + 1) * P], bdn[:, q * 512:(q + 1) * 512],
                              start=True, stop=True)

            pe.wait_ge(s_bd, 16)
            start_sums(0)
            pe.wait_ge(s_dve, dve_at["tabs"])

            def gather(n):
                pe.wait_ge(s_sel, n)
                for k in range(KD):
                    for a, src in enumerate((HH, HL)):
                        for b in range(TB):
                            mm = pe.matmul(PS[:, 6, k * SLOTS:(k + 1) * SLOTS], src[:, b, k * P:(k + 1) * P],
                                           PM[:, b, :], start=(a + b == 0), stop=(a + b == 2))
                mm.then_inc(s_gath, 1)

            def scatter():
                for b in range(TB):
                    for q in range(2):
                        rows = slice(64 * q, 64 * q + 64)
                        mm = pe.matmul(bank(2 * q + b), GTs[rows, b * P:(b + 1) * P], ysb[rows, :],
                                       start=False, stop=False, skip_group_check=True)
                mm.then_inc(s_scat, 1)

            def project(g):
                b, q = g // 2, g % 2
                for k in range(2):
                    mm = pe.matmul(bank(4 + g), pTt[:, k, b * P:(b + 1) * P], wproj[:, k, q * 512:(q + 1) * 512],
                                   start=(k == 0), stop=(k == 1))
                return mm

            def parts(q):
                w = half(ring[:, NRAW + q % NRAW, :]).rearrange("p (s k c) -> p s k c", s=2, k=KD)
                return w[:, 0], w[:, 1]

            pe.wait_ge(s_hl, 1)
            gather(1)
            start_sums(1)
            for n in range(MARKS):
                mm = pe.matmul(bank(4), half(zpad[:, 0:64]), half(zpad[:, 0:256]), start=True, stop=True)
                mm.then_inc(s_used, 1)
            last_item = pe.value_load(EI[0:1, NITEM + 1:NITEM + 2], min_val=NE - 1, max_val=NITEM - 1)

            def item(i, last=False):
                pe.wait_ge(s_xl, i + 1)
                for q in range(4):
                    wh, wl = parts(q)
                    pe.wait_ge(s_lo, 6 * i + (q + 1))
                    for f in range(4):
                        n = (q % 2) * 4 + f
                        o = PS[:, 6 + q // 2, n * SLOTS:(n + 1) * SLOTS]
                        cols = slice(f * P, (f + 1) * P)
                        for k in range(KD):
                            slots = slice(k * SLOTS, (k + 1) * SLOTS)
                            pe.matmul(o, wh[:, k, cols], xh[:, slots], start=(k == 0), stop=False)
                            pe.matmul(o, wh[:, k, cols], xl[:, slots], start=False, stop=False)
                            mm = pe.matmul(o, wl[:, k, cols], xh[:, slots], start=False, stop=(k == KD - 1))
                    mm.then_inc(s_used, 1)
                pe.wait_ge(s_glu, i + 1)
                if not last:
                    gather(i + 2)
                pe.wait_ge(s_ysb, i + 1)
                pe.wait_ge(s_gt, i + 1)
                scatter()
                for b in range(TB):
                    mm = pe.transpose(PS[:, 5, b * P:(b + 1) * P], PG[:, b, :], ident)
                mm.then_inc(s_gtp, 1)
                if last:
                    pe.wait_ge(s_tail, 80)
                    project(2)
                pe.wait_ge(s_eact, i + 1)
                for q in range(4, 6):
                    wh, wl = parts(q)
                    pe.wait_ge(s_lo, 6 * i + (q + 1))
                    o = PS[64 * (q - 4):64 * (q - 4) + 64, 4, :]
                    for k in range(KF):
                        slots = slice(k * SLOTS, (k + 1) * SLOTS)
                        pe.matmul(o, ah[:, slots], wh[:, k, :], start=(k == 0), stop=False)
                        pe.matmul(o, ah[:, slots], wl[:, k, :], start=False, stop=False)
                        mm = pe.matmul(o, al[:, slots], wh[:, k, :], start=False, stop=(k == KF - 1))
                    mm.then_inc(s_used, 1)

            with pe.Fori(0, last_item) as i:
                item(i)
            item(last_item, last=True)
            project(3)
            pe.wait_ge(s_ysb, last_item + 2)
            pe.wait_ge(s_gt, last_item + 2)
            scatter()
            project(1)
            for b in range(TB):
                pe.wait_ge(s_tdve, tdve_at[f"x3{b}"])
                for k in range(KD):
                    mm = pe.transpose(PS[:, b + 2 * (k // 4), k % 4 * P:(k % 4 + 1) * P],
                                      xs[:, b, k * P:(k + 1) * P], ident)
                finish(mm, "tpe", f"t{b}")
            finish(project(0), "tpe", "pp")
            for b in range(TB):
                pe.wait_ge(s_tact, tact_at[f"hT{b}"])
                pe.wait_ge(s_tdve, tdve_at[f"hT{b}"])
                for q in range(2):
                    w = wgate[:, q, :].rearrange("p (k c) -> p k c", k=KD)
                    for k in range(KD):
                        mm = pe.matmul(bank(2 * q + b), hT[:, k, b * P:(b + 1) * P], w[:, k, :],
                                       start=(k == 0), stop=(k == KD - 1))
                    finish(mm, "tpe", f"gate{2 * b + q}")

        @block.gpsimd
        def _(pool):
            pool.wait_ge(s_act, act_at["hh"])
            pool.tensor_tensor(HL, H2, HH, ALU.subtract).then_inc(s_hl, 1)

        @block.scalar
        def _(act):
            chain = [0]

            def link(ins):
                chain[0] += 1
                ins.then_inc(s_al, 1)
                act.wait_ge(s_al, chain[0])

            def fin(ins, name):
                finish(ins, "act", name)

            def pe_done(name):
                act.wait_ge(s_pe, pe_at[name])

            eps = epsc[:, 0:1]
            act.wait_ge(s_dve, dve_at["init"])
            for b in range(TB):
                act.wait_ge(s_x[b], 16)
                fin(act.activation(hT[:, 4 * b:4 * b + 4, :].rearrange("p a b -> p (a b)"), xs[:, b, :], ACT.Square,
                                   accum_out=col[:, b:b + 1]), f"ssq{b}")
                act.wait_ge(s_act, act_at[f"ssq{b}"])
                fin(act.activation(col[:, 2 + b:3 + b], col[:, b:b + 1], ACT.Sqrt, bias=eps, scale=1.0 / D), f"sd{b}")
            act.wait_ge(s_in, 32)
            for k in range(1, KD, 2):
                pe_done(f"hT{k}")
                fin(act.activation(hT[:, k, :], bank(k, SEQ), ACT.Copy, scale=p_("mix", k)), f"hT{k}")

            def z(n):
                pe_done(f"z{n}")
                if n < N_SHIFT:
                    if n >= 4:
                        act.wait_ge(s_dve, dve_at[f"sh{n - 4}"])
                    fin(act.activation(rz[:, n % 4, 1:SEQ + 1], bank(n % 4, SEQ), ACT.Copy), f"z{n}")
                elif n < 18:
                    fin(act.activation(QT[:, n - 14, :], bank(n % 4, SEQ), ACT.Copy), f"z{n}")
                elif n < 22:
                    fin(act.activation(KT[:, n - 18, :], bank(n % 4, SEQ), ACT.Copy), f"z{n}")
                elif n < NZ:
                    fin(act.activation(FG[:, n - 22, :], bank(n % 4, SEQ), ACT.Sigmoid), f"z{n}")
                elif n == NZ:
                    act.wait_ge(s_dve, dve_at["kn"])
                    fin(act.activation(tmp8[:, 0, :], PS[0:NHEAD, n % 4, 0:SEQ], ACT.Identity,
                                       bias=p_("fb")[0:NHEAD, :]), f"z{n}")
                else:
                    fin(act.activation(FV[:, n - NZ - 1, :], bank(n % 4), ACT.Copy), f"z{n}")

            for n in range(6):
                z(n)
            act.wait_ge(s_dve, dve_at["sh1"])
            act.activation(LZ[0:64, 0, :], LZ[0:64, 0, :], ACT.Tanh)
            fin(act.activation(LZ[:, 1, :], LZ[:, 1, :], ACT.Sigmoid), "lz")
            z(6)
            pe_done("uwua")
            for j in range(NJ):
                cols = slice((j % 2) * SEQ, (j % 2 + 1) * SEQ)
                act.activation(b4(3)[:, j, :], PS[:, 4 + j // 2, cols], ACT.Sigmoid, bias=p_("w0", j))
                ins = act.activation(b4(4)[:, j, :], PS[:, 6 + j // 2, cols], ACT.Sigmoid, bias=p_("a0", j))
            fin(ins, "swaa")
            for n in range(7, 10):
                z(n)
            act.wait_ge(s_dve, dve_at["kmax"])
            link(act.activation(B[:, 7, :], B[:, 7, :], ACT.Ln, scale=2.0 ** 30))
            fin(act.activation(B[:, 7, :], B[:, 7, :], ACT.Exp, scale=-0.5, bias=epsc[:, 2:3]), "nk")
            act.wait_ge(s_dve, dve_at["scan"])
            act.activation(B[:, 3, :], B[:, 3, :], ACT.Exp, scale=-DECAY)
            act.activation(B[:, 9, :], B[:, 8, :], ACT.Exp, scale=-DECAY)
            fin(act.activation(B[:, 8, :], B[:, 8, :], ACT.Exp, scale=DECAY), "exps")
            pe_done("g")
            fin(act.activation(B[:, 5, :], two(4), ACT.Copy), "g")
            for n in range(10, 18):
                z(n)

            act.wait_ge(s_dve, dve_at["tildes"])
            pe_done("vp0")
            fin(act.activation(B[:, 3, :], two(4), ACT.Copy), "vp")

            def rsqrt(dst, src, eps_col):
                link(act.activation(dst, src, ACT.Ln, bias=eps_col, scale=1.0 / HD))
                return act.activation(dst, dst, ACT.Exp, scale=-0.5)

            for kind, n in MIX_ORDER:
                if kind == "z":
                    z(n)
                    if n == NZ:
                        act.wait_ge(s_dve, dve_at["ffabs"])
                        fin(act.activation(tmp8[:, 1, :], tmp8[:, 1, :], ACT.Exp, scale=-1.0), "ffe")
                        act.wait_ge(s_act, act_at["ffe"])
                        fin(act.activation(tmp8[:, 1, :], tmp8[:, 1, :], ACT.Ln, bias=1.0), "ffl")
                elif kind in ("bp", "kp"):
                    i, b0 = {"bp": (6, 6), "kp": (7, 4)}[kind]
                    pe_done(f"{kind}0")
                    fin(act.activation(B[:, i, :], two(b0), ACT.Copy), kind)
                elif kind == "qss":
                    pe_done("qss0")
                    fin(rsqrt(rzf, two(0), eps), "qrs")
                elif kind == "kss":
                    pe_done("kss0")
                    fin(rsqrt(rzf, two(2), eps), "krs")
                elif kind == "q":
                    pe_done(f"q{n}")
                    fin(act.activation(B[:, 4, :], two(4), ACT.Copy), f"q{n}")
                elif kind == "sc":
                    act.wait_ge(s_dve, dve_at[f"mx{n}"])
                    a, m, u = att[:, n % 2, :], 22 + 2 * (n % 2), 26 + 2 * (n % 2)
                    act.activation(a[:, 0:P], a[:, 0:P], ACT.Exp, bias=col[:, m:m + 1], accum_out=col[:, u:u + 1])
                    fin(act.activation(a[:, P:3 * P], a[:, P:3 * P], ACT.Exp, bias=col[:, m + 1:m + 2],
                                       accum_out=col[:, u + 1:u + 2]), f"p{n}")
                elif kind == "pt":
                    pe_done(f"pt{n}")
                    if n:
                        pe_done(f"o{n - 1}")
                    fin(act.activation(lzf, PS[:, 2, 0:3 * P], ACT.Copy), f"pt{n}")
                elif kind == "x":
                    pe_done(f"x{n}")
                    fin(act.activation(XU[:, 0, :], PS[:, 4, 0:256], ACT.Copy), f"x{n}")
                elif kind == "y":
                    pe_done(f"y{n}")
                    fin(act.activation(b4(8)[:, :, n * CH:(n + 1) * CH],
                                       PS[:, 6, 0:256].rearrange("p (j t) -> p j t", j=NJ), ACT.Copy), f"y{n}")
            pe_done("var")
            fin(rsqrt(B[:, 1, :], two(6), epsc[:, 1:2]), "gsd")

            def high(i, q):
                act.wait_ge(s_slot[q % NRAW], 32 * i + (16 * ((2, 2, 1)[q % NRAW] + q // NRAW + 1)))
                if not isinstance(i, int):
                    act.wait_ge(s_used, 6 * i + (q + MARKS - 2))
                act.activation(half(ring[:, NRAW + q % NRAW, 0:2048]), ring[:, q % NRAW, :], ACT.Copy,
                               scale=WSCALE).then_inc(s_hi, 1)

            high(0, 0)
            pe_done("xo1")
            high(0, 1)
            for k in range(1, KD, 2):
                pe_done(f"h2T{k}")
                fin(act.activation(h2T[:, k, :], PS[:, 4 + k % 4, 0:SEQ], ACT.Copy, scale=p_("moe", k)), f"h2T{k}")
            for b in range(TB):
                ins = act.activation(H2[:, b, :], xs[:, b, :], ACT.Square, accum_out=col[:, b:b + 1])
            fin(ins, "ssq2")
            act.wait_ge(s_act, act_at["ssq2"])
            fin(act.activation(col[:, 2:4], col[:, 0:2], ACT.Sqrt, bias=eps, scale=1.0 / D), "sd2")
            high(0, 2)
            act.wait_ge(s_dve, dve_at["h2"])
            fin(act.activation(HH[:, :, :].rearrange("p b d -> p (b d)"), H2.rearrange("p b d -> p (b d)"), ACT.Copy),
                "hh")
            act.wait_ge(s_dve, dve_at["lg"])
            for b in range(TB):
                ins = act.activation(R[:, 20 + b, :], R[:, b, :], ACT.Exp, bias=col[:, 10 + b:11 + b])
            fin(ins, "lex")
            pe_done("grT")
            fin(act.activation(GRT, PS[:, 3, 0:SEQ], ACT.Copy), "grT")

            def gathered(n):
                act.wait_ge(s_gath, n)
                act.activation(xh, bank(6), ACT.Copy).then_inc(s_xh, 1)

            def output(n):
                act.wait_ge(s_used, n)
                act.activation(ysb, bank(4), ACT.Copy, scale=1.0 / WSCALE).then_inc(s_ysb, 1)

            gathered(1)
            last_item = act.value_load(EI[0:1, NITEM + 1:NITEM + 2], min_val=NE - 1, max_val=NITEM - 1)

            def item(i, last=False):
                output(6 * i + MARKS)
                high(i, 3)
                act.wait_ge(s_glu, i + 1)
                act.activation(e_s, e_g, ACT.Sigmoid, scale=SALPHA).then_inc(s_sig, 1)
                high(i, 4)
                high(i, 5)
                if not last:
                    act.wait_ge(s_used, 6 * i + (4 + MARKS))
                    gathered(i + 2)
                    for q in range(3):
                        high(i + 1, q)

            with act.Fori(0, last_item) as i:
                item(i)
            item(last_item, last=True)
            output(6 * last_item + (6 + MARKS))
            def fin_t(ins, name):
                finish(ins, "tact", name)

            def squares(n, b, cols, name):
                src = xs[:, b, cols]
                w = src.shape[-1]
                fin_t(act.activation(ring[:, n // 4, (n % 4) * D:(n % 4) * D + w], src, ACT.Square,
                                     accum_out=col[:, n:n + 1]), name)

            for b in range(TB):
                act.wait_ge(s_tpe, tpe_at[f"t{b}"])
                for k in range(4, KD):
                    ins = act.activation(hT[:, k, b * P:(b + 1) * P], PS[:, 2 + b, (k - 4) * P:(k - 3) * P], ACT.Copy,
                                         scale=p_("ple", k))
                fin_t(ins, f"hT{b}")
                squares(b, b, slice(0, D), f"ssq{b}")
            act.wait_ge(s_tact, tact_at["ssq1"])
            fin_t(act.activation(col[:, 2:4], col[:, 0:2], ACT.Sqrt, bias=eps, scale=1.0 / D), "sd")
            act.wait_ge(s_tdve, tdve_at["rstd"])
            for g in range(4):
                b, q = g // 2, g % 2
                act.wait_ge(s_tpe, tpe_at[f"gate{g}"])
                fin_t(act.activation(H3[:, b, q * PW:(q + 1) * PW], bank(2 * q + b), ACT.Sigmoid,
                                     scale=col[:, 4 + b:5 + b]), f"gate{g}")
                act.wait_ge(s_tdve, tdve_at[f"x4{g}"])
                squares(6 + g, b, slice(q * PW, (q + 1) * PW), f"sq{g}")
                if q:
                    act.wait_ge(s_tdve, tdve_at[f"sum{b}"])
                    fin_t(act.activation(col[:, 12 + b:13 + b], col[:, 10 + b:11 + b], ACT.Sqrt, bias=eps,
                                         scale=1.0 / D), f"sd{b}")

        @block.vector
        def _(v):
            chain = [0]

            def link(ins):
                chain[0] += 1
                ins.then_inc(s_vl, 1)
                v.wait_ge(s_vl, chain[0])

            def fin(ins, name):
                finish(ins, "dve", name)
                v.wait_ge(s_dve, dve_at[name])

            def pe_done(name):
                v.wait_ge(s_pe, pe_at[name])

            def act_done(name):
                v.wait_ge(s_act, act_at[name])

            def tt(o, a, b, op):
                return v.tensor_tensor(o, a, b, op)

            def bc(name, g=16):
                return c_(name).unsqueeze(1).to_broadcast([P, g, CH])

            v.memset(epsc[:, 0:1], EPS)
            v.memset(epsc[:, 1:2], GN_EPS)
            v.memset(epsc[:, 2:3], 15 * 0.6931471805599453)
            v.memset(rz[:, :, 0:1], 0.0)
            fin(v.memset(S[:, :, :], 0.0), "init")
            for b in range(TB):
                act_done(f"sd{b}")
                fin(v.reciprocal(col[:, 4 + b:5 + b], col[:, 2 + b:3 + b]), f"rstd{b}")
                v.wait_ge(s_x[b], 16)
                fin(v.tensor_scalar(hn[:, b, :], xs[:, b, :], col[:, 4 + b:5 + b], None, ALU.mult), f"hn{b}")
            v.wait_ge(s_in, 32)
            for k in range(0, KD, 2):
                pe_done(f"hT{k}")
                fin(v.tensor_scalar(hT[:, k, :], bank(k, SEQ), p_("mix", k), None, ALU.mult), f"hT{k}")

            def shift(n):
                dst = LZ[:, n, :] if n < 2 else b4((1, 0, 2)[(n - 2) // 4])[:, (n - 2) % 4, :]
                act_done(f"z{n}")
                link(tt(dst, rz[:, n % 4, 0:SEQ], rz[:, n % 4, 1:SEQ + 1], ALU.subtract))
                fin(v.scalar_tensor_tensor(out=dst, in0=dst, scalar=p_("mu", n), in1=rz[:, n % 4, 1:SEQ + 1],
                                           op0=ALU.mult, op1=ALU.add), f"sh{n}")

            for n in range(6):
                shift(n)
            for j in range(NJ):
                ins = v.tensor_scalar(b4(6)[:, j, :], b4(1)[:, j, :], p_("k_k", j), None, ALU.mult)
            link(ins)
            fin(tt(B[:, 7, :], B[:, 6, :], B[:, 6, :], ALU.mult), "ksq")
            act_done("swaa")
            for j in range(NJ):
                ins = v.tensor_tensor_scan(b4(8)[:, j, :], c_("reset"), b4(3)[:, j, :], 0.0, ALU.mult, ALU.add)
            link(ins)
            fin(tt(B[:, 3, :], B[:, 8, :], B[:, 3, :], ALU.subtract), "scan")
            for n in range(6, 10):
                shift(n)
            pe_done("ssk")
            fin(v.tensor_scalar(B[:, 7, :], two(6), 1e-24, None, ALU.max), "kmax")
            act_done("nk")
            fin(tt(B[:, 6, :], B[:, 6, :], B[:, 7, :], ALU.mult), "kk")
            for j in range(NJ):
                ins = v.tensor_scalar(b4(10)[:, j, :], b4(4)[:, j, :], -1.0, p_("k_a", j), ALU.add, ALU.mult)
            link(ins)
            link(v.scalar_tensor_tensor(out=B[:, 1, :], in0=B[:, 10, :], scalar=1.0, in1=B[:, 1, :],
                                        op0=ALU.add, op1=ALU.mult))
            for j in range(NJ):
                ins = v.scalar_tensor_tensor(out=b4(7)[:, j, :], in0=b4(0)[:, j, :], scalar=p_("r_k", j),
                                             in1=b4(1)[:, j, :], op0=ALU.mult, op1=ALU.mult)
            fin(ins, "bprod")
            for n in range(10, 14):
                shift(n)
            act_done("exps")
            tt(AR[:, :, 1, :], b16(0), b16(9), ALU.mult)
            v.scalar_tensor_tensor(out=AR[:, :, 0, :], in0=b16(6), scalar=-1.0, in1=b16(3),
                                   op0=ALU.mult, op1=ALU.mult)
            v.tensor_copy(WC[:, :].unsqueeze(2), b16(9)[:, :, CH - 1:CH])
            tt(B[:, 1, :], B[:, 1, :], B[:, 8, :], ALU.mult)
            link(tt(B[:, 4, :], B[:, 4, :], B[:, 6, :], ALU.mult))
            link(tt(B[:, 4, :], B[:, 4, :], B[:, 8, :], ALU.mult))
            pe_done("bn")
            fin(tt(B[:, 0, :], two(6), B[:, 2, :], ALU.mult), "tildes")

            def blocks4():
                return PSF[:, 2048:4096].rearrange("p (g s c) -> p g s c", g=16, s=2)

            def normalise(off, name, scale, step):
                link(tt(xq[:, off:off + D], xq[:, off:off + D], rzf, ALU.mult))
                fin(v.tensor_scalar(xq[:, off:off + D], xq[:, off:off + D], p_(name), scale, ALU.mult, ALU.mult), step)

            def mask_level(k):
                if k > 1:
                    pe_done(f"q{k - 1}")
                fin(tt(b16(1), b16(9), bc(f"m{k}T"), ALU.mult), f"mq{k}")

            def decay_rows(h):
                if h >= 2:
                    pe_done(f"sc{h - 2}")
                a = CONST["delta"][0] + h
                dec = slice(64 * (h % 2), 64 * (h % 2) + 40)
                fin(v.tensor_scalar(CKh[dec, :], CK[dec, :], con[dec, a:a + 1], None, ALU.mult), f"ck{h}")

            for kind, n in MIX_ORDER:
                if kind == "z" and n == NZ:
                    link(v.memset(lora[:, 0:2 * SEQ], 0.0))
                    for a in (0, 64):
                        v.memset(CQ[a + 32:a + 40, :], 1.0)
                        v.memset(CK[a:a + 8, :], 1.0)
                    act_done(f"z{NZ}")
                    link(v.tensor_scalar(tmp8[:, 1, :], tmp8[:, 0, :], -1.0, None, ALU.mult))
                    link(tt(tmp8[:, 1, :], tmp8[:, 0, :], tmp8[:, 1, :], ALU.max))
                    fin(v.tensor_scalar(tmp8[:, 2, :], tmp8[:, 0, :], 0.0, None, ALU.min), "ffabs")
                elif kind == "z" and n == NZ - 3:
                    act_done(f"z{n}")
                    fin(tt(rzf, xq[:, 0:D], xq[:, 0:D], ALU.mult), "qsq")
                elif kind == "z" and n == NZ + 1:
                    act_done("ffl")
                    link(tt(tmp8[:, 0, :], tmp8[:, 2, :], tmp8[:, 1, :], ALU.subtract))
                    link(v.tensor_tensor_scan(CQ[0:8, :], c_("ones")[0:8, :], tmp8[:, 0, :], 0.0, ALU.mult, ALU.add))
                    v.tensor_copy(CQ[64:72, :], CQ[0:8, :])
                    v.tensor_scalar(CK[96:104, :], CQ[0:8, :], -1.0, None, ALU.mult)
                    fin(v.tensor_scalar(CK[32:40, :], CQ[0:8, :], -1.0, None, ALU.mult), "fc")
                    decay_rows(0)
                    decay_rows(1)
                elif kind == "qss":
                    act_done("qrs")
                    normalise(0, "qn", HD ** -0.5, "qn")
                    fin(tt(rzf, xq[:, D:2 * D], xq[:, D:2 * D], ALU.mult), "ksqf")
                elif kind == "kss":
                    act_done("krs")
                    normalise(D, "kn", 1.0, "kn")
                elif kind == "ma":
                    pe_done("ma0")
                    tt(b16(9), blocks4()[:, :, 0, :], bc("strictT"), ALU.mult)
                    fin(tt(b16(12), blocks4()[:, :, 1, :], bc("inclT"), ALU.mult), "at")
                elif kind == "mk":
                    pe_done("mk0")
                    tt(b16(2), blocks4()[:, :, 0, :], bc("strictT"), ALU.mult)
                    fin(tt(b16(13), blocks4()[:, :, 1, :], bc("inclT"), ALU.mult), "mk")
                elif kind == "aa":
                    pe_done("aa0")
                    tt(b16(8), banks16(4), bc("m0"), ALU.mult)
                    link(tt(b16(14), b16(9), bc("m0T"), ALU.mult))
                    tt(b16(8), b16(8), bc("eye"), ALU.add)
                    fin(tt(b16(14), b16(14), bc("eye"), ALU.add), "aa")
                    mask_level(1)
                elif kind == "q" and n < 5:
                    mask_level(n + 1)
                elif kind == "t":
                    pe_done(f"t{n}")
                    fin(tt(B[:, 8, :], two(6), B[:, 8, :], ALU.add), f"t{n}")
                elif kind == "tt":
                    pe_done(f"tt{n}")
                    fin(tt(B[:, 14, :], two(4), B[:, 14, :], ALU.add), f"tt{n}")
                elif kind == "sc":
                    pe_done(f"sc{n}")
                    if n >= 2:
                        pe_done(f"pt{n - 2}")
                    a, m = att[:, n % 2, :], 22 + 2 * (n % 2)
                    link(tt(a, PS[:, n % 2, 0:3 * P], c_("causal"), ALU.add))
                    v.tensor_reduce(col[:, m:m + 1], a[:, 0:P], AX.X, ALU.max)
                    link(v.tensor_reduce(col[:, m + 1:m + 2], a[:, P:3 * P], AX.X, ALU.max))
                    fin(v.tensor_scalar(col[:, m:m + 2], col[:, m:m + 2], -1.0, None, ALU.mult), f"mx{n}")
                    if n + 2 < NHEAD:
                        decay_rows(n + 2)
                elif kind == "pt":
                    act_done(f"p{n}")
                    a, u = att[:, n % 2, :], 26 + 2 * (n % 2)
                    link(v.reciprocal(col[:, u:u + 2], col[:, u:u + 2]))
                    v.tensor_scalar(a[:, 0:P], a[:, 0:P], col[:, u:u + 1], None, ALU.mult)
                    fin(v.tensor_scalar(a[:, P:3 * P], a[:, P:3 * P], col[:, u + 1:u + 2], None, ALU.mult), f"pr{n}")
                elif kind == "o" and n % 2:
                    pe_done(f"o{n}")
                    j = n // 2
                    fin(tt(mixT[:, j, :], PS[:, 3, 0:SEQ], FG[:, j, :], ALU.mult), f"o{n}")
                elif kind == "u":
                    pe_done(f"u{n}")
                    fin(v.tensor_copy(XU[:, 1, :], PS[:, 5, 0:256]), f"u{n}")
                elif kind == "d":
                    pe_done(f"d{n}")
                    if n:
                        pe_done(f"y{n - 1}")
                    link(tt(S[:, (n + 1) % 2, :], PS[:, 7, 0:256], S[:, n % 2, :], ALU.add))
                    nxt = S[:, (n + 1) % 2, :].rearrange("p (j n) -> p j n", j=NJ)
                    w = WC[:, :].rearrange("p (j c) -> p j c", j=NJ)[:, :, n:n + 1].to_broadcast([P, NJ, HD])
                    fin(tt(nxt, nxt, w, ALU.mult), f"s{n}")
            pe_done("mean")
            fin(v.scalar_tensor_tensor(out=B[:, 8, :], in0=two(4), scalar=-1.0 / HD, in1=B[:, 8, :],
                                       op0=ALU.mult, op1=ALU.add), "cent")
            fin(tt(B[:, 1, :], B[:, 8, :], B[:, 8, :], ALU.mult), "vsq")
            act_done("gsd")
            link(tt(B[:, 8, :], B[:, 8, :], B[:, 1, :], ALU.mult))
            for j in range(NJ):
                ins = v.tensor_scalar(b4(8)[:, j, :], b4(8)[:, j, :], p_("ln_w", j), p_("ln_b", j), ALU.mult, ALU.add)
            link(ins)
            link(tt(B[:, 8, :], B[:, 8, :], B[:, 0, :], ALU.add))
            fin(tt(mixT[:, NJ:2 * NJ, :], b4(8), b4(5), ALU.mult), "mix")

            def low(i, q):
                hi, lo = (half(ring[:, NRAW + q % NRAW, a:a + 2048]) for a in (0, 2048))
                v.wait_ge(s_hi, 6 * i + (q + 1))
                v.scalar_tensor_tensor(out=lo, in0=ring[:, q % NRAW, :], scalar=WSCALE, in1=hi,
                                       op0=ALU.mult, op1=ALU.subtract).then_inc(s_lo, 1)

            low(0, 0)
            v.wait_ge(s_x2, 16)
            for g in range(4):
                pe_done(f"xo{g}")
                q, b = g // 2, g % 2
                dst = xs[:, b, q * 512:(q + 1) * 512]
                fin(tt(dst, bank(g), dst, ALU.add), f"xo{g}")
            for k in range(0, KD, 2):
                pe_done(f"h2T{k}")
                fin(v.tensor_scalar(h2T[:, k, :], PS[:, 4 + k % 4, 0:SEQ], p_("moe", k), None, ALU.mult), f"h2T{k}")
            low(0, 1)
            act_done("sd2")
            fin(v.reciprocal(col[:, 4:6], col[:, 2:4]), "rs2")
            v.wait_ge(s_gm, 16)
            for b in range(TB):
                ins = v.scalar_tensor_tensor(out=H2[:, b, :], in0=xs[:, b, :], scalar=col[:, 4 + b:5 + b], in1=gmoe,
                                             op0=ALU.mult, op1=ALU.mult)
            fin(ins, "h2")
            pe_done("logits")
            v.wait_ge(s_aux, 64)
            for b in range(TB):
                ins = v.scalar_tensor_tensor(out=R[:, b, :], in0=PS[:, 0, b * NE:(b + 1) * NE],
                                             scalar=col[:, 4 + b:5 + b], in1=brt[:, :], op0=ALU.mult, op1=ALU.add)
            link(ins)
            top = TOP
            for b in range(TB):
                ins = v.max(top[:, b, :], R[:, b, :])
            link(ins)
            fin(v.tensor_scalar(col[:, 10:12].unsqueeze(2), top[:, :, 0:1], -1.0, None, ALU.mult), "lg")
            gt, eq, cum = (GTEQ[:, a * 64:a * 64 + 64].rearrange("p (b e) -> p b e", b=TB) for a in range(3))
            for b in range(TB):
                v.tensor_scalar(gt[:, b, :], R[:, b, :], top[:, b, 3:4], None, ALU.is_gt)
                ins = v.tensor_scalar(eq[:, b, :], R[:, b, :], top[:, b, 3:4], None, ALU.is_equal)
            link(ins)
            v.tensor_reduce(col[:, 12:14], gt, AX.X, ALU.add)
            for b in range(TB):
                ins = v.tensor_tensor_scan(cum[:, b, :], c_("ones")[:, 0:NE], eq[:, b, :], 0.0, ALU.mult, ALU.add)
            link(ins)
            for b in range(TB):
                ins = v.tensor_scalar(cum[:, b, :], cum[:, b, :], col[:, 12 + b:13 + b], float(TOPK), ALU.add, ALU.is_le)
            link(ins)
            link(tt(cum, cum, eq, ALU.mult))
            SEL = R[:, 2:4, :]
            fin(tt(SEL, cum, gt, ALU.add), "sel")
            act_done("lex")
            EX = R[:, 20:22, :]
            link(tt(EX, EX, SEL, ALU.mult))
            link(v.tensor_reduce(col[:, 14:16], EX, AX.X, ALU.add))
            link(v.reciprocal(col[:, 16:18], col[:, 14:16]))
            for b in range(TB):
                ins = v.tensor_scalar(EX[:, b, :], EX[:, b, :], col[:, 16 + b:17 + b], None, ALU.mult)
            link(ins)
            for b in range(TB):
                v.tensor_copy(R[:, 12 + 4 * b:16 + 4 * b, :], EX[:, b, :].unsqueeze(1).to_broadcast([P, NCH, NE]))
                ins = v.tensor_copy(SEL4[:, b, :].rearrange("p (c e) -> p c e", c=NCH),
                                    SEL[:, b, :].unsqueeze(1).to_broadcast([P, NCH, NE]))
            fin(ins, "gr")
            pe_done("rank")
            RT = R[:, 22:24, :]
            link(v.scalar_tensor_tensor(out=RT, in0=PS[:, 1, 0:2 * NE].rearrange("p (b e) -> p b e", b=TB), scalar=FAR,
                                        in1=SEL, op0=ALU.add, op1=ALU.mult))
            for b in range(TB):
                ins = tt(R[:, 4 + 4 * b:8 + 4 * b, :], RT[:, b, :].unsqueeze(1).to_broadcast([P, NCH, NE]),
                         c_("far").rearrange("p (c e) -> p c e", c=NCH), ALU.add)
            fin(ins, "rr")
            pe_done("rrT")
            fin(v.tensor_copy(RRT, PS[:, 2, 0:SEQ]), "rrT")
            pe_done("count")
            fin(v.tensor_scalar(col[:, 20:21], PS[:, 4, 0:1], c_("thr"), None, ALU.is_gt), "valid")
            pe_done("pos")
            link(v.tensor_copy(col[:, 21:22], PS[:, 5, 0:1]))
            fin(v.tensor_scalar(OH, c_("iota_i"), col[:, 21:22], col[:, 20:21], ALU.is_equal, ALU.mult), "oh")
            v.wait_ge(s_hl, 1)
            v.memset(zpad, 0.0)
            v.memset(GTs, 0.0).then_inc(s_gt, 1)
            pe_done("ei")
            v.tensor_copy(RI[:, :, :], PS[:, 6, 0:128].rearrange("p (b i) -> p i b", b=TB)[:, 0:IW, :])
            v.tensor_copy(GI[:, :, :], PS[:, 7, 0:128].rearrange("p (b i) -> p i b", b=TB)[:, 0:IW, :])
            v.tensor_copy(EI[0:1, 0:NITEM + 1], PS[0:1, 1, 0:NITEM + 1])
            fin(v.tensor_scalar(EI[0:1, NITEM + 1:NITEM + 2], PS[0:1, 1, NITEM + 1:NITEM + 2], -1.0, None, ALU.add), "tabs")

            def tab(T, i, b):
                return T[:, i, b:b + 1] if isinstance(i, int) else T[:, bass.ds(i, 1), b]

            def select(i):
                for b in range(TB):
                    ins = v.tensor_scalar(PM[:, b, :], c_("iota_s")[:, 0:SLOTS], tab(RI, i, b), None, ALU.is_equal)
                ins.then_inc(s_sel, 1)

            def gathered(n):
                v.wait_ge(s_xh, n)
                tt(xl, bank(6), xh, ALU.subtract).then_inc(s_xl, 1)

            select(0)
            low(0, 2)
            gathered(1)
            v.wait_ge(s_bt, 16)
            base = chain[0]
            LINKS = 6
            last_item = v.value_load(EI[0:1, NITEM + 1:NITEM + 2], min_val=NE - 1, max_val=NITEM - 1)

            def item(i, last=False):
                e = v.value_load(EI[0:1, bass.ds(i, 1)], min_val=0, max_val=NE - 1)
                n = [0]

                def link_i(ins):
                    n[0] += 1
                    ins.then_inc(s_vl, 1)
                    v.wait_ge(s_vl, LINKS * i + (base + n[0]))

                def bias(a, o, b0):
                    return v.scalar_tensor_tensor(
                        out=o.rearrange("p (k t) -> p k t", k=KD), in0=bank(b0).rearrange("p (k t) -> p k t", k=KD),
                        scalar=1.0 / WSCALE, in1=bcur[:, a:a + KD].unsqueeze(2).to_broadcast([P, KD, SLOTS]),
                        op0=ALU.mult, op1=ALU.add)

                v.tensor_copy(bcur[:, :].unsqueeze(1), bT[:, bass.ds(e, 1), :])
                v.wait_ge(s_gath, i + 1)
                if not last:
                    select(i + 1)
                for b in range(TB):
                    ins = v.tensor_scalar(PG[:, b, :], c_("iota_s"), tab(RI, i, b), tab(GI, i, b),
                                          ALU.is_equal, ALU.mult)
                link_i(ins)
                v.wait_ge(s_used, 6 * i + (2 + MARKS))
                link_i(bias(0, e_g, 6))
                v.tensor_scalar(e_g, e_g, LIMIT, None, ALU.min).then_inc(s_glu, 1)
                low(i, 3)
                v.wait_ge(s_sig, i + 1)
                tt(e_s, e_g, e_s, ALU.mult)
                low(i, 4)
                v.wait_ge(s_used, 6 * i + (4 + MARKS))
                link_i(bias(KD, e_l, 7))
                link_i(v.tensor_scalar(e_l, e_l, LIMIT, -LIMIT, ALU.min, ALU.max))
                link_i(v.scalar_tensor_tensor(out=e_act, in0=e_l, scalar=1.0, in1=e_s, op0=ALU.add, op1=ALU.mult))
                link_i(v.tensor_copy(ah, e_act))
                tt(al, e_act, ah, ALU.subtract).then_inc(s_eact, 1)
                low(i, 5)
                if not last:
                    gathered(i + 2)
                v.wait_ge(s_gtp, i + 1)
                v.wait_ge(s_scat, i + 1)
                v.tensor_copy(GTs, PS[:, 5, 0:SEQ]).then_inc(s_gt, 1)
                if not last:
                    for q in range(3):
                        low(i + 1, q)
                assert n[0] == LINKS, n

            with v.Fori(0, last_item) as i:
                item(i)
            item(last_item, last=True)
            def fin_t(ins, name):
                finish(ins, "tdve", name)
                v.wait_ge(s_tdve, tdve_at[name])

            v.wait_ge(s_scat, last_item + 2)
            for b in range(TB):
                for q in range(2):
                    dst = xs[:, b, q * PW:(q + 1) * PW]
                    ins = tt(dst, bank(2 * q + b), dst, ALU.add)
                fin_t(ins, f"x3{b}")
            for b in range(TB):
                v.wait_ge(s_tpe, tpe_at[f"t{b}"])
                a = PARAM["ple"][0]
                fin_t(tt(hT[:, 0:4, b * P:(b + 1) * P], bank(b).rearrange("p (k t) -> p k t", k=4),
                         prm[:, a:a + 4].unsqueeze(2).to_broadcast([P, 4, P]), ALU.mult), f"hT{b}")
            v.wait_ge(s_tact, tact_at["sd"])
            fin_t(v.reciprocal(col[:, 4:6], col[:, 2:4]), "rstd")
            v.wait_ge(s_tail, 80)
            for g in range(4):
                b, q = g // 2, g % 2
                cols = slice(q * PW, (q + 1) * PW)
                v.wait_ge(s_tact, tact_at[f"gate{g}"])
                v.wait_ge(s_tpe, tpe_at["pp"])
                fin_t(tt(H3[:, b, cols], bank(4 + 2 * b + q), H3[:, b, cols], ALU.mult), f"gp{g}")
                fin_t(tt(xs[:, b, cols], xs[:, b, cols], H3[:, b, cols], ALU.add), f"x4{g}")
                if q:
                    v.wait_ge(s_tact, tact_at[f"sq{g}"])
                    fin_t(tt(col[:, 10 + b:11 + b], col[:, 6 + 2 * b:7 + 2 * b], col[:, 7 + 2 * b:8 + 2 * b], ALU.add),
                          f"sum{b}")
                    v.wait_ge(s_tact, tact_at[f"sd{b}"])
                    fin_t(v.reciprocal(col[:, 14 + b:15 + b], col[:, 12 + b:13 + b]), f"rstd{b}")
                    for q2 in range(2):
                        cols = slice(q2 * PW, (q2 + 1) * PW)
                        fin_t(v.scalar_tensor_tensor(out=xs[:, b, cols], in0=xs[:, b, cols],
                                                     scalar=col[:, 14 + b:15 + b], in1=gfin[:, cols],
                                                     op0=ALU.mult, op1=ALU.mult), f"out{2 * b + q2}")


def constants(np):
    con = np.zeros((P, NCONST), np.float32)

    def put(name, a):
        con[:, CONST[name][0]:CONST[name][1]] = a

    p, f = np.arange(P)[:, None], np.arange(P)[None, :]
    s, t = (p % CH), np.arange(CH)[None, :]
    put("ident", p == f)
    put("blk", p // HD == f // HD)
    put("inclT", s <= t)
    put("strictT", s < t)
    for k in range(6):
        put(f"m{k}T", ((s ^ t) >> k == 1) & (t > s))
    put("m0", ((s ^ t) == 1) & (s > t))
    put("eye", s == t)
    causal = np.where(f <= p, 0.0, -1e30)
    put("causal", np.concatenate([causal, np.zeros((P, P)), causal], 1))
    put("reset", np.broadcast_to(np.arange(SEQ)[None, :] % CH != 0, (P, SEQ)))
    put("tri", p < f)
    put("ones", 1.0)
    put("iota_s", np.arange(2 * SLOTS)[None, :] % SLOTS)
    h = np.arange(NHEAD)[None, :]
    put("delta", (p % 64 == h) | (p % 64 == h + 32))
    put("iota_i", np.arange(IW)[None, :])
    c = p // NE
    put("thr", np.where(c == 0, -1, SLOTS * c))
    put("eval", p % NE)
    put("far", -(FAR + SLOTS * (f // NE)))
    return con


def kernel(**inputs):
    import numpy as np
    import concourse.bacc as bacc
    from concourse.bass_utils import run_bass_kernel_spmd as run

    a = {k: np.asarray(v) for k, v in inputs.items()}

    def chunks(w):
        n = w.shape[-1]
        return np.ascontiguousarray(w.reshape(-1, P, n).transpose(1, 0, 2).reshape(P, -1))

    def cols(w):
        return w.reshape(-1, P).T

    def rep(w):
        return np.ascontiguousarray(np.broadcast_to(w.reshape(1, -1), (P, w.size)))

    mu = a["rwkv_mu"][0]
    R_, K_, V_, L_ = mu[0:512], mu[512:1024], mu[1024:1536], mu[1536:1792]
    prm = np.zeros((P, NPARAM), np.float32)
    for name, w in [("mix", cols(a["mix_norm"][0])), ("moe", cols(a["moe_norm"][0])), ("ple", cols(a["ple_norm"][0])),
                    ("mu", cols(np.concatenate([L_, K_, R_, V_]))),
                    ("w0", cols(a["rwkv_w0"][0])), ("a0", cols(a["rwkv_a0"][0])), ("k_k", cols(a["rwkv_k_k"][0])),
                    ("k_a", cols(a["rwkv_k_a"][0])), ("r_k", cols(a["rwkv_r_k"][0].reshape(-1))),
                    ("ln_w", cols(a["rwkv_ln_w"][0])), ("ln_b", cols(a["rwkv_ln_b"][0])),
                    ("qn", np.tile(a["fox_q_norm"][0], 2)[:, None]), ("kn", np.tile(a["fox_k_norm"][0], 2)[:, None])]:
        prm[:, PARAM[name][0]:PARAM[name][1]] = w
    prm[0:NHEAD, PARAM["fb"][0]] = a["fox_f_bias"][0]
    w_in = a["w_in"][0]
    host = {"x": chunks(a["x"][0]), "con": constants(np), "prm": prm,
            "lora": np.concatenate([np.concatenate([a["rwkv_w2"][0], a["rwkv_a2"][0]], 0), a["rwkv_g2"][0]], 1),
            "wff": chunks(w_in[:, 4 * FOXW:4 * FOXW + NHEAD]), "wr": chunks(a["w_router"][0]),
            "brt": rep(a["b_router"]), "gmoe": rep(a["moe_norm"]), "gfin": rep(a["final_norm"]),
            "pT": chunks(a["p"][0, 0].T), "wproj": chunks(a["w_ple_proj"][0]),
            "wo": np.stack([chunks(a["w_out"][0][:, q * PW:(q + 1) * PW]) for q in range(2)]),
            "wgate": np.stack([chunks(a["w_ple_gate"][0][:, q * PW:(q + 1) * PW]) for q in range(2)])}
    for n, (c0, w) in enumerate(ZP):
        host[f"wz{n}"] = chunks(w_in[:, c0:c0 + w])
    gu = a["w_gu"][0].reshape(NE, KD, P, 4, PW).transpose(0, 3, 2, 1, 4).reshape(NE, 4, P, KD * PW)
    dn = a["w_down"][0].reshape(NE, KF, P, 2, PW).transpose(0, 3, 2, 1, 4).reshape(NE, 2, P, KF * PW)
    host["we"] = np.concatenate([gu, dn], 1)
    host["bT"] = np.ascontiguousarray(a["b_gu"][0].reshape(NE, 16, P).transpose(2, 0, 1).reshape(P, NE * 16))
    host["bdn"] = a["b_down"][0]

    nc = bacc.Bacc("TRN2", target_bir_lowering=False, num_devices=1)
    arrays, t = {}, {}
    for name, w in host.items():
        w = np.ascontiguousarray(w)
        arrays[f"in_{name}"] = w
        t[name] = nc.dram_tensor(f"in_{name}", w.shape, mybir.dt.from_np(w.dtype), kind="ExternalInput").ap()
    out = nc.dram_tensor("out_0", (SEQ, D), F32, kind="ExternalOutput").ap()
    fox_rwkv7_moe_ple(nc, t, out.rearrange("(b p) d -> p b d", p=P))
    r = run(nc, [arrays], core_ids=[0])
    return r.results[0]["out_0"].reshape(1, SEQ, D)
```
